# Optimizing a Trainium2 kernel written in Bass

```python
import jax, jax.numpy as jnp
from jax import lax
import numpy as np

D_MODEL = 1024
BATCH = 1
SEQ = 256
DEPTH = 2
DEC_BATCH = 8
DEC_SEQ = 4
PAST_LEN = 1024
PAGE_SIZE = 128

N_EVEN = (DEPTH + 1) // 2
N_ODD = DEPTH // 2
EPS = 1e-6
D_A = D_MODEL // 2
CONV_A_WIDTH = 31
GDN_HEADS = 4
GDN_DK = 128
GDN_DV = 128
GDN_CONV = 4
GDN_CHUNK = 64
QKV_W = GDN_HEADS * (2 * GDN_DK + GDN_DV)
IN_AB = 2 * D_A + QKV_W + GDN_HEADS * GDN_DV + 2 * GDN_HEADS
C_PATTERNS = ((128, 1), (512, 4), (2048, 16))
N_GROUPS = len(C_PATTERNS)
C_HEADS = 8
C_HD = D_MODEL // C_HEADS
ROT_DIM = C_HD // 4
ROPE_THETA = 500000.0
ATT_BLOCK = 128
IN_C = 3 * N_GROUPS * C_HEADS * C_HD
PEER_HEADS = 8
N_KEYS = 128
N_EXPERTS = N_KEYS * N_KEYS
PEER_TOPK = 16
PEER_DKEY = 128
PEER_HALF = PEER_DKEY // 2
PEER_BLOCK = 128
PLE_DIM = 256

kernel_name = 'hybrid_conv_delta_dilated_peer_decode_step'

def _rmsnorm(x, g):
    xf = x.astype(jnp.float32)
    y = xf * lax.rsqrt(jnp.mean(xf * xf, axis=-1, keepdims=True) + EPS)
    return (y * g.astype(jnp.float32)).astype(x.dtype)

def _layernorm(x, g, b):
    xf = x.astype(jnp.float32)
    xc = xf - jnp.mean(xf, axis=-1, keepdims=True)
    y = xc * lax.rsqrt(jnp.mean(xc * xc, axis=-1, keepdims=True) + EPS)
    return (y * g.astype(jnp.float32) + b.astype(jnp.float32)).astype(x.dtype)

def _l2norm(x):
    xf = x.astype(jnp.float32)
    return xf * lax.rsqrt(jnp.sum(xf * xf, axis=-1, keepdims=True) + EPS)

def _causal_dwconv(x, buf, w):
    xx = jnp.concatenate([buf.astype(x.dtype), x], axis=1)
    y = lax.conv_general_dilated(xx, w.astype(x.dtype)[:, None, :], window_strides=(1,), padding='VALID',
                                 dimension_numbers=('NWC', 'WIO', 'NWC'), feature_group_count=x.shape[-1])
    return y, xx[:, xx.shape[1] - (w.shape[0] - 1):]

def _gated_delta(q, k, v, g, beta, s0):
    B, T, H, K = q.shape
    V = v.shape[-1]
    C = GDN_CHUNK if T % GDN_CHUNK == 0 else T
    N = T // C

    def chunks(t):
        return t.reshape(B, N, C, H, -1).transpose(1, 0, 3, 2, 4)

    qc, kc, vc = chunks(q), chunks(k), chunks(v.astype(jnp.float32))
    gc = chunks(g[..., None])[..., 0].astype(jnp.float32)
    bc = chunks(beta[..., None])[..., 0].astype(jnp.float32)
    gcum = jnp.cumsum(gc, axis=-1)
    causal = jnp.tril(jnp.ones((C, C), dtype=bool))
    strict = jnp.tril(jnp.ones((C, C), dtype=bool), -1)
    decay = jnp.exp(jnp.where(causal, gcum[..., :, None] - gcum[..., None, :], -jnp.inf))
    kb = kc * bc[..., None]
    lmat = jnp.where(strict, jnp.einsum('nbhik,nbhjk->nbhij', kb, kc) * decay, 0.0)
    amat = lmat + jnp.eye(C, dtype=jnp.float32)
    rhs = jnp.concatenate([vc * bc[..., None], kb * jnp.exp(gcum)[..., None]], axis=-1)
    sol = lax.linalg.triangular_solve(amat, rhs, left_side=True, lower=True, unit_diagonal=True)
    u, w = sol[..., :V], sol[..., V:]
    intra = jnp.where(causal, jnp.einsum('nbhik,nbhjk->nbhij', qc, kc) * decay, 0.0)

    def step(S, inp):
        qi, ki, ui, wi, gi, ai = inp
        vnew = ui - jnp.einsum('bhck,bhkv->bhcv', wi, S)
        o = (jnp.einsum('bhck,bhkv->bhcv', qi * jnp.exp(gi)[..., None], S)
             + jnp.einsum('bhij,bhjv->bhiv', ai, vnew))
        glast = gi[..., -1:]
        S = (S * jnp.exp(glast)[..., None]
             + jnp.einsum('bhck,bhcv->bhkv', ki * jnp.exp(glast - gi)[..., None], vnew))
        return S, o

    s_fin, o = lax.scan(step, s0.astype(jnp.float32), (qc, kc, u, w, gcum, intra))
    return o.transpose(1, 0, 3, 2, 4).reshape(B, T, H, V), s_fin

def _mixer_conv_delta(h, buf_a, buf_qkv, s0, w_in, conv_a_w, conv_a_b, ln_a_g, ln_a_b, conv_qkv_w,
                      a_log, dt_bias, gdn_norm_g, w_out):
    B, T, _ = h.shape
    z = h @ w_in
    o1 = 2 * D_A
    o2 = o1 + QKV_W
    o3 = o2 + GDN_HEADS * GDN_DV
    o4 = o3 + GDN_HEADS
    glu = z[..., :D_A] * jax.nn.sigmoid(z[..., D_A:o1])
    ca, new_buf_a = _causal_dwconv(glu, buf_a, conv_a_w)
    ya = jax.nn.silu(_layernorm(ca + conv_a_b, ln_a_g, ln_a_b))
    qkv, new_buf_qkv = _causal_dwconv(z[..., o1:o2], buf_qkv, conv_qkv_w)
    qkv = jax.nn.silu(qkv)
    nq = GDN_HEADS * GDN_DK
    q = _l2norm(qkv[..., :nq].reshape(B, T, GDN_HEADS, GDN_DK)) * (GDN_DK ** -0.5)
    k = _l2norm(qkv[..., nq:2 * nq].reshape(B, T, GDN_HEADS, GDN_DK))
    v = qkv[..., 2 * nq:].reshape(B, T, GDN_HEADS, GDN_DV)
    gate = z[..., o2:o3].reshape(B, T, GDN_HEADS, GDN_DV)
    beta = jax.nn.sigmoid(z[..., o3:o4].astype(jnp.float32))
    g = -jnp.exp(a_log.astype(jnp.float32)) * jax.nn.softplus(z[..., o4:].astype(jnp.float32) + dt_bias.astype(jnp.float32))
    od, s_new = _gated_delta(q, k, v, g, beta, s0)
    od = _rmsnorm(od, gdn_norm_g) * jax.nn.silu(gate.astype(jnp.float32))
    mixed = jnp.concatenate([ya.astype(h.dtype), od.reshape(B, T, GDN_HEADS * GDN_DV).astype(h.dtype)], axis=-1)
    return mixed @ w_out, new_buf_a, new_buf_qkv, s_new

def _partial_rope(x, pos):
    half = ROT_DIM // 2
    inv = 1.0 / (ROPE_THETA ** (jnp.arange(0, ROT_DIM, 2, dtype=jnp.float32) / ROT_DIM))
    ang = pos.astype(jnp.float32)[:, None] * inv[None, :]
    cos = jnp.cos(ang)[None, :, None, None, :]
    sin = jnp.sin(ang)[None, :, None, None, :]
    xf = x.astype(jnp.float32)
    x1, x2 = xf[..., :half], xf[..., half:ROT_DIM]
    return jnp.concatenate([x1 * cos - x2 * sin, x2 * cos + x1 * sin, xf[..., ROT_DIM:]], axis=-1).astype(x.dtype)

def _c_qkv(h, pos, w_in):
    B, T, _ = h.shape
    qkv = (h @ w_in).reshape(B, T, 3, N_GROUPS, C_HEADS, C_HD)
    return _partial_rope(qkv[:, :, 0], pos), _partial_rope(qkv[:, :, 1], pos), qkv[:, :, 2]

def _dilated_band_attn(q, k, v, dil, band):
    B, S, H, E = q.shape
    n = S // dil
    nb = -(-n // ATT_BLOCK)
    pad = nb * ATT_BLOCK - n

    def split(t):
        t = t.astype(jnp.float32).reshape(B, n, dil, H, E).transpose(0, 2, 1, 3, 4)
        t = jnp.pad(t, ((0, 0), (0, 0), (0, pad), (0, 0), (0, 0)))
        return t.reshape(B, dil, nb, ATT_BLOCK, H, E)

    def with_prev(t):
        prev = jnp.pad(t, ((0, 0), (0, 0), (1, 0), (0, 0), (0, 0), (0, 0)))[:, :, :nb]
        return jnp.concatenate([prev, t], axis=3)

    qb = split(q)
    kk, vv = with_prev(split(k)), with_prev(split(v))
    s = jnp.einsum('brnqhe,brnkhe->brnqhk', qb, kk) * (E ** -0.5)
    qi = jnp.arange(ATT_BLOCK)[:, None]
    ki = jnp.arange(2 * ATT_BLOCK)[None, :]
    rel = ATT_BLOCK + qi - ki
    in_band = (rel >= 0) & (rel <= band)
    has_prev = (jnp.arange(nb)[:, None, None] > 0) | (ki[None] >= ATT_BLOCK)
    mask = (in_band[None] & has_prev)[:, :, None, :]
    s = jnp.where(mask, s, -jnp.inf)
    m = jnp.max(s, axis=-1, keepdims=True)
    p = jnp.exp(s - m)
    den = jnp.sum(p, axis=-1, keepdims=True)
    o = jnp.einsum('brnqhk,brnkhe->brnqhe', p, vv) / den
    lse = (m + jnp.log(den))[..., 0]
    o = o.reshape(B, dil, nb * ATT_BLOCK, H, E)[:, :, :n].transpose(0, 2, 1, 3, 4).reshape(B, S, H, E)
    lse = lse.reshape(B, dil, nb * ATT_BLOCK, H)[:, :, :n].transpose(0, 2, 1, 3).reshape(B, S, H)
    return o, lse

def _dilated_gather_attn(q, kv_all, L, dil, band):
    T = q.shape[1]
    E = q.shape[-1]
    idx = L + jnp.arange(T)[:, None] - dil * jnp.arange(band + 1)[None, :]
    valid = idx >= 0
    kvg = jnp.take(kv_all, jnp.maximum(idx, 0), axis=1).astype(jnp.float32)
    s = jnp.einsum('bthe,btjhe->bthj', q.astype(jnp.float32), kvg[:, :, :, 0]) * (E ** -0.5)
    s = jnp.where(valid[None, :, None, :], s, -jnp.inf)
    m = jnp.max(s, axis=-1, keepdims=True)
    p = jnp.exp(s - m)
    den = jnp.sum(p, axis=-1, keepdims=True)
    o = jnp.einsum('bthj,btjhe->bthe', p, kvg[:, :, :, 1]) / den
    return o, (m + jnp.log(den))[..., 0]

def _combine_groups(outs, lses, w_out, dtype):
    o = jnp.stack(outs)
    wts = jax.nn.softmax(jnp.stack(lses), axis=0)
    mixed = jnp.sum(wts[..., None] * o, axis=0)
    B, T = mixed.shape[:2]
    return mixed.reshape(B, T, C_HEADS * C_HD).astype(dtype) @ w_out

def _mixer_dilated_prompt(h, pos, w_in, w_out):
    T = h.shape[1]
    q, k, v = _c_qkv(h, pos, w_in)
    outs, lses, bufs = [], [], []
    for gi, (win, dil) in enumerate(C_PATTERNS):
        o, l = _dilated_band_attn(q[:, :, gi], k[:, :, gi], v[:, :, gi], dil, win // dil)
        outs.append(o)
        lses.append(l)
        keep = min(win, T)
        bufs.append(jnp.stack([k[:, T - keep:, gi], v[:, T - keep:, gi]], axis=2))
    return _combine_groups(outs, lses, w_out, h.dtype), bufs

def _mixer_dilated_sample(h, pos, caches, w_in, w_out):
    T = h.shape[1]
    q, k, v = _c_qkv(h, pos, w_in)
    outs, lses, bufs = [], [], []
    for gi, (win, dil) in enumerate(C_PATTERNS):
        cache = caches[gi]
        L = cache.shape[1]
        kv_new = jnp.stack([k[:, :, gi], v[:, :, gi]], axis=2).astype(cache.dtype)
        kv_all = jnp.concatenate([cache, kv_new], axis=1)
        o, l = _dilated_gather_attn(q[:, :, gi], kv_all, L, dil, win // dil)
        outs.append(o)
        lses.append(l)
        keep = min(win, L + T)
        bufs.append(kv_all[:, L + T - keep:])
    return _combine_groups(outs, lses, w_out, h.dtype), bufs

def _peer(x, w_q, sub_keys, u_tab, v_tab):
    lead = x.shape[:-1]
    xt = x.reshape(-1, D_MODEL)
    n = xt.shape[0]
    q = (xt @ w_q).reshape(n, PEER_HEADS, 2, PEER_HALF)
    s = jnp.einsum('nhck,hcmk->nhcm', q, sub_keys).astype(jnp.float32)
    ts, ti = lax.top_k(s, PEER_TOPK)
    cand_s = (ts[:, :, 0, :, None] + ts[:, :, 1, None, :]).reshape(n, PEER_HEADS, PEER_TOPK * PEER_TOPK)
    cand_i = (ti[:, :, 0, :, None] * N_KEYS + ti[:, :, 1, None, :]).reshape(n, PEER_HEADS, PEER_TOPK * PEER_TOPK)
    best_s, best_p = lax.top_k(cand_s, PEER_TOPK)
    idx = jnp.take_along_axis(cand_i, best_p, axis=-1)
    gate = jax.nn.softmax(best_s, axis=-1)
    nblk = -(-n // PEER_BLOCK)
    pad = nblk * PEER_BLOCK - n
    xb = jnp.pad(xt, ((0, pad), (0, 0))).reshape(nblk, PEER_BLOCK, D_MODEL)
    ib = jnp.pad(idx, ((0, pad), (0, 0), (0, 0))).reshape(nblk, PEER_BLOCK, PEER_HEADS, PEER_TOPK)
    gb = jnp.pad(gate, ((0, pad), (0, 0), (0, 0))).reshape(nblk, PEER_BLOCK, PEER_HEADS, PEER_TOPK)

    def block(args):
        xc, ic, gc = args
        ue = u_tab[ic]
        ve = v_tab[ic]
        a = jax.nn.gelu(jnp.einsum('nd,nhkd->nhk', xc, ue).astype(jnp.float32), approximate=False) * gc
        return jnp.einsum('nhk,nhkd->nd', a.astype(ve.dtype), ve)

    out = lax.map(block, (xb, ib, gb)).reshape(nblk * PEER_BLOCK, D_MODEL)[:n]
    return out.reshape(lead + (D_MODEL,))

def _tail(x, p, norm_ffn, peer_wq, peer_keys, peer_u, peer_v, norm_ple, ple_gate, ple_proj):
    x = x + _peer(_rmsnorm(x, norm_ffn), peer_wq, peer_keys, peer_u, peer_v).astype(x.dtype)
    gate = jax.nn.sigmoid((_rmsnorm(x, norm_ple) @ ple_gate).astype(jnp.float32))
    emb = (p.astype(x.dtype) @ ple_proj).astype(jnp.float32)
    return x + (gate * emb).astype(x.dtype)

def setup_inputs(seed: int = 0) -> dict:
    key = jax.random.key(seed)
    ks = iter(jax.random.split(key, 48))

    def nrm(shape, scale):
        return jax.random.normal(next(ks), shape, jnp.float32) * scale

    def gain(shape):
        return 1.0 + nrm(shape, 0.05)

    dt = jnp.exp(jax.random.uniform(next(ks), (N_EVEN, GDN_HEADS), jnp.float32,
                                    minval=float(np.log(1e-3)), maxval=float(np.log(1e-1))))
    return {
        'x_prompt': nrm((BATCH, SEQ, D_MODEL), 1.0),
        'x_sample': nrm((DEC_BATCH, DEC_SEQ, D_MODEL), 1.0),
        'state_conv_a': nrm((N_EVEN, DEC_BATCH, CONV_A_WIDTH - 1, D_A), 1.0),
        'state_conv_qkv': nrm((N_EVEN, DEC_BATCH, GDN_CONV - 1, QKV_W), 1.0),
        'state_delta': nrm((N_EVEN, DEC_BATCH, GDN_HEADS, GDN_DK, GDN_DV), 0.05),
        'cache_kv_w128': nrm((N_ODD, DEC_BATCH, min(C_PATTERNS[0][0], PAST_LEN), 2, C_HEADS, C_HD), 1.0),
        'cache_kv_w512': nrm((N_ODD, DEC_BATCH, min(C_PATTERNS[1][0], PAST_LEN), 2, C_HEADS, C_HD), 1.0),
        'cache_kv_w2048': nrm((N_ODD, DEC_BATCH, min(C_PATTERNS[2][0], PAST_LEN), 2, C_HEADS, C_HD), 1.0),
        'p_prompt': nrm((DEPTH, BATCH, SEQ, PLE_DIM), 1.0),
        'p_sample': nrm((DEPTH, DEC_BATCH, DEC_SEQ, PLE_DIM), 1.0),
        'norm_mix': gain((DEPTH, D_MODEL)),
        'norm_ffn': gain((DEPTH, D_MODEL)),
        'norm_ple': gain((DEPTH, D_MODEL)),
        'norm_final': gain((D_MODEL,)),
        'w_in_ab': nrm((N_EVEN, D_MODEL, IN_AB), D_MODEL ** -0.5),
        'conv_a_w': nrm((N_EVEN, CONV_A_WIDTH, D_A), CONV_A_WIDTH ** -0.5),
        'conv_a_b': nrm((N_EVEN, D_A), 0.02),
        'ln_a_g': gain((N_EVEN, D_A)),
        'ln_a_b': nrm((N_EVEN, D_A), 0.02),
        'conv_qkv_w': nrm((N_EVEN, GDN_CONV, QKV_W), GDN_CONV ** -0.5),
        'a_log': jnp.log(jax.random.uniform(next(ks), (N_EVEN, GDN_HEADS), jnp.float32, minval=1.0, maxval=16.0)),
        'dt_bias': dt + jnp.log(-jnp.expm1(-dt)),
        'gdn_norm_g': gain((N_EVEN, GDN_DV)),
        'w_out_ab': nrm((N_EVEN, D_A + GDN_HEADS * GDN_DV, D_MODEL), 0.5 * (D_A + GDN_HEADS * GDN_DV) ** -0.5),
        'w_in_c': nrm((N_ODD, D_MODEL, IN_C), D_MODEL ** -0.5),
        'w_out_c': nrm((N_ODD, C_HEADS * C_HD, D_MODEL), 0.5 * (C_HEADS * C_HD) ** -0.5),
        'peer_wq': nrm((DEPTH, D_MODEL, PEER_HEADS * PEER_DKEY), D_MODEL ** -0.5),
        'peer_keys': nrm((DEPTH, PEER_HEADS, 2, N_KEYS, PEER_HALF), PEER_HALF ** -0.5),
        'peer_u': nrm((DEPTH, N_EXPERTS, D_MODEL), D_MODEL ** -0.5),
        'peer_v': nrm((DEPTH, N_EXPERTS, D_MODEL), 0.3),
        'ple_gate': nrm((DEPTH, D_MODEL, D_MODEL), D_MODEL ** -0.5),
        'ple_proj': nrm((DEPTH, PLE_DIM, D_MODEL), 0.5 * PLE_DIM ** -0.5),
    }

def reference(x_prompt, x_sample, state_conv_a, state_conv_qkv, state_delta, cache_kv_w128, cache_kv_w512,
              cache_kv_w2048, p_prompt, p_sample, norm_mix, norm_ffn, norm_ple, norm_final, w_in_ab, conv_a_w,
              conv_a_b, ln_a_g, ln_a_b, conv_qkv_w, a_log, dt_bias, gdn_norm_g, w_out_ab, w_in_c, w_out_c,
              peer_wq, peer_keys, peer_u, peer_v, ple_gate, ple_proj):
    Bp, S = x_prompt.shape[0], x_prompt.shape[1]
    T = x_sample.shape[1]
    pos_p = jnp.arange(S)
    pos_s = PAST_LEN + jnp.arange(T)
    kv_caches = (cache_kv_w128, cache_kv_w512, cache_kv_w2048)
    xp, xs = x_prompt, x_sample
    pa, pq, pd, sa, sq, sd = [], [], [], [], [], []
    pkv = [[] for _ in C_PATTERNS]
    skv = [[] for _ in C_PATTERNS]
    for i in range(DEPTH):
        hp = _rmsnorm(xp, norm_mix[i])
        hs = _rmsnorm(xs, norm_mix[i])
        if i % 2 == 0:
            e = i // 2
            wts = (w_in_ab[e], conv_a_w[e], conv_a_b[e], ln_a_g[e], ln_a_b[e], conv_qkv_w[e],
                   a_log[e], dt_bias[e], gdn_norm_g[e], w_out_ab[e])
            yp, ba, bq, st = _mixer_conv_delta(
                hp, jnp.zeros((Bp, CONV_A_WIDTH - 1, D_A), hp.dtype), jnp.zeros((Bp, GDN_CONV - 1, QKV_W), hp.dtype),
                jnp.zeros((Bp, GDN_HEADS, GDN_DK, GDN_DV), jnp.float32), *wts)
            pa.append(ba)
            pq.append(bq)
            pd.append(st)
            ys, ba, bq, st = _mixer_conv_delta(hs, state_conv_a[e], state_conv_qkv[e], state_delta[e], *wts)
            sa.append(ba)
            sq.append(bq)
            sd.append(st)
        else:
            o = i // 2
            yp, bufs = _mixer_dilated_prompt(hp, pos_p, w_in_c[o], w_out_c[o])
            ys, bufs_s = _mixer_dilated_sample(hs, pos_s, [c[o] for c in kv_caches], w_in_c[o], w_out_c[o])
            for gi in range(N_GROUPS):
                pkv[gi].append(bufs[gi])
                skv[gi].append(bufs_s[gi])
        xp = xp + yp.astype(xp.dtype)
        xs = xs + ys.astype(xs.dtype)
        xp = _tail(xp, p_prompt[i], norm_ffn[i], peer_wq[i], peer_keys[i], peer_u[i], peer_v[i],
                   norm_ple[i], ple_gate[i], ple_proj[i])
        xs = _tail(xs, p_sample[i], norm_ffn[i], peer_wq[i], peer_keys[i], peer_u[i], peer_v[i],
                   norm_ple[i], ple_gate[i], ple_proj[i])
    y_prompt = _rmsnorm(xp, norm_final)
    y_sample = _rmsnorm(xs, norm_final)
    return (y_prompt, y_sample,
            jnp.stack(pa), jnp.stack(pq), jnp.stack(pd),
            jnp.stack(pkv[0]), jnp.stack(pkv[1]), jnp.stack(pkv[2]),
            jnp.stack(sa), jnp.stack(sq), jnp.stack(sd),
            jnp.stack(skv[0]), jnp.stack(skv[1]), jnp.stack(skv[2]))


_drawn_inputs = setup_inputs


def setup_inputs(seed=0):
    import zlib

    import numpy as np

    out = dict(_drawn_inputs(seed))
    spreads = {}
    factors = {'norm_ple': 4.461, 'ln_a_b': 3.23}
    for name, (base, spread) in spreads.items():
        noise = np.random.default_rng([zlib.crc32(name.encode()), seed]).standard_normal(out[name].shape)
        drawn = base * np.exp(spread * noise) if base else spread * noise
        out[name] = __import__('jax').numpy.asarray(drawn.astype(out[name].dtype))
    for name, factor in factors.items():
        out[name] = (out[name] * factor).astype(out[name].dtype)
    return out
```

```python
from contextlib import ExitStack

import numpy as np
import concourse.bass as bass
from concourse import mybir

F32 = mybir.dt.float32
U32 = mybir.dt.uint32
ALU = mybir.AluOpType
ACT = mybir.ActivationFunctionType
AX_X = mybir.AxisListType.X

D = 1024
KC = D // 128
SEQ, DEC_B, DEC_T = 256, 8, 4
PAST = 1024
NS = DEC_B * DEC_T
NTOK = SEQ + NS
TILES = ((0, 128), (128, 128), (256, NS))
DEPTH = 2
EPS = 1e-6
D_A = 512
CAW = 31
GH, GD = 4, 128
CQW = 4
QKV_W = 1536
IN_AB = 2 * D_A + QKV_W + GH * GD + 2 * GH
CHUNK = 64
PATTERNS = ((128, 1), (512, 4), (2048, 16))
NG, CH, HD = 3, 8, 128
ROT = HD // 4
THETA = 500000.0
NEG = -1.0e30
PH, NKEY, TOPK = 8, 128, 16
SLOTS = PH * TOPK
PLE = 256
ATT_SCALE = HD ** -0.5


class Chain:

    def __init__(self, eng, sem):
        self.eng, self.sem, self.n = eng, sem, 0

    def step(self, ins):
        self.n += 1
        ins.then_inc(self.sem, 1)

    def settle(self, lag=0):
        if self.n - lag > 0:
            self.eng.wait_ge(self.sem, self.n - lag)

    def __call__(self, ins):
        self.step(ins)
        self.settle()


class Phase:

    def __init__(self, nc, ctx, name, clears=True):
        self.nc, self.ctx, self.name, self.sems = nc, ctx, name, []
        if clears:
            ctx.callback(self.clear)

    def clear(self):
        if self.sems:
            self.nc.clear_and_free_semaphores(self.sems)
            self.nc.all_engine_barrier(sem_only=True)

    def sb(self, name, shape, dt=F32):
        return self.ctx.enter_context(self.nc.sbuf_tensor(f"{self.name}_{name}", shape, dt))

    def ps(self, name, shape):
        return self.ctx.enter_context(self.nc.psum_tensor(f"{self.name}_{name}", shape, F32))

    def sem(self, name):
        self.sems.append(self.nc.alloc_semaphore(f"{self.name}_{name}"))
        return self.sems[-1]


def broadcast_rows(dram_row, n, parts=128):
    return bass.AP(tensor=dram_row.tensor, offset=dram_row.offset, ap=[[0, parts], [1, n]])


def over(ap, axis, n):
    pat = [list(p) for p in ap.ap]
    pat.insert(axis, [0, n])
    return bass.AP(tensor=ap.tensor, offset=ap.offset, ap=pat)


def shape_constants():
    i = np.arange(128)
    c = {}
    c["ident"] = np.eye(128)
    tok = np.concatenate([np.arange(SEQ), PAST + np.tile(np.arange(DEC_T), DEC_B), np.zeros(96)])
    inv = 1.0 / (np.float32(THETA) ** (np.arange(0, ROT, 2, dtype=np.float32) / np.float32(ROT)))
    ang = (tok.astype(np.float32)[:, None] * inv.astype(np.float32)[None, :]).astype(np.float32)
    cos, sin = np.cos(ang.astype(np.float64)), np.sin(ang.astype(np.float64))
    cc = np.concatenate([cos, cos, -sin, sin], 1)
    c["rope"] = cc.reshape(3, 128, 64).transpose(1, 0, 2).reshape(128, 192)
    c["four"] = np.tile(np.eye(32), (4, 1))
    c["iota"] = np.tile(np.arange(16.0), (128, 1))
    g = []
    for size in (CHUNK, DEC_T):
        same = i[:, None] // size == i[None, :] // size
        g += [same & (i[:, None] <= i[None, :]), same, same & (i[:, None] > i[None, :])]
    for lev in range(6):
        s = 1 << lev
        g.append((i[:, None] // (2 * s) == i[None, :] // (2 * s))
                 & (i[:, None] % (2 * s) >= s) & (i[None, :] % (2 * s) < s))
    c["gdn"] = np.stack([m.astype(float) for m in g], 1).reshape(128, -1)
    c["owner"] = np.repeat((i[:32, None] // DEC_T == np.arange(DEC_B)[None]).astype(float), 1, 1)
    c["owner"] = np.tile(c["owner"], (4, 1))
    m = np.full((128, 2, NG, SEQ), NEG)
    for it in range(2):
        rel = (it * 128 + i)[:, None] - np.arange(SEQ)[None]
        for gi, (win, dil) in enumerate(PATTERNS):
            m[:, it, gi][(rel >= 0) & (rel % dil == 0) & (rel // dil <= win // dil)] = 0
    c["band"] = m.reshape(128, -1)
    s = np.full((128, 2, 7 * 128 + 3 * NS), NEG)
    for p in range(128):
        b4, t = p // 32, p % DEC_T
        for bb in range(2):
            b = bb * 4 + b4
            s[p, bb, t:128] = 0
            s[p, bb, 128 * (1 + t):128 * (2 + t)] = 0
            s[p, bb, 640 + 64 * t:640 + 64 * t + 64] = 0
            s[p, bb, 896 + b * DEC_T:896 + b * DEC_T + t + 1] = 0
            for gi in (1, 2):
                s[p, bb, 896 + gi * NS + b * DEC_T + t] = 0
    c["samp"] = s.reshape(128, -1)
    return {k: np.ascontiguousarray(v, dtype=np.float32) for k, v in c.items()}


def norm_phase(nc, name, K, gain, h, hT=None, out=None):
    x = K["x"]
    with ExitStack() as ctx:
        P = Phase(nc, ctx, name)
        gain_b, sq, st = P.sb("gain", [128, D]), P.sb("sq", [128, 3, D]), P.sb("st", [128, 3, 3])
        pt = [P.ps(f"pt{t}", [128, KC * 128]) for t in range(3)] if hT is not None else None
        gain_in, mean_ready, root_ready, rows_ready, cols_ready, stored, steps = (
            P.sem(s) for s in ("gain_in", "mean_ready", "root_ready", "rows_ready", "cols_ready", "stored",
                               "dve_steps"))
        hT_done = P.sem("hT_done")
        with nc.Block() as block:
            @block.sync
            def _(sp):
                sp.dma_start(gain_b[:], broadcast_rows(gain, D)).then_inc(gain_in, 16)
                if out is not None:
                    for t, (o, p) in enumerate(TILES):
                        sp.wait_ge(rows_ready, t + 1)
                        sp.dma_start(out[t], h[0:p, t, :]).then_inc(stored, 16)
                    sp.wait_ge(stored, 48)

            @block.scalar
            def _(act):
                act.wait_ge(mean_ready, 1)
                nc.scalar.activation(st[:, :, 1], st[:, :, 0], ACT.Sqrt).then_inc(root_ready, 1)
                if hT is not None:
                    for t, (o, p) in enumerate(TILES):
                        act.wait_ge(cols_ready, t + 1)
                        nc.scalar.activation(
                            hT[:, :, o:o + p], pt[t][:, 0:KC * 128].rearrange("q (k c) -> q k c", k=KC)[:, :, 0:p],
                            ACT.Copy).then_inc(hT_done, 1)

            @block.vector
            def _(dve):
                ch = Chain(dve, steps)
                ch(nc.vector.memset(st[:], 1.0))
                for t, (o, p) in enumerate(TILES):
                    ch.step(nc.vector.tensor_tensor_reduce(
                        out=sq[0:p, t, :], in0=x[0:p, t, :], in1=x[0:p, t, :], scale=1.0, scalar=0.0,
                        op0=ALU.mult, op1=ALU.add, accum_out=st[0:p, t, 0:1]))
                ch.settle()
                nc.vector.tensor_scalar(st[:, :, 0], st[:, :, 0], 1.0 / D, EPS, ALU.mult, ALU.add).then_inc(
                    mean_ready, 1)
                dve.wait_ge(root_ready, 1)
                ch(nc.vector.reciprocal(st[:, :, 2], st[:, :, 1]))
                dve.wait_ge(gain_in, 16)
                for t, (o, p) in enumerate(TILES):
                    nc.vector.scalar_tensor_tensor(
                        out=h[0:p, t, :], in0=x[0:p, t, :], scalar=st[0:p, t, 2:3], in1=gain_b[0:p, :],
                        op0=ALU.mult, op1=ALU.mult).then_inc(rows_ready, 1)

            if hT is not None:
                @block.tensor
                def _(pe):
                    for t, (o, p) in enumerate(TILES):
                        pe.wait_ge(rows_ready, t + 1)
                        for k in range(KC):
                            last = nc.tensor.transpose(pt[t][:, k * 128:k * 128 + p],
                                                       h[0:p, t, k * 128:(k + 1) * 128], K["ident"][0:p, 0:p])
                        last.then_inc(cols_ready, 1)


BANKS = 6


def linear_phase(nc, name, K, xT, w, kc, width, rows, consume, on="vector", ring=3, extra_sb=None,
                 stores=None):
    wv = w.rearrange("(k p) n -> p k n", p=128)
    chunks = [(c, min(512, width - c)) for c in range(0, width, 512)]
    with ExitStack() as ctx:
        P = Phase(nc, ctx, name)
        ring = min(ring, len(chunks))
        wt = P.sb("w", [128, ring, kc, 512])
        acc = [P.ps(f"acc{b}", [128, 512]) for b in range(BANKS)]
        w_in = [P.sem(f"w_in{r}") for r in range(ring)]
        product_ready, bank_free, steps = P.sem("product_ready"), P.sem("bank_free"), P.sem("steps")
        ex = extra_sb(P) if extra_sb else None
        parts = 3 if rows else 4
        jobs = [(c, s, part) for c, (_, n) in enumerate(chunks) for s in (c,)
                for part in range(parts if rows else n // 128)]
        done_by = [sum(1 for j in jobs if j[0] <= c) for c in range(len(chunks))]
        with nc.Block() as block:
            @block.sync
            def _(sp):
                for c, (c0, n) in enumerate(chunks):
                    if c >= ring:
                        sp.wait_ge(product_ready, done_by[c - ring])
                    sp.dma_start(wt[:, c % ring, :, 0:n], wv[:, :, c0:c0 + n]).then_inc(w_in[c % ring], 16)

            @block.tensor
            def _(pe):
                for n, (c, _, part) in enumerate(jobs):
                    if n == 0 or jobs[n - 1][0] != c:
                        pe.wait_ge(w_in[c % ring], 16 * (c // ring + 1))
                    if n >= BANKS:
                        pe.wait_ge(bank_free, n - BANKS + 1)
                    for k in range(kc):
                        if rows:
                            o, p = TILES[part]
                            last = nc.tensor.matmul(acc[n % BANKS][0:p, 0:chunks[c][1]], xT[:, k, o:o + p],
                                                    wt[:, c % ring, k, 0:chunks[c][1]],
                                                    start=(k == 0), stop=(k == kc - 1))
                        else:
                            last = nc.tensor.matmul(acc[n % BANKS][:, 0:NTOK],
                                                    wt[:, c % ring, k, part * 128:(part + 1) * 128],
                                                    xT[:, k, 0:NTOK], start=(k == 0), stop=(k == kc - 1))
                    last.then_inc(product_ready, 1)

            def take(eng):
                ch = Chain(eng, steps)
                for n, (c, _, part) in enumerate(jobs):
                    eng.wait_ge(product_ready, n + 1)
                    consume(eng, c, part, acc[n % BANKS], ch, ex).then_inc(bank_free, 1)

            if on == "vector":
                block.vector(take)
            else:
                block.scalar(take)


def add_rows_phase(nc, name, K, xT, w):
    x = K["x"]

    def consume(eng, c, part, acc, ch, ex):
        o, p = TILES[part]
        cols = x[0:p, part, c * 512:(c + 1) * 512]
        return nc.vector.tensor_tensor(cols, cols, acc[0:p, :], ALU.add)

    linear_phase(nc, name, K, xT, w, KC, D, True, consume)


def columns_phase(nc, name, K, xT, w, width, outT):
    def consume(eng, c, part, acc, ch, ex):
        return nc.scalar.activation(outT[:, c * 4 + part, :], acc[:, 0:NTOK], ACT.Copy)

    linear_phase(nc, name, K, xT, w, KC, width, False, consume, on="scalar")


def conv_phase(nc, name, K, T, zT, mixT, conv):
    with ExitStack() as ctx:
        P = Phase(nc, ctx, name)
        ra = P.sb("rows_state_a", [120, 2, D_A])
        rw = P.sb("rows_weights_a", [34, D_A])
        rq = P.sb("rows_qkv", [28, QKV_W])
        glu = P.sb("glu", [128, 4, NTOK])
        pa = P.sb("padded_a", [128, 4, CAW - 1 + SEQ])
        sa = P.sb("sample_a", [128, 4, DEC_B, CAW - 1 + DEC_T])
        pq = P.sb("padded_q", [128, 12, CQW - 1 + SEQ])
        sq = P.sb("sample_q", [128, 12, DEC_B, CQW - 1 + DEC_T])
        wa, wq = P.sb("taps_a", [128, 4, 34]), P.sb("taps_q", [128, 12, CQW])
        ca, tmp, ones = P.sb("conv_a", [128, 4, NTOK]), P.sb("tmp", [128, 8, NTOK]), P.sb("ones", [128, 128])
        root = P.sb("root", [128, 4, NTOK])
        tail_a, tail_q = P.sb("tail_a", [62, D_A]), P.sb("tail_q", [35, QKV_W])
        p_hist, p_w = P.ps("p_hist", [128, 1024]), P.ps("p_w", [128, 512])
        p_sum = P.ps("p_sum", [128, 4 * 512])
        loaded, hist_ready, w_ready, sig_ready = (
            P.sem(s) for s in ("loaded", "hist_ready", "w_ready", "sig_ready"))
        dve_steps, tail_ready, tail_copied, stored = (
            P.sem(s) for s in ("dve_steps", "tail_ready", "tail_copied", "stored"))
        sum_ready, root_ready, silu_ready, qkv_silu = (
            P.sem(s) for s in ("sum_ready", "root_ready", "silu_ready", "qkv_silu"))
        A0, Q0 = NTOK - NS - 30, NTOK - NS - 3

        mark = {}
        with nc.Block() as block:
            @block.vector
            def _(dve):
                ch = Chain(dve, dve_steps)
                V = nc.vector
                ch.step(V.memset(ones[:], 1.0))
                ch.step(V.memset(pa[:, :, 0:30], 0.0))
                ch.step(V.memset(pq[:, :, 0:3], 0.0))
                ch.step(V.tensor_copy(pq[:, :, 3:], zT[:, 8:20, 0:SEQ]))
                for c in range(12):
                    ch.step(V.tensor_copy(sq[:, c, :, 3:], zT[:, 8 + c, SEQ:].rearrange("p (b t) -> p b t", b=DEC_B)))
                dve.wait_ge(sig_ready, 1)
                ch(V.tensor_tensor(glu[:], zT[:, 0:4, :], zT[:, 4:8, :], ALU.mult))
                mark["glu"] = ch.n
                ch.step(V.tensor_copy(pa[:, :, 30:], glu[:, :, 0:SEQ]))
                for c in range(4):
                    ch.step(V.tensor_copy(sa[:, c, :, 30:], glu[:, c, SEQ:].rearrange("p (b t) -> p b t", b=DEC_B)))
                dve.wait_ge(hist_ready, 1)
                for hf in range(2):
                    for c in range(4):
                        ch.step(V.tensor_copy(
                            sa[:, c, hf * 4:hf * 4 + 4, 0:30],
                            p_hist[:, hf * 512 + c * 120:hf * 512 + (c + 1) * 120].rearrange(
                                "p (b t) -> p b t", b=4)))
                dve.wait_ge(w_ready, 1)
                ch.step(V.tensor_copy(wa[:], p_w[:, 0:136].rearrange("p (c r) -> p c r", c=4)))
                pw = p_w[:, 136:472].rearrange("p (c r) -> p c r", c=12)
                ch.step(V.tensor_copy(wq[:], pw[:, :, 24:28]))
                for c in range(12):
                    ch.step(V.tensor_copy(sq[:, c, :, 0:3], pw[:, c, 0:24].rearrange("p (b t) -> p b t", b=DEC_B)))
                ch.settle()

                def conv_taps(taps, tiles, pad, smp, wt, acc, bias):
                    for k in range(taps):
                        for c in range(tiles):
                            for part in range(2):
                                if k:
                                    ch.settle(lag=2 * tiles - 1)
                                if part == 0:
                                    src, dst = pad[:, c, k:k + SEQ], acc[:, c, 0:SEQ]
                                else:
                                    src = smp[:, c, :, k:k + DEC_T]
                                    dst = acc[:, c, SEQ:].rearrange("p (b t) -> p b t", b=DEC_B)
                                if k == 0 and bias is not None:
                                    ch.step(V.tensor_scalar(dst, src, wt[:, c, 0:1], bias(c), ALU.mult, ALU.add))
                                elif k == 0:
                                    ch.step(V.tensor_scalar(dst, src, wt[:, c, 0:1], None, ALU.mult))
                                else:
                                    ch.step(V.scalar_tensor_tensor(out=dst, in0=src, scalar=wt[:, c, k:k + 1],
                                                                   in1=dst, op0=ALU.mult, op1=ALU.add))
                    ch.settle()

                conv_taps(CQW, 12, pq, sq, wq, conv, None)
                mark["qkv"] = ch.n
                conv_taps(CAW, 4, pa, sa, wa, ca, lambda c: wa[:, c, 31:32])
                mark["sum", 0] = ch.n
                dve.wait_ge(sum_ready, 1)
                for c in range(4):
                    ch.step(V.scalar_tensor_tensor(out=ca[:, c, :], in0=p_sum[:, 0:NTOK], scalar=-1.0 / D_A,
                                                   in1=ca[:, c, :], op0=ALU.mult, op1=ALU.add))
                ch.settle()
                ch(V.tensor_tensor(tmp[:, 0:4, :], ca[:], ca[:], ALU.mult))
                mark["sum", 1] = ch.n
                dve.wait_ge(sum_ready, 2)
                ch(V.tensor_scalar(root[:, 0, :], p_sum[:, 0:NTOK], 1.0 / D_A, EPS, ALU.mult, ALU.add))
                mark["root", 0] = ch.n
                dve.wait_ge(root_ready, 1)
                ch(V.reciprocal(root[:, 0, :], root[:, 0, :]))
                for c in range(4):
                    ch.step(V.tensor_tensor(ca[:, c, :], ca[:, c, :], root[:, 0, :], ALU.mult))
                ch.settle()
                mark["silu"] = ch.n
                dve.wait_ge(qkv_silu, 1)
                ch(V.tensor_tensor(tmp[:], conv[:, 0:8, :], conv[:, 0:8, :], ALU.mult))
                for n in range(2):
                    mark["sum", 2 + n] = ch.n
                    dve.wait_ge(sum_ready, 3 + n)
                    ch(V.tensor_scalar(root[:], p_sum[:].rearrange("p (c n) -> p c n", c=4)[:, :, 0:NTOK], 1.0,
                                       EPS, ALU.mult, ALU.add))
                    mark["root", 1 + n] = ch.n
                    dve.wait_ge(root_ready, 2 + n)
                    ch(V.reciprocal(root[:], root[:]))
                    ch(V.scalar_tensor_tensor(out=conv[:, n * 4:n * 4 + 4, :], in0=conv[:, n * 4:n * 4 + 4, :],
                                              scalar=GD ** -0.5 if n == 0 else 1.0, in1=root[:],
                                              op0=ALU.mult, op1=ALU.mult))

            @block.sync
            def _(sp):
                st = T["state_conv_a"][0].rearrange("b r c -> (b r) c")
                for hf in range(2):
                    sp.dma_start(ra[:, hf, :], st[hf * 120:(hf + 1) * 120, :]).then_inc(loaded, 16)
                sp.dma_start(rw[0:31, :], T["conv_a_w"][0]).then_inc(loaded, 16)
                for n, w in enumerate(("conv_a_b", "ln_a_g", "ln_a_b")):
                    sp.dma_start(rw[31 + n:32 + n, :], T[w]).then_inc(loaded, 16)
                sp.dma_start(rq[0:24, :], T["state_conv_qkv"][0].rearrange("b r c -> (b r) c")).then_inc(loaded, 16)
                sp.dma_start(rq[24:28, :], T["conv_qkv_w"][0]).then_inc(loaded, 16)
                sp.dma_start(T["out_conv_a_s"][0, :, 0:26, :], T["state_conv_a"][0, :, 4:30, :]).then_inc(stored, 16)
                sp.wait_ge(tail_copied, 4)
                sp.dma_start(T["out_conv_a_p"][0, 0], tail_a[0:30, :]).then_inc(stored, 16)
                sp.dma_start(T["out_conv_qkv_p"][0, 0], tail_q[0:3, :]).then_inc(stored, 16)
                for b in range(DEC_B):
                    sp.dma_start(T["out_conv_a_s"][0, b, 26:30, :],
                                 tail_a[30 + 4 * b:34 + 4 * b, :]).then_inc(stored, 16)
                    sp.dma_start(T["out_conv_qkv_s"][0, b, :, :],
                                 tail_q[4 + 4 * b:7 + 4 * b, :]).then_inc(stored, 16)
                sp.wait_ge(stored, 16 * (3 + 2 * DEC_B))

            @block.tensor
            def _(pe):
                idn = K["ident"]
                pe.wait_ge(loaded, 128)
                for hf in range(2):
                    for c in range(4):
                        last = nc.tensor.transpose(p_hist[:, hf * 512 + c * 120:hf * 512 + (c + 1) * 120],
                                                   ra[0:120, hf, c * 128:(c + 1) * 128], idn[0:120, 0:120])
                last.then_inc(hist_ready, 1)
                for c in range(4):
                    nc.tensor.transpose(p_w[:, c * 34:(c + 1) * 34], rw[0:34, c * 128:(c + 1) * 128],
                                        idn[0:34, 0:34])
                for c in range(12):
                    last = nc.tensor.transpose(p_w[:, 136 + c * 28:136 + (c + 1) * 28],
                                               rq[0:28, c * 128:(c + 1) * 128], idn[0:28, 0:28])
                last.then_inc(w_ready, 1)
                pe.wait_ge(dve_steps, mark["glu"])
                for r in range(4):
                    for c in range(4):
                        if r == 0:
                            last = nc.tensor.transpose(p_sum[0:62, c * 128:(c + 1) * 128], glu[:, c, A0:NTOK], idn[:])
                        else:
                            last = nc.tensor.transpose(p_sum[0:35, r * 512 + c * 128:r * 512 + (c + 1) * 128],
                                                       zT[:, 8 + (r - 1) * 4 + c, Q0:NTOK], idn[:])
                    last.then_inc(tail_ready, 1)
                for n in range(4):
                    pe.wait_ge(dve_steps, mark["sum", n])
                    pe.wait_ge(tail_copied, 4)
                    src = ca if n == 0 else tmp
                    for c in range(4):
                        dst = p_sum[:, 0:NTOK] if n < 2 else p_sum[:, c * 512:c * 512 + NTOK]
                        s = src[:, (n == 3) * 4 + c, :]
                        last = nc.tensor.matmul(dst, ones[:], s, start=(c == 0 or n > 1), stop=(c == 3 or n > 1))
                    last.then_inc(sum_ready, 1)

            @block.scalar
            def _(act):
                nc.scalar.activation(zT[:, 4:8, :], zT[:, 4:8, :], ACT.Sigmoid).then_inc(sig_ready, 1)
                for r in range(4):
                    act.wait_ge(tail_ready, r + 1)
                    src = p_sum[0:62 if r == 0 else 35, r * 512:(r + 1) * 512]
                    dst = tail_a[:] if r == 0 else tail_q[:, (r - 1) * 512:r * 512]
                    nc.scalar.activation(dst, src, ACT.Copy).then_inc(tail_copied, 1)
                act.wait_ge(dve_steps, mark["qkv"])
                nc.scalar.activation(conv[:], conv[:], ACT.Silu).then_inc(qkv_silu, 1)
                act.wait_ge(dve_steps, mark["root", 0])
                nc.scalar.activation(root[:, 0, :], root[:, 0, :], ACT.Sqrt).then_inc(root_ready, 1)
                act.wait_ge(dve_steps, mark["silu"])
                for c in range(4):
                    nc.scalar.activation(mixT[:, c, :], ca[:, c, :], ACT.Silu, scale=wa[:, c, 32:33],
                                         bias=wa[:, c, 33:34]).then_inc(silu_ready, 1)
                for n in (1, 2):
                    act.wait_ge(dve_steps, mark["root", n])
                    nc.scalar.activation(root[:], root[:], ACT.Sqrt).then_inc(root_ready, 1)
                act.wait_ge(silu_ready, 4)


def delta_phase(nc, name, K, T, hT, zT, conv, mixT):
    levels = (6, 6, 2)
    order = ["ab pe", "ab dve", "ab act", "g dve"]
    for t in range(3):
        order += [f"{t} gsum pe", f"{t} gsum dve", f"{t} wide pe", f"{t} args dve", f"{t} exps act",
                  f"{t} cross pe", f"{t} prep dve"]
        for lev in range(levels[t]):
            order += [f"{t} P {lev} pe", f"{t} P {lev} dve", f"{t} X {lev} pe", f"{t} X {lev} dve"]
        order += [f"{t} solve pe", f"{t} solve dve"]
    for n in range(4):
        order += [f"c{n} wS pe", f"c{n} v dve", f"c{n} o pe", f"c{n} S dve"]
    order += ["s wS pe", "s wS dve", "s wST pe", "s v dve", "s o pe", "s o dve"]
    for h in range(GH):
        order += [f"s S {h} pe", f"s S {h} dve"]
    order += ["sum pe", "root dve", "root act", "out dve"]
    at = {n: i for i, n in enumerate(order)}

    with ExitStack() as ctx:
        P = Phase(nc, ctx, name)
        cst = P.sb("masks", [128, 12, 128])
        own = P.sb("owner", [128, DEC_B])
        wab = P.sb("w_ab", [128, KC, 8])
        alog, dtb, gn = P.sb("a_log", [128, 4]), P.sb("dt_bias", [128, 4]), P.sb("norm_gain", [128, 1])
        ab, gt = P.sb("ab", [128, 3, 8]), P.sb("g_tmp", [128, 3, 4])
        beta, g = P.sb("beta", [128, 3, 4]), P.sb("g", [128, 3, 4])
        gc = P.sb("gc", [128, 5, 4])
        gbc = P.sb("g_wide", [128, 4, 128])
        dec, decT = P.sb("decay", [128, 4, 128]), P.sb("decayT", [128, 4, 128])
        eg = P.sb("exp_gcum", [128, 3, 4, 128])
        L, Lm = P.sb("L", [128, 4, 128]), P.sb("Lm", [128, 4, 128])
        X, XT, P1 = P.sb("X", [128, 4, 128]), P.sb("XT", [128, 4, 128]), P.sb("P1", [128, 4, 128])
        inT = P.sb("intraT", [128, 3, 4, 128])
        Rv, Rk, kd = P.sb("Rv", [128, 4, 128]), P.sb("Rk", [128, 4, 128]), P.sb("k_decay", [128, 3, 4, 128])
        u, wT, qe = P.sb("u", [128, 3, 4, 128]), P.sb("wT", [128, 3, 4, 128]), P.sb("q_exp", [128, 3, 4, 128])
        S, vn = P.sb("S", [128, 4, 128]), P.sb("v_new", [128, 4, 128])
        S0 = P.sb("S_sample", [128, DEC_B, 4, 128])
        wS, vm = P.sb("wS", [128, 4, 32]), P.sb("v_owner", [32, DEC_B, 128])
        oT, ones = P.sb("oT", [128, 4, NTOK]), P.sb("ones", [128, 128])
        sqr = P.sb("sqr", [128, 4, NTOK])
        bank = [P.ps(f"bank{i}", [128, 512]) for i in range(8)]
        loaded, turn, dve_steps, act_steps, stored = (
            P.sem(s) for s in ("loaded", "turn", "dve_steps", "act_steps", "stored"))
        heads = [b[:].rearrange("q (h c) -> q h c", h=4) for b in bank]
        ident = K["ident"]
        GM = lambda t, k: cst[:, (3 if t == 2 else 0) + k, :]

        def begin(eng, what):
            if at[what]:
                eng.wait_ge(turn, at[what])

        with nc.Block() as block:
            @block.sync
            def _(sp):
                sp.dma_start(wab[:], T["w_in_ab"][0].rearrange("(k p) n -> p k n", p=128)[:, :, IN_AB - 8:IN_AB]
                             ).then_inc(loaded, 16)
                sp.dma_start(cst[:], T["c_gdn"].rearrange("p (k n) -> p k n", k=12)).then_inc(loaded, 16)
                sp.dma_start(own[:], T["c_owner"]).then_inc(loaded, 16)
                sp.dma_start(alog[:], broadcast_rows(T["a_log"], 4)).then_inc(loaded, 16)
                sp.dma_start(dtb[:], broadcast_rows(T["dt_bias"], 4)).then_inc(loaded, 16)
                sp.dma_start(gn[:], T["gdn_norm_g"].rearrange("a n -> n a")).then_inc(loaded, 16)
                for b in range(DEC_B):
                    sp.dma_start(S0[:, b, :, :], T["state_delta"][0, b].rearrange("h k v -> k h v")
                                 ).then_inc(loaded, 16)
                sp.wait_ge(turn, at["c3 S dve"] + 1)
                sp.dma_start(T["out_delta_p"][0, 0].rearrange("h k v -> k h v"), S[:]).then_inc(stored, 16)
                sp.wait_ge(turn, at[f"s S {GH - 1} dve"] + 1)
                for b in range(DEC_B):
                    sp.dma_start(T["out_delta_s"][0, b].rearrange("h k v -> k h v"), S0[:, b, :, :]
                                 ).then_inc(stored, 16)
                sp.wait_ge(stored, 16 * (1 + DEC_B))

            @block.tensor
            def _(pe):
                mm = nc.tensor.matmul
                pe.wait_ge(loaded, 16 * (6 + DEC_B))
                for t, (o, p) in enumerate(TILES):
                    for k in range(KC):
                        last = mm(bank[0][0:p, t * 8:t * 8 + 8], hT[:, k, o:o + p], wab[:, k, :],
                                  start=(k == 0), stop=(k == KC - 1))
                last.then_inc(turn, 1)
                for t, (o, p) in enumerate(TILES):
                    begin(pe, f"{t} gsum pe")
                    mm(bank[0][0:p, 0:4], GM(t, 0)[0:p, 0:p], g[0:p, t, :], start=True, stop=True)
                    mm(bank[0][0:p, 4:8], GM(t, 1)[0:p, 0:p], g[0:p, t, :], start=True, stop=True).then_inc(turn, 1)
                    begin(pe, f"{t} wide pe")
                    for h in range(GH):
                        last = mm(heads[1][:, h, 0:p], gbc[0:p, h, :], GM(t, 0)[0:p, 0:p], start=True, stop=True)
                    last.then_inc(turn, 1)
                    begin(pe, f"{t} cross pe")
                    for h in range(GH):
                        kk, qq, vv = conv[:, 4 + h, o:o + p], conv[:, h, o:o + p], conv[:, 8 + h, o:o + p]
                        mm(heads[2][0:p, h, 0:p], kk, kk, start=True, stop=True)
                        mm(heads[3][0:p, h, 0:p], kk, qq, start=True, stop=True)
                        nc.tensor.transpose(heads[4][0:p, h, :], kk, ident[:])
                        last = nc.tensor.transpose(heads[5][0:p, h, :], vv, ident[:])
                    last.then_inc(turn, 1)
                    for lev in range(levels[t]):
                        begin(pe, f"{t} P {lev} pe")
                        for h in range(GH):
                            last = mm(heads[6][0:p, h, 0:p], Lm[0:p, h, 0:p], XT[0:p, h, 0:p], start=True, stop=True)
                        last.then_inc(turn, 1)
                        begin(pe, f"{t} X {lev} pe")
                        for h in range(GH):
                            mm(heads[7][0:p, h, 0:p], P1[0:p, h, 0:p], X[0:p, h, 0:p], start=True, stop=True)
                            last = mm(heads[0][0:p, h, 0:p], X[0:p, h, 0:p], P1[0:p, h, 0:p], start=True, stop=True)
                        last.then_inc(turn, 1)
                    begin(pe, f"{t} solve pe")
                    for h in range(GH):
                        mm(heads[1][0:p, h, :], XT[0:p, h, 0:p], Rv[0:p, h, :], start=True, stop=True)
                        last = mm(heads[2][:, h, 0:p], Rk[0:p, h, :], XT[0:p, h, 0:p], start=True, stop=True)
                    last.then_inc(turn, 1)
                for n in range(4):
                    t, r = n // 2, slice(n % 2 * CHUNK, (n % 2 + 1) * CHUNK)
                    begin(pe, f"c{n} wS pe")
                    for h in range(GH):
                        last = mm(heads[3][r, h, :], wT[:, t, h, r], S[:, h, :], start=True, stop=True)
                    last.then_inc(turn, 1)
                    begin(pe, f"c{n} o pe")
                    for h in range(GH):
                        mm(heads[4][:, h, 0:CHUNK], S[:, h, :], qe[:, t, h, r], start=True, stop=False)
                        mm(heads[4][:, h, 0:CHUNK], vn[r, h, :], inT[r, t, h, r], start=False, stop=True)
                        last = mm(heads[5][:, h, :], kd[r, t, h, :], vn[r, h, :], start=True, stop=True)
                    last.then_inc(turn, 1)
                begin(pe, "s wS pe")
                for h in range(GH):
                    for b in range(DEC_B):
                        last = mm(heads[3][:, h, 4 * b:4 * b + 4], S0[:, b, h, :], wT[:, 2, h, 4 * b:4 * b + 4],
                                  start=True, stop=True)
                last.then_inc(turn, 1)
                begin(pe, "s wST pe")
                for h in range(GH):
                    last = nc.tensor.transpose(heads[4][0:NS, h, :], wS[:, h, :], ident[:])
                last.then_inc(turn, 1)
                begin(pe, "s o pe")
                for h in range(GH):
                    mm(heads[5][:, h, 0:NS], vn[0:NS, h, :], inT[0:NS, 2, h, 0:NS], start=True, stop=True)
                    for b in range(DEC_B):
                        last = mm(heads[3][:, h, 4 * b:4 * b + 4], S0[:, b, h, :], qe[:, 2, h, 4 * b:4 * b + 4],
                                  start=True, stop=True)
                last.then_inc(turn, 1)
                for h in range(GH):
                    begin(pe, f"s S {h} pe")
                    for hf in range(2):
                        last = mm(bank[6 + hf][:], kd[0:NS, 2, h, :], vm[:, hf * 4:hf * 4 + 4, :], start=True, stop=True)
                    last.then_inc(turn, 1)
                begin(pe, "sum pe")
                for h in range(GH):
                    last = mm(bank[h][:, 0:NTOK], ones[:], sqr[:, h, :], start=True, stop=True)
                last.then_inc(turn, 1)

            @block.scalar
            def _(act):
                ch = Chain(act, act_steps)
                A = nc.scalar.activation
                begin(act, "ab act")
                ch.step(A(beta[:], ab[:, :, 0:4], ACT.Sigmoid))
                ch.step(A(alog[:], alog[:], ACT.Exp))
                ch(A(gt[:], gt[:], ACT.Exp, scale=-1.0))
                A(gt[:], gt[:], ACT.Ln, bias=1.0).then_inc(turn, 1)
                for t, (o, p) in enumerate(TILES):
                    begin(act, f"{t} exps act")
                    A(dec[0:p, :, 0:p], dec[0:p, :, 0:p], ACT.Exp, scale=-1.0)
                    A(decT[0:p, :, 0:p], decT[0:p, :, 0:p], ACT.Exp)
                    A(eg[:, t, :, 0:p], heads[1][:, :, 0:p], ACT.Exp)
                    A(gc[0:p, 2:4, :], gc[0:p, 2:4, :], ACT.Exp).then_inc(turn, 1)
                begin(act, "root act")
                A(sqr[:], sqr[:], ACT.Sqrt)
                A(zT[:, 20:24, :], zT[:, 20:24, :], ACT.Silu).then_inc(turn, 1)

            @block.vector
            def _(dve):
                ch = Chain(dve, dve_steps)
                V = nc.vector
                TT, TS, STT = V.tensor_tensor, V.tensor_scalar, V.scalar_tensor_tensor
                ch.step(V.memset(ab[:], 0.0))
                ch.step(V.memset(ones[:], 1.0))
                ch(V.memset(S[:], 0.0))
                begin(dve, "ab dve")
                for t, (o, p) in enumerate(TILES):
                    ch.step(V.tensor_copy(ab[0:p, t, :], bank[0][0:p, t * 8:t * 8 + 8]))
                ch.settle()
                ch(TT(ab[:, :, 4:8], ab[:, :, 4:8], over(dtb[:], 1, 3), ALU.add))
                ch(TS(gt[:], ab[:, :, 4:8], -1.0, None, ALU.mult))
                TT(gt[:], gt[:], ab[:, :, 4:8], ALU.max).then_inc(turn, 1)
                begin(dve, "g dve")
                ch(STT(out=gt[:], in0=ab[:, :, 4:8], scalar=0.0, in1=gt[:], op0=ALU.max, op1=ALU.add))
                STT(out=g[:], in0=gt[:], scalar=-1.0, in1=over(alog[:], 1, 3), op0=ALU.mult,
                    op1=ALU.mult).then_inc(turn, 1)
                for t, (o, p) in enumerate(TILES):
                    begin(dve, f"{t} gsum dve")
                    ch.step(V.tensor_copy(gc[0:p, 0:2, :], bank[0][0:p, 0:8].rearrange("q (a h) -> q a h", a=2)))
                    V.tensor_copy(gbc[0:p, :, :], over(g[0:p, t, :], 2, 128)).then_inc(turn, 1)
                    begin(dve, f"{t} args dve")
                    ch.settle()
                    for h in range(GH):
                        ch.step(TS(dec[0:p, h, 0:p], heads[1][0:p, h, 0:p], gc[0:p, 0, h:h + 1], 0.0,
                                   ALU.subtract, ALU.max))
                        ch.step(TS(decT[0:p, h, 0:p], heads[1][0:p, h, 0:p], gc[0:p, 0, h:h + 1], 0.0,
                                   ALU.subtract, ALU.min))
                    ch.step(V.tensor_copy(gc[0:p, 2, :], gc[0:p, 0, :]))
                    TT(gc[0:p, 3, :], gc[0:p, 1, :], gc[0:p, 0, :], ALU.subtract).then_inc(turn, 1)
                    begin(dve, f"{t} prep dve")
                    ch.step(TT(gc[0:p, 4, :], gc[0:p, 2, :], beta[0:p, t, :], ALU.mult))
                    ch.step(TT(qe[:, t, :, 0:p], conv[:, 0:4, o:o + p], eg[:, t, :, 0:p], ALU.mult))
                    ch.step(TT(inT[0:p, t, :, 0:p], heads[3][0:p, :, 0:p], decT[0:p, :, 0:p], ALU.mult))
                    ch.step(V.tensor_copy(X[0:p, :, 0:p], over(ident[0:p, 0:p], 1, 4)))
                    ch.step(V.tensor_copy(XT[0:p, :, 0:p], over(ident[0:p, 0:p], 1, 4)))
                    ch.settle()
                    for h in range(GH):
                        ch.step(STT(out=L[0:p, h, 0:p], in0=heads[2][0:p, h, 0:p], scalar=beta[0:p, t, h:h + 1],
                                    in1=dec[0:p, h, 0:p], op0=ALU.mult, op1=ALU.mult))
                        ch.step(TS(Rv[0:p, h, :], heads[5][0:p, h, :], beta[0:p, t, h:h + 1], None, ALU.mult))
                        ch.step(TS(Rk[0:p, h, :], heads[4][0:p, h, :], gc[0:p, 4, h:h + 1], None, ALU.mult))
                        ch.step(TS(kd[0:p, t, h, :], heads[4][0:p, h, :], gc[0:p, 3, h:h + 1], None, ALU.mult))
                    ch(TT(inT[0:p, t, :, 0:p], inT[0:p, t, :, 0:p], over(GM(t, 0)[0:p, 0:p], 1, 4), ALU.mult))
                    ch(TT(L[0:p, :, 0:p], L[0:p, :, 0:p], over(GM(t, 2)[0:p, 0:p], 1, 4), ALU.mult))
                    mask = lambda lev: over(cst[0:p, 6 + lev, 0:p], 1, 4)
                    TT(Lm[0:p, :, 0:p], L[0:p, :, 0:p], mask(0), ALU.mult).then_inc(turn, 1)
                    for lev in range(levels[t]):
                        begin(dve, f"{t} P {lev} dve")
                        V.tensor_copy(P1[0:p, :, 0:p], heads[6][0:p, :, 0:p]).then_inc(turn, 1)
                        begin(dve, f"{t} X {lev} dve")
                        ch.step(TT(X[0:p, :, 0:p], X[0:p, :, 0:p], heads[7][0:p, :, 0:p], ALU.subtract))
                        if lev + 1 < levels[t]:
                            ch.step(TT(Lm[0:p, :, 0:p], L[0:p, :, 0:p], mask(lev + 1), ALU.mult))
                        TT(XT[0:p, :, 0:p], XT[0:p, :, 0:p], heads[0][0:p, :, 0:p], ALU.subtract).then_inc(turn, 1)
                    begin(dve, f"{t} solve dve")
                    ch.step(V.tensor_copy(u[0:p, t, :, :], heads[1][0:p, :, :]))
                    V.tensor_copy(wT[:, t, :, 0:p], heads[2][:, :, 0:p]).then_inc(turn, 1)
                for n in range(4):
                    t, r = n // 2, slice(n % 2 * CHUNK, (n % 2 + 1) * CHUNK)
                    begin(dve, f"c{n} v dve")
                    ch.settle()
                    TT(vn[r, :, :], u[r, t, :, :], heads[3][r, :, :], ALU.subtract).then_inc(turn, 1)
                    begin(dve, f"c{n} S dve")
                    ch.step(V.tensor_copy(oT[:, :, n * CHUNK:(n + 1) * CHUNK], heads[4][:, :, 0:CHUNK]))
                    for h in range(GH):
                        last = STT(out=S[:, h, :], in0=S[:, h, :], scalar=eg[:, t, h, r.stop - 1:r.stop],
                                   in1=heads[5][:, h, :], op0=ALU.mult, op1=ALU.add)
                    last.then_inc(turn, 1)
                begin(dve, "s wS dve")
                V.tensor_copy(wS[:], heads[3][:, :, 0:NS]).then_inc(turn, 1)
                begin(dve, "s v dve")
                TT(vn[0:NS, :, :], u[0:NS, 2, :, :], heads[4][0:NS, :, :], ALU.subtract).then_inc(turn, 1)
                begin(dve, "s o dve")
                ch(V.tensor_copy(oT[:, :, SEQ:], heads[5][:, :, 0:NS]))
                ch.step(TT(oT[:, :, SEQ:], oT[:, :, SEQ:], heads[3][:, :, 0:NS], ALU.add))
                for h in range(GH):
                    glast = eg[:, 2, h, 0:NS].rearrange("p (b t) -> p b t", t=DEC_T)[:, :, DEC_T - 1]
                    ch.step(TT(S0[:, :, h, :], S0[:, :, h, :], over(glast, 2, 128), ALU.mult))
                ch.settle()
                for h in range(GH):
                    if h:
                        begin(dve, f"s S {h - 1} dve")
                        for hf in range(2):
                            d = S0[:, hf * 4:hf * 4 + 4, h - 1, :]
                            ch.step(TT(d, d, heads[6 + hf], ALU.add))
                        ch.settle()
                    TT(vm[:], over(vn[0:NS, h, :], 1, DEC_B), over(own[0:NS, :], 2, 128), ALU.mult).then_inc(turn, 1)
                begin(dve, f"s S {GH - 1} dve")
                for hf in range(2):
                    d = S0[:, hf * 4:hf * 4 + 4, GH - 1, :]
                    ch.step(TT(d, d, heads[6 + hf], ALU.add))
                ch.settle()
                TT(sqr[:], oT[:], oT[:], ALU.mult).then_inc(turn, 1)
                begin(dve, "root dve")
                for h in range(GH):
                    last = TS(sqr[:, h, :], bank[h][:, 0:NTOK], 1.0 / GD, EPS, ALU.mult, ALU.add)
                last.then_inc(turn, 1)
                begin(dve, "out dve")
                ch.step(TS(oT[:], oT[:], gn[:, 0:1], None, ALU.mult))
                ch(V.reciprocal(sqr[:], sqr[:]))
                ch(TT(oT[:], oT[:], sqr[:], ALU.mult))
                TT(mixT[:, 4:8, :], oT[:], zT[:, 20:24, :], ALU.mult).then_inc(turn, 1)


def keys_phase(nc, name, K, keys, keysT):
    with ExitStack() as ctx:
        P = Phase(nc, ctx, name)
        rows = P.sb("rows", [128, 2 * PH, 64])
        pt = P.ps("pt", [128, PH * 128])
        loaded, ready, copied = P.sem("loaded"), P.sem("ready"), P.sem("copied")
        with nc.Block() as block:
            @block.sync
            def _(sp):
                sp.dma_start(rows[:], keys.rearrange("h c m k -> m (h c) k")).then_inc(loaded, 16)

            @block.tensor
            def _(pe):
                pe.wait_ge(loaded, 16)
                for h in range(PH):
                    last = nc.tensor.transpose(pt[:, h * 128:(h + 1) * 128], rows[:, 2 * h:2 * h + 2, :],
                                               K["ident"][:])
                last.then_inc(ready, 1)

            @block.scalar
            def _(act):
                act.wait_ge(ready, 1)
                nc.scalar.activation(keysT[:], pt[:].rearrange("p (h m) -> p h m", h=PH), ACT.Copy).then_inc(copied, 1)


def topk_phase(nc, name, K, T, qT, keysT, layer, R):
    NH2 = 2 * PH
    with ExitStack() as ctx:
        P = Phase(nc, ctx, name)
        iota = P.sb("iota", [128, 16])
        sc = P.sb("scores", [128, NH2, NKEY])
        ts, ti = P.sb("top", [128, NH2, TOPK]), P.sb("top_at", [128, NH2, TOPK], U32)
        tif = P.sb("top_at_f", [128, NH2, TOPK])
        cand = P.sb("cand", [128, PH, TOPK * TOPK])
        cand2 = P.sb("cand2", [128, PH, TOPK * TOPK])
        bs, bp = P.sb("best", [128, PH, TOPK]), P.sb("best_at", [128, PH, TOPK], U32)
        be = P.sb("best_exp", [128, PH, TOPK])
        part, partf = P.sb("part", [128, 2, SLOTS], U32), P.sb("part_f", [128, 2, SLOTS])
        hot = P.sb("one_hot", [128, SLOTS, TOPK])
        rowf, idx3 = P.sb("row_f", [128, 2, SLOTS]), P.sb("row_s", [NS, SLOTS], U32)
        gate = R["gate"]
        gate3, total = P.sb("gate_s", [NS, SLOTS]), P.sb("total", [128, PH])
        ps = P.ps("ps", [128, NH2 * NKEY])
        loaded, score_ready, score_free, exp_in, exp_ready, dve_steps, table_ready, moved = (
            P.sem(s) for s in ("loaded", "score_ready", "score_free", "exp_in", "exp_ready", "dve_steps",
                               "table_ready", "moved"))
        mark = {}
        col = lambda n: (n % 2 * PH + n // 2) * NKEY
        with nc.Block() as block:
            @block.vector
            def _(dve):
                ch = Chain(dve, dve_steps)
                V = nc.vector
                dve.wait_ge(loaded, 16)
                for t, (o, p) in enumerate(TILES):
                    dve.wait_ge(score_ready, t + 1)
                    s_in = lambda n: ps[0:p, col(n):col(n) + NKEY]
                    for n in range(NH2):
                        ch.step(V.max(ts[0:p, n, 0:8], s_in(n)))
                    for n in range(NH2):
                        ch.settle(lag=NH2 - 1)
                        ch.step(V.match_replace(sc[0:p, n, :], ts[0:p, n, 0:8], s_in(n), NEG))
                    for n in range(NH2):
                        ch.settle(lag=NH2 - 1)
                        ch.step(V.max(ts[0:p, n, 8:16], sc[0:p, n, :]))
                    for n in range(NH2):
                        ch.step(V.max_index(ti[0:p, n, 0:8], ts[0:p, n, 0:8], s_in(n)))
                    mark["scores", t] = ch.n
                    for n in range(NH2):
                        ch.settle(lag=2 * NH2 - 1)
                        ch.step(V.max_index(ti[0:p, n, 8:16], ts[0:p, n, 8:16], sc[0:p, n, :]))
                    ch.settle()
                    ch.step(V.tensor_copy(tif[0:p], ti[0:p]))
                    for h in range(PH):
                        ch.step(V.tensor_tensor(cand[0:p, h, :].rearrange("q (a b) -> q a b", a=TOPK),
                                                over(ts[0:p, 2 * h, :], 2, TOPK), over(ts[0:p, 2 * h + 1, :], 1, TOPK),
                                                ALU.add))
                    ch.settle()
                    for h in range(PH):
                        ch.step(V.max(bs[0:p, h, 0:8], cand[0:p, h, :]))
                    for h in range(PH):
                        ch.settle(lag=PH - 1)
                        ch.step(V.match_replace(cand2[0:p, h, :], bs[0:p, h, 0:8], cand[0:p, h, :], NEG))
                    for h in range(PH):
                        ch.settle(lag=PH - 1)
                        ch.step(V.max(bs[0:p, h, 8:16], cand2[0:p, h, :]))
                    for h in range(PH):
                        ch.step(V.max_index(bp[0:p, h, 0:8], bs[0:p, h, 0:8], cand[0:p, h, :]))
                    for h in range(PH):
                        ch.settle(lag=2 * PH - 1)
                        ch.step(V.max_index(bp[0:p, h, 8:16], bs[0:p, h, 8:16], cand2[0:p, h, :]))
                    ch.settle()
                    ch(V.tensor_tensor(be[0:p], bs[0:p], over(bs[0:p, :, 0], 2, TOPK), ALU.subtract))
                    mark["exp", t] = ch.n
                    bpv = bp[0:p].rearrange("q h k -> q (h k)")
                    ch.step(V.tensor_scalar(part[0:p, 0, :], bpv, 4, None, ALU.logical_shift_right))
                    ch(V.tensor_scalar(part[0:p, 1, :], bpv, 15, None, ALU.bitwise_and))
                    ch(V.tensor_copy(partf[0:p], part[0:p]))
                    for half in range(2):
                        ch(V.tensor_tensor(hot[0:p], over(partf[0:p, half, :], 2, TOPK), over(iota[0:p, :], 1, SLOTS),
                                           ALU.is_equal))
                        for h in range(PH):
                            hs = hot[0:p, h * TOPK:(h + 1) * TOPK, :]
                            ch.step(V.tensor_tensor(hs, hs, over(tif[0:p, 2 * h + half, :], 1, TOPK), ALU.mult))
                        ch.settle()
                        ch(V.tensor_reduce(rowf[0:p, half, :], hot[0:p], AX_X, ALU.add))
                    ch(V.tensor_scalar(rowf[0:p, 0, :], rowf[0:p, 0, :], float(NKEY), float(layer * NKEY * NKEY),
                                       ALU.mult, ALU.add))
                    ch.step(V.tensor_tensor(R["idx"][:, t, :] if t < 2 else idx3[:], rowf[0:p, 0, :], rowf[0:p, 1, :],
                                            ALU.add))
                    dve.wait_ge(exp_ready, t + 1)
                    gt = gate[:, t, :] if t < 2 else gate3[:]
                    ch(V.tensor_reduce(total[0:p], be[0:p], AX_X, ALU.add))
                    ch(V.reciprocal(total[0:p], total[0:p]))
                    ch(V.tensor_tensor(gt.rearrange("q (h k) -> q h k", h=PH), be[0:p], over(total[0:p, :], 2, TOPK),
                                       ALU.mult))
                mark["tables"] = ch.n

            @block.scalar
            def _(act):
                for t, (o, p) in enumerate(TILES):
                    act.wait_ge(dve_steps, mark["exp", t])
                    nc.scalar.activation(be[0:p], be[0:p], ACT.Exp).then_inc(exp_ready, 1)

            @block.tensor
            def _(pe):
                for t, (o, p) in enumerate(TILES):
                    if t:
                        pe.wait_ge(dve_steps, mark["scores", t - 1])
                    for n in range(NH2):
                        r = slice(n % 2 * 64, n % 2 * 64 + 64)
                        last = nc.tensor.matmul(ps[0:p, col(n):col(n) + NKEY], qT[r, n // 2, o:o + p],
                                                keysT[r, n // 2, :], start=True, stop=True)
                    last.then_inc(score_ready, 1)

            @block.sync
            def _(sp):
                sp.dma_start(iota[:], T["c_iota"]).then_inc(loaded, 16)
                for s in range(4):
                    sp.dma_start(R["h_s"][32 * s:32 * s + 32, :], K["h"][0:NS, 2, :]).then_inc(moved, 16)
                sp.wait_ge(dve_steps, mark["tables"])
                for s in range(4):
                    sp.dma_start(R["idx_s"][32 * s:32 * s + 32, :], idx3[:, 32 * s:32 * s + 32]).then_inc(moved, 16)
                    sp.dma_start(R["gate_s"][32 * s:32 * s + 32, :], gate3[:, 32 * s:32 * s + 32]).then_inc(moved, 16)
                sp.wait_ge(moved, 12 * 16)


RING = 8
HALF = RING
def experts_phase(nc, name, K, T, R):
    groups = (("p0", SLOTS), ("p1", SLOTS), ("s", SLOTS // 4))
    x, h = K["x"], K["h"]
    u_tab, v_tab = (T[n].rearrange("l e d -> (l e) d") for n in ("peer_u", "peer_v"))
    idx = lambda gi: R["idx"][:, gi, :] if gi < 2 else R["idx_s"][:]
    gate = lambda gi: R["gate"][:, gi, :] if gi < 2 else R["gate_s"][:]
    hid = lambda gi: h[:, gi, :] if gi < 2 else R["h_s"][:]
    steps = [n for _, n in groups] * 2
    before = [sum(steps[:i]) // HALF for i in range(7)]
    with ExitStack() as ctx:
        P = Phase(nc, ctx, name)
        ring = P.sb("ring", [128, RING, D])
        cur = P.sb("cur_idx", [128, 2, HALF], U32)
        dots, act_w = P.sb("dots", [128, 3, SLOTS]), P.sb("weights", [128, 3, SLOTS])
        dot_blk = P.sb("dot_block", [128, 2, HALF])
        w_blk = P.sb("weight_block", [128, 2, HALF])
        NDIAG = 4
        diag = P.sb("diag", [128, HALF, 128])
        zero = P.sb("zero", [128, 128])
        four = P.sb("four", [128, 32])
        acc = [P.ps(f"acc{gi}", [128, D]) for gi in range(3)]
        landed = [P.sem(f"landed{r}") for r in range(RING)]
        dotted = [P.sem(f"dotted{r}") for r in range(RING)]
        added = [P.sem(f"added{r}") for r in range(RING)]
        idx_copied, four_in, dve_steps, gelu_ready, gated, act_steps, diag_ready, acc_done, blk_ready = (
            P.sem(s) for s in ("idx_copied", "four_in", "dve_steps", "gelu_ready", "gated", "act_steps",
                               "diag_ready", "acc_done", "blk_ready"))
        zero_ready, go = P.sem("zero_ready"), P.sem("go")
        with nc.Block() as block:
            @block.sync
            def _(sp):
                sp.dma_start(four[:], T["c_four"]).then_inc(four_in, 16)

            @block.gpsimd
            def _(pool):
                for n in range(6):
                    tab, gi, u_pass = (u_tab, n, True) if n < 3 else (v_tab, n - 3, False)
                    with pool.Fori(0, steps[n] // (2 * HALF)) as i:
                        for hf in range(2):
                            nc.gpsimd.tensor_copy(cur[:, hf, :], idx(gi)[:, bass.ds(i * (2 * HALF) + hf * HALF, HALF)]
                                                  ).then_inc(idx_copied, 1)
                            for r in range(RING):
                                k = before[n] + hf
                                if u_pass:
                                    pool.wait_ge(dotted[r], i * 2 + (k + 1))
                                elif n == 3 and hf == 0:
                                    pool.wait_ge(dotted[r], before[3] + 1)
                                    pool.wait_ge(added[r], i * 2 + 1)
                                else:
                                    pool.wait_ge(added[r], i * 2 + (k - before[3] + 1))
                                if r == 0:
                                    pool.wait_ge(idx_copied, i * 2 + k + 1)
                                pool.sem_inc(go, 1)
                                pool.indirect_dma_start(ring[:, r, :], None, tab,
                                                        bass.IndirectOffsetOnAxis(ap=cur[:, hf, r:r + 1], axis=0)
                                                        ).then_inc(landed[r], 16)

            @block.vector
            def _(dve):
                ch = Chain(dve, dve_steps)
                V = nc.vector
                V.memset(zero[:], 0.0).then_inc(zero_ready, 1)
                for r in range(RING):
                    dve.sem_inc(dotted[r], 1)
                for gi in range(3):
                    with dve.Fori(0, steps[gi] // (2 * HALF)) as i:
                        for hf in range(2):
                            for r in range(RING):
                                dve.wait_ge(landed[r], (i * 2 + (before[gi] + hf + 1)) * 16)
                                V.tensor_tensor_reduce(out=ring[:, r, :], in0=ring[:, r, :], in1=hid(gi), scale=1.0,
                                                       scalar=0.0, op0=ALU.mult, op1=ALU.add,
                                                       accum_out=dot_blk[:, hf, r:r + 1]).then_inc(dotted[r], 1)
                            dve.wait_ge(dotted[RING - 1], i * 2 + (before[gi] + hf + 2))
                            V.tensor_copy(dots[:, gi, bass.ds(i * (2 * HALF) + hf * HALF, HALF)],
                                          dot_blk[:, hf, :]).then_inc(blk_ready, 1)
                for gi in range(3):
                    n = steps[gi]
                    dve.wait_ge(gelu_ready, gi + 1)
                    V.tensor_tensor(act_w[:, gi, 0:n], act_w[:, gi, 0:n], gate(gi), ALU.mult).then_inc(gated, 1)
                dve.wait_ge(acc_done, 3)
                for gi, (o, p) in enumerate(TILES):
                    ch.step(V.tensor_tensor(x[0:p, gi, :], x[0:p, gi, :], acc[gi][0:p, :], ALU.add))
                ch.settle()

            @block.scalar
            def _(act):
                for gi in range(3):
                    n = steps[gi]
                    act.wait_ge(blk_ready, before[gi + 1])
                    nc.scalar.activation(act_w[:, gi, 0:n], dots[:, gi, 0:n], ACT.Gelu).then_inc(gelu_ready, 1)
                act.wait_ge(four_in, 16)
                for gi in range(3):
                    idn = K["ident"] if gi < 2 else four
                    w = 128 if gi < 2 else 32
                    act.wait_ge(gated, gi + 1)
                    with act.Fori(0, steps[gi] // (2 * HALF)) as i:
                        for hf in range(2):
                            k = before[gi] + hf
                            nc.scalar.activation(w_blk[:, hf, :],
                                                 act_w[:, gi, bass.ds(i * (2 * HALF) + hf * HALF, HALF)],
                                                 ACT.Copy).then_inc(act_steps, 1)
                            act.wait_ge(act_steps, i * 2 + k + 1)
                            for r in range(RING):
                                act.wait_ge(added[r], i * 2 + (k + 1))
                                nc.scalar.activation(diag[:, r, 0:w], idn[:, 0:w], ACT.Copy,
                                                     scale=w_blk[:, hf, r:r + 1]).then_inc(diag_ready, 1)

            @block.tensor
            def _(pe):
                pe.wait_ge(zero_ready, 1)
                for r in range(RING):
                    pe.sem_inc(added[r], 1)
                for gi in range(3):
                    w = 128 if gi < 2 else 32
                    for c in range(2):
                        nc.tensor.matmul(acc[gi][0:w, c * 512:(c + 1) * 512], zero[:, 0:w],
                                         h[:, 0, c * 512:(c + 1) * 512], start=True, stop=False)
                    with pe.Fori(0, steps[gi] // (2 * HALF)) as i:
                        for hf in range(2):
                            k = before[gi] + hf
                            for r in range(RING):
                                pe.wait_ge(landed[r], (i * 2 + (before[3] + k + 1)) * 16)
                                pe.wait_ge(diag_ready, i * (2 * RING) + (k * RING + r + 1))
                                for c in range(2):
                                    last = nc.tensor.matmul(acc[gi][0:w, c * 512:(c + 1) * 512], diag[:, r, 0:w],
                                                            ring[:, r, c * 512:(c + 1) * 512], start=False, stop=False)
                                last.then_inc(added[r], 1)
                    for c in range(2):
                        last = nc.tensor.matmul(acc[gi][0:w, c * 512:(c + 1) * 512], zero[:, 0:w],
                                                h[:, 0, c * 512:(c + 1) * 512], start=False, stop=True)
                    last.then_inc(acc_done, 1)


def ple_phase(nc, name, K, T, layer):
    x, hT = K["x"], K["hT"]
    with ExitStack() as ctx:
        P = Phase(nc, ctx, name)
        pr, pT = P.sb("p_rows", [128, 3, PLE]), P.sb("pT", [128, 2, NTOK])
        wg, wp = P.sb("w_gate", [128, 2, KC, 512]), P.sb("w_proj", [128, 2, D])
        sg = P.sb("gate", [128, 2, 512])
        pt = P.ps("pt", [128, 512])
        acc = [P.ps(f"acc{b}", [128, 2, 512]) for b in range(2)]
        p_in, wg_in, wp_in = P.sem("p_in"), [P.sem(f"wg_in{c}") for c in range(2)], P.sem("wp_in")
        pt_ready, pT_ready, acc_ready, gate_ready, acc_free, dve_steps = (
            P.sem(s) for s in ("pt_ready", "pT_ready", "acc_ready", "gate_ready", "acc_free", "dve_steps"))
        jobs = [(c, t) for c in range(2) for t in range(3)]
        with nc.Block() as block:
            @block.sync
            def _(sp):
                sp.dma_start(pr[:, 0:2, :], T["p_prompt"][layer, 0].rearrange("(t p) d -> p t d", p=128)).then_inc(p_in, 16)
                sp.dma_start(pr[0:NS, 2, :], T["p_sample"][layer].rearrange("b t d -> (b t) d")).then_inc(p_in, 16)
                sp.dma_start(wp[:], T["ple_proj"][layer].rearrange("(k p) n -> p k n", p=128)).then_inc(wp_in, 16)
                for c in range(2):
                    sp.dma_start(wg[:, c, :, :], T["ple_gate"][layer].rearrange("(k p) n -> p k n", p=128)
                                 [:, :, c * 512:(c + 1) * 512]).then_inc(wg_in[c], 16)

            @block.tensor
            def _(pe):
                pe.wait_ge(p_in, 32)
                for t, (o, p) in enumerate(TILES):
                    if t:
                        pe.wait_ge(pT_ready, t)
                    for k in range(2):
                        last = nc.tensor.transpose(pt[:, k * 128:k * 128 + p], pr[0:p, t, k * 128:(k + 1) * 128],
                                                   K["ident"][0:p, 0:p])
                    last.then_inc(pt_ready, 1)
                pe.wait_ge(pT_ready, 3)
                pe.wait_ge(wp_in, 16)
                for n, (c, t) in enumerate(jobs):
                    o, p = TILES[t]
                    if t == 0:
                        pe.wait_ge(wg_in[c], 16)
                    if n >= 2:
                        pe.wait_ge(acc_free, n - 1)
                    for k in range(KC):
                        nc.tensor.matmul(acc[n % 2][0:p, 0, :], hT[:, k, o:o + p], wg[:, c, k, :],
                                         start=(k == 0), stop=(k == KC - 1))
                    for k in range(2):
                        last = nc.tensor.matmul(acc[n % 2][0:p, 1, :], pT[:, k, o:o + p],
                                                wp[:, k, c * 512:(c + 1) * 512], start=(k == 0), stop=(k == 1))
                    last.then_inc(acc_ready, 1)

            @block.scalar
            def _(act):
                for t, (o, p) in enumerate(TILES):
                    act.wait_ge(pt_ready, t + 1)
                    nc.scalar.activation(pT[:, :, o:o + p], pt[:, 0:256].rearrange("q (k c) -> q k c", k=2)[:, :, 0:p],
                                         ACT.Copy).then_inc(pT_ready, 1)
                for n, (c, t) in enumerate(jobs):
                    p = TILES[t][1]
                    act.wait_ge(acc_ready, n + 1)
                    if n >= 2:
                        act.wait_ge(acc_free, n - 1)
                    nc.scalar.activation(sg[0:p, n % 2, :], acc[n % 2][0:p, 0, :], ACT.Sigmoid).then_inc(gate_ready, 1)

            @block.vector
            def _(dve):
                ch = Chain(dve, dve_steps)
                for n, (c, t) in enumerate(jobs):
                    p = TILES[t][1]
                    dve.wait_ge(gate_ready, n + 1)
                    ch(nc.vector.tensor_tensor(sg[0:p, n % 2, :], sg[0:p, n % 2, :], acc[n % 2][0:p, 1, :], ALU.mult))
                    xs = x[0:p, t, c * 512:(c + 1) * 512]
                    nc.vector.tensor_tensor(xs, xs, sg[0:p, n % 2, :], ALU.add).then_inc(acc_free, 1)


def tail(nc, K, T, layer, phases=99, stop=99):
    h, hT = K["h"], K["hT"]
    norm_phase(nc, f"nf{layer}", K, T["norm_ffn"][layer:layer + 1, :], h, hT)
    with ExitStack() as ctx:
        P = Phase(nc, ctx, f"peer{layer}")
        R = {"idx": P.sb("idx", [128, 2, SLOTS], U32), "idx_s": P.sb("idx_s", [128, SLOTS // 4], U32),
             "gate": P.sb("gate", [128, 2, SLOTS]), "gate_s": P.sb("gate_s", [128, SLOTS // 4]),
             "h_s": P.sb("h_s", [128, D])}
        with ExitStack() as c2:
            P2 = Phase(nc, c2, f"search{layer}")
            qT, keysT = P2.sb("qT", [128, PH, NTOK]), P2.sb("keysT", [128, PH, NKEY])
            keys_phase(nc, f"keys{layer}", K, T["peer_keys"][layer], keysT)
            columns_phase(nc, f"wq{layer}", K, hT, T["peer_wq"][layer], D, qT)
            topk_phase(nc, f"topk{layer}", K, T, qT, keysT, layer, R)
        experts_phase(nc, f"exp{layer}", K, T, R)
    if phases == stop: return
    norm_phase(nc, f"np{layer}", K, T["norm_ple"][layer:layer + 1, :], h, hT)
    ple_phase(nc, f"ple{layer}", K, T, layer)


def qkv_phase(nc, name, K, T, qP, kP, vP, qS, kS, vS):
    hT = K["hT"]
    w = T["w_in_c"][0].rearrange("(k p) n -> p k n", p=128)
    chunks, WR = 18, 2
    jobs = [(c, t) for c in range(chunks) for t in range(3)]
    turned = [n for n, (c, t) in enumerate(jobs) if c < 12]

    def k_stores(slot, n):
        kept = lambda c, t: t == 2 or TILES[t][0] >= SEQ - min(PATTERNS[c % 6 // 2][0], SEQ)
        return sum(1 for m in turned[:n] if m % 4 == slot and jobs[m][0] >= 6 and kept(*jobs[m]))

    with ExitStack() as ctx:
        P = Phase(nc, ctx, name)
        wt = P.sb("w", [128, WR, KC, 512])
        rope = P.sb("rope", [128, 3, 2, ROT])
        rows = P.sb("rows", [128, 4, 4, HD])
        r1, r2 = P.sb("r1", [128, 2, 4, ROT]), P.sb("r2", [128, 2, 4, ROT])
        acc = [P.ps(f"acc{b}", [128, 512]) for b in range(4)]
        pt = [P.ps(f"pt{b}", [128, 512]) for b in range(4)]
        w_in = [P.sem(f"w_in{r}") for r in range(WR)]
        rope_in, product_ready, copied, dve_steps, roped, turned_ready, turned_out, stored = (
            P.sem(s) for s in ("rope_in", "product_ready", "copied", "dve_steps", "roped", "turned_ready",
                               "turned_out", "stored"))
        slot_stored = [P.sem(f"slot_stored{i}") for i in range(4)]
        with nc.Block() as block:
            @block.sync
            def _(sp):
                sp.dma_start(rope[:], T["c_rope"].rearrange("p (t a r) -> p t a r", t=3, a=2)).then_inc(rope_in, 16)
                for c in range(chunks):
                    if c >= WR:
                        sp.wait_ge(product_ready, 3 * (c - WR + 1))
                    sp.dma_start(wt[:, c % WR, :, :], w[:, :, c * 512:(c + 1) * 512]).then_inc(w_in[c % WR], 16)

            @block.gpsimd
            def _(pool):
                n_out = 0
                for n, (c, t) in enumerate(jobs):
                    kind, gi, half = c // 6, c % 6 // 2, c % 2
                    if kind == 0:
                        continue
                    o, p = TILES[t]
                    if kind == 1:
                        pool.wait_ge(roped, turned.index(n) + 1)
                        src = rows[0:p, turned.index(n) % 4, :, :]
                    else:
                        pool.wait_ge(copied, n + 1)
                        src = (vP[:, t] if t < 2 else vS[:])[:, gi, half * 4:half * 4 + 4, :]
                    hs = slice(half * 4, half * 4 + 4)
                    keep = min(PATTERNS[gi][0], SEQ)
                    done = slot_stored[turned.index(n) % 4] if kind == 1 else stored
                    if t < 2:
                        if o >= SEQ - keep:
                            pool.dma_start(T[f"out_kv{gi}_p"][0, 0, o - SEQ + keep:o - SEQ + keep + 128, kind - 1, hs, :],
                                           src).then_inc(done, 16)
                            n_out += kind == 2
                    else:
                        full = T[f"out_kv{gi}_s"].shape[2]
                        pool.dma_start(T[f"out_kv{gi}_s"][0, :, full - DEC_T:full, kind - 1, hs, :], src).then_inc(
                            done, 16)
                        n_out += kind == 2
                pool.wait_ge(stored, 16 * n_out)
                for i in range(4):
                    pool.wait_ge(slot_stored[i], 16 * k_stores(i, len(turned)))

            @block.tensor
            def _(pe):
                def turn(m):
                    n = turned[m]
                    o, p = TILES[jobs[n][1]]
                    pe.wait_ge(roped, m + 1)
                    if m >= 4:
                        pe.wait_ge(turned_out, m - 3)
                    for h in range(4):
                        last = nc.tensor.transpose(pt[m % 4][:, h * 128:h * 128 + p], rows[0:p, m % 4, h, :],
                                                   K["ident"][0:p, 0:p])
                    last.then_inc(turned_ready, 1)

                for n, (c, t) in enumerate(jobs):
                    o, p = TILES[t]
                    if t == 0:
                        pe.wait_ge(w_in[c % WR], 16 * (c // WR + 1))
                    if n >= 4:
                        pe.wait_ge(copied, n - 3)
                        if n - 4 < len(turned):
                            pe.wait_ge(roped, n - 3)
                    for k in range(KC):
                        last = nc.tensor.matmul(acc[n % 4][0:p, :], hT[:, k, o:o + p], wt[:, c % WR, k, :],
                                                start=(k == 0), stop=(k == KC - 1))
                    last.then_inc(product_ready, 1)
                    if 2 <= n < len(turned) + 2:
                        turn(n - 2)

            @block.scalar
            def _(act):
                for n, (c, t) in enumerate(jobs):
                    p = TILES[t][1]
                    act.wait_ge(product_ready, n + 1)
                    gi, half = c % 6 // 2, c % 2
                    if c < 12:
                        if n >= 4:
                            act.wait_ge(turned_ready, n - 3)
                            if k_stores(n % 4, n):
                                act.wait_ge(slot_stored[n % 4], 16 * k_stores(n % 4, n))
                        dst = rows[0:p, n % 4, :, :]
                    else:
                        dst = (vP[:, t] if t < 2 else vS[:])[:, gi, half * 4:half * 4 + 4, :]
                    nc.scalar.activation(dst, acc[n % 4][0:p, :].rearrange("q (h e) -> q h e", h=4), ACT.Copy
                                         ).then_inc(copied, 1)
                    if 3 <= n < len(turned) + 3:
                        m = n - 3
                        cm, tm = jobs[turned[m]]
                        om, pm = TILES[tm]
                        dstT = (qP if cm < 6 else kP) if tm < 2 else (qS if cm < 6 else kS)
                        om = om % SEQ
                        h0 = cm % 6 * 4
                        act.wait_ge(turned_ready, m + 1)
                        nc.scalar.activation(dstT[:, h0:h0 + 4, om:om + pm],
                                             pt[m % 4][:].rearrange("q (h c) -> q h c", h=4)[:, :, 0:pm], ACT.Copy
                                             ).then_inc(turned_out, 1)

            @block.vector
            def _(dve):
                ch = Chain(dve, dve_steps)
                V = nc.vector
                dve.wait_ge(rope_in, 16)
                HR = ROT // 2
                for m, n in enumerate(turned):
                    c, t = jobs[n]
                    p = TILES[t][1]
                    a4 = acc[n % 4][0:p, :].rearrange("q (h e) -> q h e", h=4)
                    dve.wait_ge(copied, n + 1)
                    a, b = r1[0:p, m % 2], r2[0:p, m % 2]
                    ch.step(V.tensor_tensor(a, a4[:, :, 0:ROT], over(rope[0:p, t, 0, :], 1, 4), ALU.mult))
                    ch.step(V.tensor_tensor(b[:, :, 0:HR], a4[:, :, HR:ROT], over(rope[0:p, t, 1, 0:HR], 1, 4), ALU.mult))
                    ch(V.tensor_tensor(b[:, :, HR:], a4[:, :, 0:HR], over(rope[0:p, t, 1, HR:], 1, 4), ALU.mult))
                    V.tensor_tensor(rows[0:p, m % 4, :, 0:ROT], a, b, ALU.add).then_inc(roped, 1)


def prompt_attention_phase(nc, name, K, T, qT, kT, v, mixT):
    units = [(h, it) for it in range(2) for h in range(CH)]
    with ExitStack() as ctx:
        P = Phase(nc, ctx, name)
        band = P.sb("band", [128, 2, NG, SEQ])
        s, pT = P.sb("s", [128, 2, NG, SEQ]), P.sb("pT", [128, 2, NG * 2, 128])
        st = P.sb("stats", [128, 2, 4])
        ps = [P.ps(f"scores{b}", [128, 1024]) for b in range(2)]
        pp = P.ps("turned", [128, 1024])
        po = [P.ps(f"out{b}", [128, 512]) for b in range(2)]
        band_in, score_ready, dve_steps, max_ready, exp_ready, norm_ready, turned, copied, out_ready, out_done = (
            P.sem(x) for x in ("band_in", "score_ready", "dve_steps", "max_ready", "exp_ready", "norm_ready",
                               "turned", "copied", "out_ready", "out_done"))
        with nc.Block() as block:
            @block.sync
            def _(sp):
                sp.dma_start(band[:], T["c_band"].rearrange("p (t g n) -> p t g n", t=2, g=NG)).then_inc(band_in, 16)

            @block.tensor
            def _(pe):
                def scores(n):
                    h, it = units[n]
                    if n >= 2:
                        pe.wait_ge(max_ready, n - 1)
                    for gi in range(NG):
                        last = nc.tensor.matmul(ps[n % 2][:, gi * SEQ:gi * SEQ + 128 * (it + 1)],
                                                qT[:, gi * CH + h, it * 128:(it + 1) * 128],
                                                kT[:, gi * CH + h, 0:128 * (it + 1)], start=True, stop=True)
                    last.then_inc(score_ready, 1)

                scores(0)
                for n, (h, it) in enumerate(units):
                    if n + 1 < len(units):
                        scores(n + 1)
                    pe.wait_ge(norm_ready, n + 1)
                    if n:
                        pe.wait_ge(copied, n)
                    for gi in range(NG):
                        for jt in range(it + 1):
                            last = nc.tensor.transpose(pp[:, (gi * 2 + jt) * 128:(gi * 2 + jt + 1) * 128],
                                                       s[:, n % 2, gi, jt * 128:(jt + 1) * 128], K["ident"][:])
                    last.then_inc(turned, 1)
                    pe.wait_ge(copied, n + 1)
                    if n >= 2:
                        pe.wait_ge(out_done, n - 1)
                    parts = [(gi, jt) for gi in range(NG) for jt in range(it + 1)]
                    for m, (gi, jt) in enumerate(parts):
                        last = nc.tensor.matmul(po[n % 2][:, 0:128], v[:, jt, gi, h, :], pT[:, n % 2, gi * 2 + jt, :],
                                                start=(m == 0), stop=(m == len(parts) - 1))
                    last.then_inc(out_ready, 1)

            @block.vector
            def _(dve):
                ch = Chain(dve, dve_steps)
                V = nc.vector
                dve.wait_ge(band_in, 16)
                for n, (h, it) in enumerate(units):
                    w = 128 * (it + 1)
                    sv = s[:, n % 2, :, 0:w]
                    dve.wait_ge(score_ready, n + 1)
                    if n >= 2:
                        dve.wait_ge(turned, n - 1)
                    ch(V.scalar_tensor_tensor(out=sv, in0=ps[n % 2][:, 0:NG * SEQ].rearrange("p (g n) -> p g n", g=NG)[:, :, 0:w],
                                              scalar=ATT_SCALE, in1=band[:, it, :, 0:w], op0=ALU.mult, op1=ALU.add))
                    ch(V.tensor_reduce(st[:, n % 2, 0:1], sv, mybir.AxisListType.XY, ALU.max))
                    V.tensor_scalar(st[:, n % 2, 1:2], st[:, n % 2, 0:1], -1.0, None, ALU.mult).then_inc(max_ready, 1)
                    dve.wait_ge(exp_ready, n + 1)
                    ch(V.reciprocal(st[:, n % 2, 3:4], st[:, n % 2, 2:3]))
                    V.tensor_scalar(sv, sv, st[:, n % 2, 3:4], None, ALU.mult).then_inc(norm_ready, 1)

            @block.scalar
            def _(act):
                for n, (h, it) in enumerate(units):
                    sv = s[:, n % 2, :, 0:128 * (it + 1)]
                    act.wait_ge(max_ready, n + 1)
                    nc.scalar.activation(sv, sv, ACT.Exp, bias=st[:, n % 2, 1:2], accum_out=st[:, n % 2, 2:3]
                                         ).then_inc(exp_ready, 1)
                    act.wait_ge(turned, n + 1)
                    src = pp[:, 0:NG * 256].rearrange("p (g j n) -> p g j n", g=NG, j=2)[:, :, 0:it + 1, :]
                    if n >= 2:
                        act.wait_ge(out_ready, n - 1)
                    nc.scalar.activation(pT[:, n % 2].rearrange("p (g j) n -> p g j n", j=2)[:, :, 0:it + 1, :], src,
                                         ACT.Copy).then_inc(copied, 1)
                    act.wait_ge(out_ready, n + 1)
                    nc.scalar.activation(mixT[:, h, it * 128:(it + 1) * 128], po[n % 2][:, 0:128], ACT.Copy
                                         ).then_inc(out_done, 1)


def sample_attention_phase(nc, name, K, T, qS, kS, vS, mixT):
    KT, NB, NEWK = 7, 4, 3
    WID = KT * 128 + NEWK * NS
    caches = [T["cache_kv_w128"][0], T["cache_kv_w512"][0], T["cache_kv_w2048"][0]]

    def key_tiles(dst, b, kv):
        c0, c1, c2 = (c[b, :, kv, :, :].rearrange("r h e -> r (h e)") for c in caches)
        c1 = c1.rearrange("(r t) c -> r t c", t=4)
        c2 = c2.rearrange("(r t) c -> r t c", t=16)
        out = [(dst[:, 0, :], c0), (dst[:, 1:5, :], c1)]
        for half in range(2):
            out.append((dst[half * 64:half * 64 + 64, 5:7, :],
                        c2[:, half:half + 3:2, :]))
        return out

    with ExitStack() as ctx:
        P = Phase(nc, ctx, name)
        kc, vc = P.sb("k_rows", [128, KT, D]), P.sb("v_rows", [128, KT, D])
        kTc = P.sb("k_cols", [128, 2, D])
        mask = P.sb("mask", [128, 2, WID])
        sT, s = P.sb("sT", [128, KT + NEWK, 128]), P.sb("s", [128, WID])
        pT, st = P.sb("pT", [128, KT + NEWK, 128]), P.sb("stats", [128, 4])
        p_kt = [P.ps(f"keys{b}", [128, 1024]) for b in range(2)]
        p_sc = P.ps("scores", [128, 512])
        p_w = P.ps("wide", [128, 1024])
        p_o = P.ps("out", [128, 512])
        mask_in, k_in, v_in, keys_ready, keys_copied, col_ready, col_copied = (
            P.sem(x) for x in ("mask_in", "k_in", "v_in", "keys_ready", "keys_copied", "col_ready", "col_copied"))
        new_ready, new_copied, row_ready, dve_steps, max_ready, exp_ready, norm_ready = (
            P.sem(x) for x in ("new_ready", "new_copied", "row_ready", "dve_steps", "max_ready", "exp_ready",
                               "norm_ready"))
        back_ready, back_copied, out_ready, out_done = (
            P.sem(x) for x in ("back_ready", "back_copied", "out_ready", "out_done"))
        span = lambda k: slice(k * 128, k * 128 + 128) if k < KT else slice(896 + (k - KT) * NS, 896 + (k - KT + 1) * NS)
        with nc.Block() as block:
            @block.sync
            def _(sp):
                sp.dma_start(mask[:], T["c_samp"].rearrange("p (b n) -> p b n", b=2)).then_inc(mask_in, 16)
                for b in range(DEC_B):
                    if b:
                        sp.wait_ge(keys_ready, KT * b)
                    for to, frm in key_tiles(kc, b, 0):
                        sp.dma_start(to, frm).then_inc(k_in, 16)

            @block.gpsimd
            def _(pool):
                for b in range(DEC_B):
                    if b:
                        pool.wait_ge(v_in, 64 * b)
                        pool.wait_ge(out_ready, b)
                    for to, frm in key_tiles(vc, b, 1):
                        pool.dma_start(to, frm).then_inc(v_in, 16)

            @block.tensor
            def _(pe):
                mm = nc.tensor.matmul
                group = lambda k: 0 if k == 0 else (1 if k < 5 else 2)
                tiles = [(b, k) for b in range(DEC_B) for k in range(KT)]

                def turn(n):
                    b, k = tiles[n]
                    if k == 0:
                        pe.wait_ge(k_in, 64 * (b + 1))
                    if n >= 2:
                        pe.wait_ge(keys_copied, n - 1)
                    for h in range(CH):
                        last = nc.tensor.transpose(p_kt[n % 2][:, h * 128:(h + 1) * 128],
                                                   kc[:, k, h * 128:(h + 1) * 128], K["ident"][:])
                    last.then_inc(keys_ready, 1)

                turn(0)
                for bb in range(2):
                    for b in range(bb * NB, bb * NB + NB):
                        for k in range(KT):
                            n = b * KT + k
                            if n + 1 < len(tiles):
                                turn(n + 1)
                            pe.wait_ge(keys_copied, n + 1)
                            if n:
                                pe.wait_ge(col_copied, n)
                            if n == NB * KT:
                                pe.wait_ge(new_copied, 1)
                            for h in range(CH):
                                q = qS[:, group(k) * CH + h, 4 * b:4 * b + 4]
                                last = mm(p_sc[:, h * 4:h * 4 + 4], kTc[:, n % 2, h * 128:(h + 1) * 128], q,
                                          start=True, stop=True)
                            last.then_inc(col_ready, 1)
                    pe.wait_ge(col_copied, (bb + 1) * NB * KT)
                    for gi in range(NG):
                        for h in range(CH):
                            q = qS[:, gi * CH + h, 16 * bb:16 * bb + 16].rearrange("e (b t) -> e b t", t=4)
                            dst = p_sc[0:NS, gi * 128:(gi + 1) * 128].rearrange("j (b h t) -> j b h t", b=4, h=CH)
                            last = mm(dst[:, :, h, :], kS[:, gi * CH + h, :], q, start=True, stop=True)
                    last.then_inc(new_ready, 1)
                    pe.wait_ge(new_copied, bb + 1)
                    if bb:
                        pe.wait_ge(back_copied, bb)
                    for k in range(KT + NEWK):
                        r = 128 if k < KT else NS
                        last = nc.tensor.transpose(p_w[:, span(k)], sT[0:r, k, :], K["ident"][0:r, 0:r])
                    last.then_inc(row_ready, 1)
                    pe.wait_ge(norm_ready, bb + 1)
                    for half in range(2):
                        ks = range(0, 8) if half == 0 else range(8, KT + NEWK)
                        if half:
                            pe.wait_ge(back_copied, 2 * bb + 1)
                        for k in ks:
                            r = 128 if k < KT else NS
                            last = nc.tensor.transpose(p_w[0:r, (k % 8) * 128:(k % 8) * 128 + 128], s[:, span(k)],
                                                       K["ident"][:])
                        last.then_inc(back_ready, 1)
                    pe.wait_ge(back_copied, 2 * bb + 2)
                    if bb:
                        pe.wait_ge(out_done, bb)
                    for b4 in range(NB):
                        b = bb * NB + b4
                        pe.wait_ge(v_in, 64 * (b + 1))
                        for h in range(CH):
                            c = b4 * 32 + h * 4
                            for k in range(KT + NEWK):
                                if k < KT:
                                    l, r = vc[:, k, h * 128:(h + 1) * 128], pT[:, k, c:c + 4]
                                else:
                                    l, r = vS[:, k - KT, h, :], pT[0:NS, k, c:c + 4]
                                last = mm(p_o[:, c:c + 4], l, r, start=(k == 0), stop=(k == KT + NEWK - 1))
                        last.then_inc(out_ready, 1)

            @block.vector
            def _(dve):
                ch = Chain(dve, dve_steps)
                V = nc.vector
                dve.wait_ge(mask_in, 16)
                for bb in range(2):
                    for b in range(bb * NB, bb * NB + NB):
                        for k in range(KT):
                            n = b * KT + k
                            dve.wait_ge(keys_ready, n + 1)
                            if n >= 2:
                                dve.wait_ge(col_ready, n - 1)
                            V.tensor_copy(kTc[:, n % 2, :], p_kt[n % 2][:]).then_inc(keys_copied, 1)
                    dve.wait_ge(row_ready, bb + 1)
                    ch(V.scalar_tensor_tensor(out=s[:], in0=p_w[:, 0:WID], scalar=ATT_SCALE, in1=mask[:, bb, :],
                                              op0=ALU.mult, op1=ALU.add))
                    ch(V.tensor_reduce(st[:, 0:1], s[:], AX_X, ALU.max))
                    V.tensor_scalar(st[:, 1:2], st[:, 0:1], -1.0, None, ALU.mult).then_inc(max_ready, 1)
                    dve.wait_ge(exp_ready, bb + 1)
                    ch(V.reciprocal(st[:, 3:4], st[:, 2:3]))
                    V.tensor_scalar(s[:], s[:], st[:, 3:4], None, ALU.mult).then_inc(norm_ready, 1)

            @block.scalar
            def _(act):
                A = nc.scalar.activation
                for bb in range(2):
                    if bb:
                        act.wait_ge(row_ready, bb)
                    for b in range(bb * NB, bb * NB + NB):
                        for k in range(KT):
                            act.wait_ge(col_ready, b * KT + k + 1)
                            A(sT[:, k, b % NB * 32:b % NB * 32 + 32], p_sc[:, 0:32], ACT.Copy).then_inc(col_copied, 1)
                    act.wait_ge(new_ready, bb + 1)
                    A(sT[0:NS, KT:, :], p_sc[0:NS, 0:NEWK * 128].rearrange("j (g n) -> j g n", g=NEWK), ACT.Copy
                      ).then_inc(new_copied, 1)
                    act.wait_ge(max_ready, bb + 1)
                    A(s[:], s[:], ACT.Exp, bias=st[:, 1:2], accum_out=st[:, 2:3]).then_inc(exp_ready, 1)
                    act.wait_ge(back_ready, 2 * bb + 1)
                    if bb:
                        act.wait_ge(out_ready, NB)
                    A(pT[:, 0:KT, :], p_w[:, 0:KT * 128].rearrange("p (k n) -> p k n", k=KT), ACT.Copy)
                    A(pT[0:NS, KT, :], p_w[0:NS, KT * 128:(KT + 1) * 128], ACT.Copy).then_inc(back_copied, 1)
                    act.wait_ge(back_ready, 2 * bb + 2)
                    A(pT[0:NS, KT + 1:, :], p_w[0:NS, 0:256].rearrange("p (k n) -> p k n", k=2), ACT.Copy
                      ).then_inc(back_copied, 1)
                    act.wait_ge(out_ready, NB * (bb + 1))
                    dst = mixT[:, :, SEQ + 16 * bb:SEQ + 16 * bb + 16].rearrange("e h (b t) -> e h b t", t=4)
                    src = p_o[:, 0:128].rearrange("e (b h t) -> e h b t", b=4, h=CH)
                    for h in range(CH):
                        last = A(dst[:, h], src[:, h], ACT.Copy)
                    last.then_inc(out_done, 1)


OUTS = [("y_p", (1, SEQ, D)), ("y_s", (DEC_B, DEC_T, D)), ("conv_a_p", (1, 1, 30, D_A)),
        ("conv_qkv_p", (1, 1, 3, QKV_W)), ("delta_p", (1, 1, GH, GD, GD)),
        ("kv0_p", (1, 1, 128, 2, CH, HD)), ("kv1_p", (1, 1, SEQ, 2, CH, HD)), ("kv2_p", (1, 1, SEQ, 2, CH, HD)),
        ("conv_a_s", (1, DEC_B, 30, D_A)), ("conv_qkv_s", (1, DEC_B, 3, QKV_W)),
        ("delta_s", (1, DEC_B, GH, GD, GD)), ("kv0_s", (1, DEC_B, 128, 2, CH, HD)),
        ("kv1_s", (1, DEC_B, 512, 2, CH, HD)), ("kv2_s", (1, DEC_B, PAST + DEC_T, 2, CH, HD))]


def build(nc, T, phases=99):
    with ExitStack() as ctx:
        P = Phase(nc, ctx, "all", clears=False)
        K = {"x": P.sb("x", [128, 3, D]), "ident": P.sb("ident", [128, 128]), "h": P.sb("h", [128, 3, D]),
             "hT": P.sb("hT", [128, KC, NTOK])}
        x, h, hT = K["x"], K["h"], K["hT"]
        mixT = P.sb("mixT", [128, KC, NTOK])
        x_in = P.sem("x_in")
        with nc.Block() as block:
            @block.sync
            def _(sp):
                sp.dma_start(K["ident"][:], T["c_ident"]).then_inc(x_in, 16)
                sp.dma_start(x[:, 0:2, :], T["x_prompt"][0].rearrange("(t p) d -> p t d", p=128)).then_inc(x_in, 16)
                sp.dma_start(x[0:NS, 2, :], T["x_sample"].rearrange("b t d -> (b t) d")).then_inc(x_in, 16)
                sp.wait_ge(x_in, 48)
        cache_out = P.sem("cache_out")
        with nc.Block() as block:
            @block.scalar
            def _(act):
                for gi, cache in enumerate(("cache_kv_w128", "cache_kv_w512", "cache_kv_w2048")):
                    src, dst = T[cache][0], T[f"out_kv{gi}_s"][0]
                    keep = dst.shape[1] - DEC_T
                    drop = src.shape[1] - keep
                    act.dma_start(dst[:, 0:keep].rearrange("b r k h e -> b (r k h e)"),
                                  src[:, drop:].rearrange("b r k h e -> b (r k h e)")).then_inc(cache_out, 16)
        norm_phase(nc, "n0", K, T["norm_mix"][0:1, :], h, hT)
        if phases == 1: return dump(nc, T, h)
        with ExitStack() as c2:
            P0 = Phase(nc, c2, "l0")
            zT, conv = P0.sb("zT", [128, 24, NTOK]), P0.sb("conv", [128, 12, NTOK])
            columns_phase(nc, "ab", K, hT, T["w_in_ab"][0], IN_AB - 8, zT)
            conv_phase(nc, "cv", K, T, zT, mixT, conv)
            delta_phase(nc, "gd", K, T, hT, zT, conv, mixT)
        add_rows_phase(nc, "oab", K, mixT, T["w_out_ab"][0])
        if phases == 2: return dump(nc, T, x)
        tail(nc, K, T, 0, phases, 3)
        if phases in (3, 4): return dump(nc, T, x)
        norm_phase(nc, "n1", K, T["norm_mix"][1:2, :], h, hT)
        with ExitStack() as c2:
            P1 = Phase(nc, c2, "l1")
            qS, kS = P1.sb("qS", [128, NG * CH, NS]), P1.sb("kS", [128, NG * CH, NS])
            vS = P1.sb("vS", [NS, NG, CH, HD])
            with ExitStack() as c3:
                P2 = Phase(nc, c3, "l1p")
                qP, kP = P2.sb("q", [128, NG * CH, SEQ]), P2.sb("k", [128, NG * CH, SEQ])
                vP = P2.sb("v", [128, 2, NG, CH, HD])
                qkv_phase(nc, "qkv", K, T, qP, kP, vP, qS, kS, vS)
                prompt_attention_phase(nc, "pa", K, T, qP, kP, vP, mixT)
            sample_attention_phase(nc, "sa", K, T, qS, kS, vS, mixT)
        add_rows_phase(nc, "oc", K, mixT, T["w_out_c"][0])
        if phases == 5: return dump(nc, T, x)
        tail(nc, K, T, 1, phases, 6)
        if phases == 6: return dump(nc, T, x)
        y = [T["out_y_p"][0, 0:128, :], T["out_y_p"][0, 128:256, :], T["out_y_s"].rearrange("b t d -> (b t) d")]
        norm_phase(nc, "nl", K, T["norm_final"].rearrange("(a n) -> a n", a=1), h, None, y)
        with nc.Block() as block:
            @block.sync
            def _(sp):
                sp.wait_ge(cache_out, 16 * 3)


def dump(nc, T, x):
    with nc.semaphore("dbg") as s, nc.Block() as block:
        @block.sync
        def _(sp):
            sp.dma_start(T["dbg"][:, 0:2, :], x[:, 0:2, :]).then_inc(s, 16)
            sp.dma_start(T["dbg"][0:NS, 2, :], x[0:NS, 2, :]).then_inc(s, 16)
            sp.wait_ge(s, 32)


def kernel(**inputs):
    import concourse.bacc as bacc
    from concourse.bass_utils import run_bass_kernel_spmd

    nc = bacc.Bacc("TRN2", target_bir_lowering=False, num_devices=1)
    arrays = {k: np.ascontiguousarray(v) for k, v in inputs.items()}
    arrays.update({f"c_{k}": v for k, v in shape_constants().items()})
    T = {k: nc.dram_tensor(f"in_{k}", a.shape, mybir.dt.from_np(a.dtype), kind="ExternalInput").ap()
         for k, a in arrays.items()}
    for name, shape in OUTS:
        T[f"out_{name}"] = nc.dram_tensor(f"out_{name}", shape, F32, kind="ExternalOutput").ap()
    build(nc, T)
    r = run_bass_kernel_spmd(nc, [{f"in_{k}": a for k, a in arrays.items()}], core_ids=[0]).results[0]
    return tuple(r[f"out_{name}"] for name, _ in OUTS)
```

```python
from contextlib import ExitStack

import numpy as np
import concourse.bass as bass
from concourse import mybir

F32 = mybir.dt.float32
U32 = mybir.dt.uint32
ALU = mybir.AluOpType
ACT = mybir.ActivationFunctionType
AX_X = mybir.AxisListType.X

D = 1024
KC = D // 128
SEQ, DEC_B, DEC_T = 256, 8, 4
PAST = 1024
NS = DEC_B * DEC_T
NTOK = SEQ + NS
TILES = ((0, 128), (128, 128), (256, NS))
DEPTH = 2
EPS = 1e-6
D_A = 512
CAW = 31
GH, GD = 4, 128
CQW = 4
QKV_W = 1536
IN_AB = 2 * D_A + QKV_W + GH * GD + 2 * GH
CHUNK = 64
PATTERNS = ((128, 1), (512, 4), (2048, 16))
NG, CH, HD = 3, 8, 128
ROT = HD // 4
THETA = 500000.0
NEG = -1.0e30
PH, NKEY, TOPK = 8, 128, 16
SLOTS = PH * TOPK
PLE = 256
ATT_SCALE = HD ** -0.5


class Chain:

    def __init__(self, eng, sem):
        self.eng, self.sem, self.n = eng, sem, 0

    def step(self, ins):
        self.n += 1
        ins.then_inc(self.sem, 1)

    def settle(self, lag=0):
        if self.n - lag > 0:
            self.eng.wait_ge(self.sem, self.n - lag)

    def __call__(self, ins):
        self.step(ins)
        self.settle()


class Phase:

    def __init__(self, nc, ctx, name, clears=True):
        self.nc, self.ctx, self.name, self.sems = nc, ctx, name, []
        if clears:
            ctx.callback(self.clear)

    def clear(self):
        if self.sems:
            self.nc.clear_and_free_semaphores(self.sems)
            self.nc.all_engine_barrier(sem_only=True)

    def sb(self, name, shape, dt=F32):
        return self.ctx.enter_context(self.nc.sbuf_tensor(f"{self.name}_{name}", shape, dt))

    def ps(self, name, shape):
        return self.ctx.enter_context(self.nc.psum_tensor(f"{self.name}_{name}", shape, F32))

    def sem(self, name):
        self.sems.append(self.nc.alloc_semaphore(f"{self.name}_{name}"))
        return self.sems[-1]


def broadcast_rows(dram_row, n, parts=128):
    return bass.AP(tensor=dram_row.tensor, offset=dram_row.offset, ap=[[0, parts], [1, n]])


def over(ap, axis, n):
    pat = [list(p) for p in ap.ap]
    pat.insert(axis, [0, n])
    return bass.AP(tensor=ap.tensor, offset=ap.offset, ap=pat)


def shape_constants():
    i = np.arange(128)
    c = {}
    c["ident"] = np.eye(128)
    tok = np.concatenate([np.arange(SEQ), PAST + np.tile(np.arange(DEC_T), DEC_B), np.zeros(96)])
    inv = 1.0 / (np.float32(THETA) ** (np.arange(0, ROT, 2, dtype=np.float32) / np.float32(ROT)))
    ang = (tok.astype(np.float32)[:, None] * inv.astype(np.float32)[None, :]).astype(np.float32)
    cos, sin = np.cos(ang.astype(np.float64)), np.sin(ang.astype(np.float64))
    cc = np.concatenate([cos, cos, -sin, sin], 1)
    c["rope"] = cc.reshape(3, 128, 64).transpose(1, 0, 2).reshape(128, 192)
    c["four"] = np.tile(np.eye(32), (4, 1))
    c["iota"] = np.tile(np.arange(16.0), (128, 1))
    g = []
    for size in (CHUNK, DEC_T):
        same = i[:, None] // size == i[None, :] // size
        g += [same & (i[:, None] <= i[None, :]), same, same & (i[:, None] > i[None, :])]
    for lev in range(6):
        s = 1 << lev
        g.append((i[:, None] // (2 * s) == i[None, :] // (2 * s))
                 & (i[:, None] % (2 * s) >= s) & (i[None, :] % (2 * s) < s))
    c["gdn"] = np.stack([m.astype(float) for m in g], 1).reshape(128, -1)
    c["owner"] = np.repeat((i[:32, None] // DEC_T == np.arange(DEC_B)[None]).astype(float), 1, 1)
    c["owner"] = np.tile(c["owner"], (4, 1))
    m = np.full((128, 2, NG, SEQ), NEG)
    for it in range(2):
        rel = (it * 128 + i)[:, None] - np.arange(SEQ)[None]
        for gi, (win, dil) in enumerate(PATTERNS):
            m[:, it, gi][(rel >= 0) & (rel % dil == 0) & (rel // dil <= win // dil)] = 0
    c["band"] = m.reshape(128, -1)
    s = np.full((128, 2, 7 * 128 + 3 * NS), NEG)
    for p in range(128):
        b4, t = p // 32, p % DEC_T
        for bb in range(2):
            b = bb * 4 + b4
            s[p, bb, t:128] = 0
            s[p, bb, 128 * (1 + t):128 * (2 + t)] = 0
            s[p, bb, 640 + 64 * t:640 + 64 * t + 64] = 0
            s[p, bb, 896 + b * DEC_T:896 + b * DEC_T + t + 1] = 0
            for gi in (1, 2):
                s[p, bb, 896 + gi * NS + b * DEC_T + t] = 0
    c["samp"] = s.reshape(128, -1)
    return {k: np.ascontiguousarray(v, dtype=np.float32) for k, v in c.items()}


def norm_phase(nc, name, K, gain, h, hT=None, out=None):
    x = K["x"]
    with ExitStack() as ctx:
        P = Phase(nc, ctx, name)
        gain_b, sq, st = P.sb("gain", [128, D]), P.sb("sq", [128, 3, D]), P.sb("st", [128, 3, 3])
        pt = [P.ps(f"pt{t}", [128, KC * 128]) for t in range(3)] if hT is not None else None
        gain_in, mean_ready, root_ready, rows_ready, cols_ready, stored, steps = (
            P.sem(s) for s in ("gain_in", "mean_ready", "root_ready", "rows_ready", "cols_ready", "stored",
                               "dve_steps"))
        hT_done = P.sem("hT_done")
        with nc.Block() as block:
            @block.sync
            def _(sp):
                sp.dma_start(gain_b[:], broadcast_rows(gain, D)).then_inc(gain_in, 16)
                if out is not None:
                    for t, (o, p) in enumerate(TILES):
                        sp.wait_ge(rows_ready, t + 1)
                        sp.dma_start(out[t], h[0:p, t, :]).then_inc(stored, 16)
                    sp.wait_ge(stored, 48)

            @block.scalar
            def _(act):
                act.wait_ge(mean_ready, 1)
                nc.scalar.activation(st[:, :, 1], st[:, :, 0], ACT.Sqrt).then_inc(root_ready, 1)
                if hT is not None:
                    for t, (o, p) in enumerate(TILES):
                        act.wait_ge(cols_ready, t + 1)
                        nc.scalar.activation(
                            hT[:, :, o:o + p], pt[t][:, 0:KC * 128].rearrange("q (k c) -> q k c", k=KC)[:, :, 0:p],
                            ACT.Copy).then_inc(hT_done, 1)

            @block.vector
            def _(dve):
                ch = Chain(dve, steps)
                ch(nc.vector.memset(st[:], 1.0))
                for t, (o, p) in enumerate(TILES):
                    ch.step(nc.vector.tensor_tensor_reduce(
                        out=sq[0:p, t, :], in0=x[0:p, t, :], in1=x[0:p, t, :], scale=1.0, scalar=0.0,
                        op0=ALU.mult, op1=ALU.add, accum_out=st[0:p, t, 0:1]))
                ch.settle()
                nc.vector.tensor_scalar(st[:, :, 0], st[:, :, 0], 1.0 / D, EPS, ALU.mult, ALU.add).then_inc(
                    mean_ready, 1)
                dve.wait_ge(root_ready, 1)
                ch(nc.vector.reciprocal(st[:, :, 2], st[:, :, 1]))
                dve.wait_ge(gain_in, 16)
                for t, (o, p) in enumerate(TILES):
                    nc.vector.scalar_tensor_tensor(
                        out=h[0:p, t, :], in0=x[0:p, t, :], scalar=st[0:p, t, 2:3], in1=gain_b[0:p, :],
                        op0=ALU.mult, op1=ALU.mult).then_inc(rows_ready, 1)

            if hT is not None:
                @block.tensor
                def _(pe):
                    for t, (o, p) in enumerate(TILES):
                        pe.wait_ge(rows_ready, t + 1)
                        for k in range(KC):
                            last = nc.tensor.transpose(pt[t][:, k * 128:k * 128 + p],
                                                       h[0:p, t, k * 128:(k + 1) * 128], K["ident"][0:p, 0:p])
                        last.then_inc(cols_ready, 1)


BANKS = 6


def linear_phase(nc, name, K, xT, w, kc, width, rows, consume, on="vector", ring=3, extra_sb=None,
                 stores=None):
    wv = w.rearrange("(k p) n -> p k n", p=128)
    chunks = [(c, min(512, width - c)) for c in range(0, width, 512)]
    with ExitStack() as ctx:
        P = Phase(nc, ctx, name)
        ring = min(ring, len(chunks))
        wt = P.sb("w", [128, ring, kc, 512])
        acc = [P.ps(f"acc{b}", [128, 512]) for b in range(BANKS)]
        w_in = [P.sem(f"w_in{r}") for r in range(ring)]
        product_ready, bank_free, steps = P.sem("product_ready"), P.sem("bank_free"), P.sem("steps")
        ex = extra_sb(P) if extra_sb else None
        parts = 3 if rows else 4
        jobs = [(c, s, part) for c, (_, n) in enumerate(chunks) for s in (c,)
                for part in range(parts if rows else n // 128)]
        done_by = [sum(1 for j in jobs if j[0] <= c) for c in range(len(chunks))]
        with nc.Block() as block:
            @block.sync
            def _(sp):
                for c, (c0, n) in enumerate(chunks):
                    if c >= ring:
                        sp.wait_ge(product_ready, done_by[c - ring])
                    sp.dma_start(wt[:, c % ring, :, 0:n], wv[:, :, c0:c0 + n]).then_inc(w_in[c % ring], 16)

            @block.tensor
            def _(pe):
                for n, (c, _, part) in enumerate(jobs):
                    if n == 0 or jobs[n - 1][0] != c:
                        pe.wait_ge(w_in[c % ring], 16 * (c // ring + 1))
                    if n >= BANKS:
                        pe.wait_ge(bank_free, n - BANKS + 1)
                    for k in range(kc):
                        if rows:
                            o, p = TILES[part]
                            last = nc.tensor.matmul(acc[n % BANKS][0:p, 0:chunks[c][1]], xT[:, k, o:o + p],
                                                    wt[:, c % ring, k, 0:chunks[c][1]],
                                                    start=(k == 0), stop=(k == kc - 1))
                        else:
                            last = nc.tensor.matmul(acc[n % BANKS][:, 0:NTOK],
                                                    wt[:, c % ring, k, part * 128:(part + 1) * 128],
                                                    xT[:, k, 0:NTOK], start=(k == 0), stop=(k == kc - 1))
                    last.then_inc(product_ready, 1)

            def take(eng):
                ch = Chain(eng, steps)
                for n, (c, _, part) in enumerate(jobs):
                    eng.wait_ge(product_ready, n + 1)
                    consume(eng, c, part, acc[n % BANKS], ch, ex).then_inc(bank_free, 1)

            if on == "vector":
                block.vector(take)
            else:
                block.scalar(take)


def add_rows_phase(nc, name, K, xT, w):
    x = K["x"]

    def consume(eng, c, part, acc, ch, ex):
        o, p = TILES[part]
        cols = x[0:p, part, c * 512:(c + 1) * 512]
        return nc.vector.tensor_tensor(cols, cols, acc[0:p, :], ALU.add)

    linear_phase(nc, name, K, xT, w, KC, D, True, consume)


def columns_phase(nc, name, K, xT, w, width, outT):
    def consume(eng, c, part, acc, ch, ex):
        return nc.scalar.activation(outT[:, c * 4 + part, :], acc[:, 0:NTOK], ACT.Copy)

    linear_phase(nc, name, K, xT, w, KC, width, False, consume, on="scalar")


def conv_phase(nc, name, K, T, zT, mixT, conv, cache_out):
    with ExitStack() as ctx:
        P = Phase(nc, ctx, name)
        ra = P.sb("rows_state_a", [120, 2, D_A])
        rw = P.sb("rows_weights_a", [34, D_A])
        rq = P.sb("rows_qkv", [28, QKV_W])
        glu = P.sb("glu", [128, 4, NTOK])
        pa = P.sb("padded_a", [128, 4, CAW - 1 + SEQ])
        sa = P.sb("sample_a", [128, 4, DEC_B, CAW - 1 + DEC_T])
        pq = P.sb("padded_q", [128, 12, CQW - 1 + SEQ])
        sq = P.sb("sample_q", [128, 12, DEC_B, CQW - 1 + DEC_T])
        wa, wq = P.sb("taps_a", [128, 4, 34]), P.sb("taps_q", [128, 12, CQW])
        ca, tmp, ones = P.sb("conv_a", [128, 4, NTOK]), P.sb("tmp", [128, 8, NTOK]), P.sb("ones", [128, 128])
        root = P.sb("root", [128, 4, NTOK])
        tail_a, tail_q = P.sb("tail_a", [62, D_A]), P.sb("tail_q", [35, QKV_W])
        p_hist, p_w = P.ps("p_hist", [128, 1024]), P.ps("p_w", [128, 512])
        p_sum = P.ps("p_sum", [128, 4 * 512])
        loaded, hist_ready, w_ready, sig_ready = (
            P.sem(s) for s in ("loaded", "hist_ready", "w_ready", "sig_ready"))
        dve_steps, tail_ready, tail_copied, stored = (
            P.sem(s) for s in ("dve_steps", "tail_ready", "tail_copied", "stored"))
        sum_ready, root_ready, silu_ready, qkv_silu = (
            P.sem(s) for s in ("sum_ready", "root_ready", "silu_ready", "qkv_silu"))
        A0, Q0 = NTOK - NS - 30, NTOK - NS - 3

        mark = {}
        with nc.Block() as block:
            @block.vector
            def _(dve):
                ch = Chain(dve, dve_steps)
                V = nc.vector
                ch.step(V.memset(ones[:], 1.0))
                ch.step(V.memset(pa[:, :, 0:30], 0.0))
                ch.step(V.memset(pq[:, :, 0:3], 0.0))
                ch.step(V.tensor_copy(pq[:, :, 3:], zT[:, 8:20, 0:SEQ]))
                for c in range(12):
                    ch.step(V.tensor_copy(sq[:, c, :, 3:], zT[:, 8 + c, SEQ:].rearrange("p (b t) -> p b t", b=DEC_B)))
                dve.wait_ge(sig_ready, 1)
                ch(V.tensor_tensor(glu[:], zT[:, 0:4, :], zT[:, 4:8, :], ALU.mult))
                mark["glu"] = ch.n
                ch.step(V.tensor_copy(pa[:, :, 30:], glu[:, :, 0:SEQ]))
                for c in range(4):
                    ch.step(V.tensor_copy(sa[:, c, :, 30:], glu[:, c, SEQ:].rearrange("p (b t) -> p b t", b=DEC_B)))
                dve.wait_ge(hist_ready, 1)
                for hf in range(2):
                    for c in range(4):
                        ch.step(V.tensor_copy(
                            sa[:, c, hf * 4:hf * 4 + 4, 0:30],
                            p_hist[:, hf * 512 + c * 120:hf * 512 + (c + 1) * 120].rearrange(
                                "p (b t) -> p b t", b=4)))
                dve.wait_ge(w_ready, 1)
                ch.step(V.tensor_copy(wa[:], p_w[:, 0:136].rearrange("p (c r) -> p c r", c=4)))
                pw = p_w[:, 136:472].rearrange("p (c r) -> p c r", c=12)
                ch.step(V.tensor_copy(wq[:], pw[:, :, 24:28]))
                for c in range(12):
                    ch.step(V.tensor_copy(sq[:, c, :, 0:3], pw[:, c, 0:24].rearrange("p (b t) -> p b t", b=DEC_B)))
                ch.settle()

                def conv_taps(taps, tiles, pad, smp, wt, acc, bias):
                    for k in range(taps):
                        for c in range(tiles):
                            for part in range(2):
                                if k:
                                    ch.settle(lag=2 * tiles - 1)
                                if part == 0:
                                    src, dst = pad[:, c, k:k + SEQ], acc[:, c, 0:SEQ]
                                else:
                                    src = smp[:, c, :, k:k + DEC_T]
                                    dst = acc[:, c, SEQ:].rearrange("p (b t) -> p b t", b=DEC_B)
                                if k == 0 and bias is not None:
                                    ch.step(V.tensor_scalar(dst, src, wt[:, c, 0:1], bias(c), ALU.mult, ALU.add))
                                elif k == 0:
                                    ch.step(V.tensor_scalar(dst, src, wt[:, c, 0:1], None, ALU.mult))
                                else:
                                    ch.step(V.scalar_tensor_tensor(out=dst, in0=src, scalar=wt[:, c, k:k + 1],
                                                                   in1=dst, op0=ALU.mult, op1=ALU.add))
                    ch.settle()

                conv_taps(CQW, 12, pq, sq, wq, conv, None)
                mark["qkv"] = ch.n
                conv_taps(CAW, 4, pa, sa, wa, ca, lambda c: wa[:, c, 31:32])
                mark["sum", 0] = ch.n
                dve.wait_ge(sum_ready, 1)
                for c in range(4):
                    ch.step(V.scalar_tensor_tensor(out=ca[:, c, :], in0=p_sum[:, 0:NTOK], scalar=-1.0 / D_A,
                                                   in1=ca[:, c, :], op0=ALU.mult, op1=ALU.add))
                ch.settle()
                ch(V.tensor_tensor(tmp[:, 0:4, :], ca[:], ca[:], ALU.mult))
                mark["sum", 1] = ch.n
                dve.wait_ge(sum_ready, 2)
                ch(V.tensor_scalar(root[:, 0, :], p_sum[:, 0:NTOK], 1.0 / D_A, EPS, ALU.mult, ALU.add))
                mark["root", 0] = ch.n
                dve.wait_ge(root_ready, 1)
                ch(V.reciprocal(root[:, 0, :], root[:, 0, :]))
                for c in range(4):
                    ch.step(V.tensor_tensor(ca[:, c, :], ca[:, c, :], root[:, 0, :], ALU.mult))
                ch.settle()
                mark["silu"] = ch.n
                dve.wait_ge(qkv_silu, 1)
                ch(V.tensor_tensor(tmp[:], conv[:, 0:8, :], conv[:, 0:8, :], ALU.mult))
                for n in range(2):
                    mark["sum", 2 + n] = ch.n
                    dve.wait_ge(sum_ready, 3 + n)
                    ch(V.tensor_scalar(root[:], p_sum[:].rearrange("p (c n) -> p c n", c=4)[:, :, 0:NTOK], 1.0,
                                       EPS, ALU.mult, ALU.add))
                    mark["root", 1 + n] = ch.n
                    dve.wait_ge(root_ready, 2 + n)
                    ch(V.reciprocal(root[:], root[:]))
                    ch(V.scalar_tensor_tensor(out=conv[:, n * 4:n * 4 + 4, :], in0=conv[:, n * 4:n * 4 + 4, :],
                                              scalar=GD ** -0.5 if n == 0 else 1.0, in1=root[:],
                                              op0=ALU.mult, op1=ALU.mult))

            @block.sync
            def _(sp):
                st = T["state_conv_a"][0].rearrange("b r c -> (b r) c")
                for hf in range(2):
                    sp.dma_start(ra[:, hf, :], st[hf * 120:(hf + 1) * 120, :]).then_inc(loaded, 16)
                sp.dma_start(rw[0:31, :], T["conv_a_w"][0]).then_inc(loaded, 16)
                for n, w in enumerate(("conv_a_b", "ln_a_g", "ln_a_b")):
                    sp.dma_start(rw[31 + n:32 + n, :], T[w]).then_inc(loaded, 16)
                sp.dma_start(rq[0:24, :], T["state_conv_qkv"][0].rearrange("b r c -> (b r) c")).then_inc(loaded, 16)
                sp.dma_start(rq[24:28, :], T["conv_qkv_w"][0]).then_inc(loaded, 16)
                sp.dma_start(T["out_conv_a_s"][0, :, 0:26, :], T["state_conv_a"][0, :, 4:30, :]).then_inc(stored, 16)
                roll_cache(sp, T, 0, cache_out)
                roll_cache(sp, T, 1, cache_out)
                sp.wait_ge(tail_copied, 4)
                sp.dma_start(T["out_conv_a_p"][0, 0], tail_a[0:30, :]).then_inc(stored, 16)
                sp.dma_start(T["out_conv_qkv_p"][0, 0], tail_q[0:3, :]).then_inc(stored, 16)
                for b in range(DEC_B):
                    sp.dma_start(T["out_conv_a_s"][0, b, 26:30, :],
                                 tail_a[30 + 4 * b:34 + 4 * b, :]).then_inc(stored, 16)
                    sp.dma_start(T["out_conv_qkv_s"][0, b, :, :],
                                 tail_q[4 + 4 * b:7 + 4 * b, :]).then_inc(stored, 16)
                sp.wait_ge(stored, 16 * (3 + 2 * DEC_B))

            @block.tensor
            def _(pe):
                idn = K["ident"]
                pe.wait_ge(loaded, 128)
                for hf in range(2):
                    for c in range(4):
                        last = nc.tensor.transpose(p_hist[:, hf * 512 + c * 120:hf * 512 + (c + 1) * 120],
                                                   ra[0:120, hf, c * 128:(c + 1) * 128], idn[0:120, 0:120])
                last.then_inc(hist_ready, 1)
                for c in range(4):
                    nc.tensor.transpose(p_w[:, c * 34:(c + 1) * 34], rw[0:34, c * 128:(c + 1) * 128],
                                        idn[0:34, 0:34])
                for c in range(12):
                    last = nc.tensor.transpose(p_w[:, 136 + c * 28:136 + (c + 1) * 28],
                                               rq[0:28, c * 128:(c + 1) * 128], idn[0:28, 0:28])
                last.then_inc(w_ready, 1)
                pe.wait_ge(dve_steps, mark["glu"])
                for r in range(4):
                    for c in range(4):
                        if r == 0:
                            last = nc.tensor.transpose(p_sum[0:62, c * 128:(c + 1) * 128], glu[:, c, A0:NTOK], idn[:])
                        else:
                            last = nc.tensor.transpose(p_sum[0:35, r * 512 + c * 128:r * 512 + (c + 1) * 128],
                                                       zT[:, 8 + (r - 1) * 4 + c, Q0:NTOK], idn[:])
                    last.then_inc(tail_ready, 1)
                for n in range(4):
                    pe.wait_ge(dve_steps, mark["sum", n])
                    pe.wait_ge(tail_copied, 4)
                    src = ca if n == 0 else tmp
                    for c in range(4):
                        dst = p_sum[:, 0:NTOK] if n < 2 else p_sum[:, c * 512:c * 512 + NTOK]
                        s = src[:, (n == 3) * 4 + c, :]
                        last = nc.tensor.matmul(dst, ones[:], s, start=(c == 0 or n > 1), stop=(c == 3 or n > 1))
                    last.then_inc(sum_ready, 1)

            @block.scalar
            def _(act):
                nc.scalar.activation(zT[:, 4:8, :], zT[:, 4:8, :], ACT.Sigmoid).then_inc(sig_ready, 1)
                for r in range(4):
                    act.wait_ge(tail_ready, r + 1)
                    src = p_sum[0:62 if r == 0 else 35, r * 512:(r + 1) * 512]
                    dst = tail_a[:] if r == 0 else tail_q[:, (r - 1) * 512:r * 512]
                    nc.scalar.activation(dst, src, ACT.Copy).then_inc(tail_copied, 1)
                act.wait_ge(dve_steps, mark["qkv"])
                nc.scalar.activation(conv[:], conv[:], ACT.Silu).then_inc(qkv_silu, 1)
                act.wait_ge(dve_steps, mark["root", 0])
                nc.scalar.activation(root[:, 0, :], root[:, 0, :], ACT.Sqrt).then_inc(root_ready, 1)
                act.wait_ge(dve_steps, mark["silu"])
                for c in range(4):
                    nc.scalar.activation(mixT[:, c, :], ca[:, c, :], ACT.Silu, scale=wa[:, c, 32:33],
                                         bias=wa[:, c, 33:34]).then_inc(silu_ready, 1)
                for n in (1, 2):
                    act.wait_ge(dve_steps, mark["root", n])
                    nc.scalar.activation(root[:], root[:], ACT.Sqrt).then_inc(root_ready, 1)
                act.wait_ge(silu_ready, 4)


def delta_phase(nc, name, K, T, hT, zT, conv, mixT, cache_out):
    levels = (6, 6, 2)
    order = {"gates": ["ab pe", "ab dve", "ab act", "g dve"], "main": [], 0: [], 1: [], 2: []}
    for t in range(3):
        order[t] += ["gsum pe", "gsum dve", "wide pe", "args dve", "exps act", "cross pe", "cross dve", "rows pe",
                     "rows dve"]
        for lev in range(levels[t]):
            order[t] += [f"P {lev} pe", f"P {lev} dve", f"X {lev} pe", f"X {lev} dve"]
        order[t] += ["solve pe", "solve dve"]
    order[2] += ["wS pe", "wS dve", "wST pe", "v dve", "o pe", "o dve"]
    for h in range(GH):
        order[2] += [f"S {h} pe", f"S {h} dve"]
    for n in range(4):
        order["main"] += [f"c{n} wS pe", f"c{n} v dve", f"c{n} o pe", f"c{n} S dve"]
    order["main"] += ["square dve", "sum pe", "root dve", "root act", "out dve"]
    at = {(lane, n): i for lane, names in order.items() for i, n in enumerate(names)}

    def interleave(lanes):
        heads_of = [[next(lane), i, lane] for i, lane in enumerate(lanes)]
        while heads_of:
            first = min(heads_of, key=lambda e: e[:2])
            first[0] = next(first[2], None)
            if first[0] is None:
                heads_of.remove(first)

    with ExitStack() as ctx:
        P = Phase(nc, ctx, name)
        cst = P.sb("masks", [128, 12, 128])
        own = P.sb("owner", [128, DEC_B])
        wab = P.sb("w_ab", [128, KC, 8])
        alog, dtb, gn = P.sb("a_log", [128, 4]), P.sb("dt_bias", [128, 4]), P.sb("norm_gain", [128, 1])
        ab, gt = P.sb("ab", [128, 3, 8]), P.sb("g_tmp", [128, 3, 4])
        beta, g = P.sb("beta", [128, 3, 4]), P.sb("g", [128, 3, 4])
        per_tile = lambda name, shape: [P.sb(f"{name}{t}", shape) for t in range(3)]
        gc = per_tile("gc", [128, 5, 4])
        gbc = per_tile("g_wide", [128, 4, 128])
        dec, decT = per_tile("decay", [128, 4, 128]), per_tile("decayT", [128, 4, 128])
        eg = P.sb("exp_gcum", [128, 3, 4, 128])
        L, Lm = per_tile("L", [128, 4, 128]), gbc
        X, XT, P1 = dec, decT, per_tile("P1", [128, 4, 128])
        inT = P.sb("intraT", [128, 3, 4, 128])
        Rv, Rk, kd = per_tile("Rv", [128, 4, 128]), per_tile("Rk", [128, 4, 128]), P.sb("k_decay", [128, 3, 4, 128])
        u, wT, qe = P.sb("u", [128, 3, 4, 128]), P.sb("wT", [128, 3, 4, 128]), P.sb("q_exp", [128, 3, 4, 128])
        S, vn, vs = P.sb("S", [128, 4, 128]), P.sb("v_new", [128, 4, 128]), P.sb("v_new_s", [NS, 4, 128])
        S0 = P.sb("S_sample", [128, DEC_B, 4, 128])
        wS, vm = P.sb("wS", [128, 4, 32]), P.sb("v_owner", [32, DEC_B, 128])
        oT, ones = P.sb("oT", [128, 4, NTOK]), P.sb("ones", [128, 128])
        sqr = P.sb("sqr", [128, 4, NTOK])
        bank = [P.ps(f"bank{i}", [128, 512]) for i in range(8)]
        loaded, dve_steps, act_steps, stored = (P.sem(s) for s in ("loaded", "dve_steps", "act_steps", "stored"))
        turn = {"gates": P.sem("gate_turn"), "main": P.sem("main_turn")}
        turn.update({t: P.sem(f"tile{t}_turn") for t in range(3)})
        heads = [b[:].rearrange("q (h c) -> q h c", h=4) for b in bank]
        ident = K["ident"]
        GM = lambda t, k: cst[:, (3 if t == 2 else 0) + k, :]

        def rows_of(t, k):
            return heads[3 * t + k][0:TILES[t][1], :, :]

        def cols_of(t, k):
            if t < 2:
                return heads[3 * t + k]
            return bank[6 + k % 2][:, k // 2 * 128:k // 2 * 128 + 128].rearrange("q (h c) -> q h c", h=4)

        square = lambda t, k: cols_of(t, k)[0:TILES[t][1]]

        def begin(eng, lane, what):
            if lane == "main" and what == "c0 wS pe":
                eng.wait_ge(turn[0], len(order[0]))
                eng.wait_ge(turn[1], len(order[1]))
            elif lane in (0, 1, 2) and at[lane, what] == 0:
                eng.wait_ge(turn["gates"], len(order["gates"]))
            elif at[lane, what]:
                eng.wait_ge(turn[lane], at[lane, what])

        with nc.Block() as block:
            @block.sync
            def _(sp):
                sp.dma_start(wab[:], T["w_in_ab"][0].rearrange("(k p) n -> p k n", p=128)[:, :, IN_AB - 8:IN_AB]
                             ).then_inc(loaded, 16)
                sp.dma_start(cst[:], T["c_gdn"].rearrange("p (k n) -> p k n", k=12)).then_inc(loaded, 16)
                sp.dma_start(own[:], T["c_owner"]).then_inc(loaded, 16)
                sp.dma_start(alog[:], broadcast_rows(T["a_log"], 4)).then_inc(loaded, 16)
                sp.dma_start(dtb[:], broadcast_rows(T["dt_bias"], 4)).then_inc(loaded, 16)
                sp.dma_start(gn[:], T["gdn_norm_g"].rearrange("a n -> n a")).then_inc(loaded, 16)
                for b in range(DEC_B):
                    sp.dma_start(S0[:, b, :, :], T["state_delta"][0, b].rearrange("h k v -> k h v")
                                 ).then_inc(loaded, 16)
                roll_cache(sp, T, 2, cache_out, range(4))
                sp.wait_ge(turn["main"], at["main", "c3 S dve"] + 1)
                sp.dma_start(T["out_delta_p"][0, 0].rearrange("h k v -> k h v"), S[:]).then_inc(stored, 16)
                sp.wait_ge(turn[2], len(order[2]))
                for b in range(DEC_B):
                    sp.dma_start(T["out_delta_s"][0, b].rearrange("h k v -> k h v"), S0[:, b, :, :]
                                 ).then_inc(stored, 16)
                sp.wait_ge(stored, 16 * (1 + DEC_B))

            @block.tensor
            def _(pe):
                mm = nc.tensor.matmul

                def tile(t):
                    (o, p), done = TILES[t], turn[t]
                    yield at[t, "gsum pe"]
                    begin(pe, t, "gsum pe")
                    g0 = rows_of(t, 0)[:, 0, 0:8]
                    mm(g0[:, 0:4], GM(t, 0)[0:p, 0:p], g[0:p, t, :], start=True, stop=True)
                    mm(g0[:, 4:8], GM(t, 1)[0:p, 0:p], g[0:p, t, :], start=True, stop=True).then_inc(done, 1)
                    yield at[t, "wide pe"]
                    begin(pe, t, "wide pe")
                    for h in range(GH):
                        last = mm(cols_of(t, 1)[:, h, 0:p], gbc[t][0:p, h, :], GM(t, 0)[0:p, 0:p], start=True, stop=True)
                    last.then_inc(done, 1)
                    yield at[t, "cross pe"]
                    begin(pe, t, "cross pe")
                    for h in range(GH):
                        kk, qq = conv[:, 4 + h, o:o + p], conv[:, h, o:o + p]
                        mm(square(t, 0)[:, h, 0:p], kk, kk, start=True, stop=True)
                        last = mm(square(t, 2)[:, h, 0:p], kk, qq, start=True, stop=True)
                    last.then_inc(done, 1)
                    yield at[t, "rows pe"]
                    begin(pe, t, "rows pe")
                    for h in range(GH):
                        nc.tensor.transpose(rows_of(t, 0)[:, h, :], conv[:, 4 + h, o:o + p], ident[:])
                        last = nc.tensor.transpose(rows_of(t, 1)[:, h, :], conv[:, 8 + h, o:o + p], ident[:])
                    last.then_inc(done, 1)
                    for lev in range(levels[t]):
                        yield at[t, f"P {lev} pe"]
                        begin(pe, t, f"P {lev} pe")
                        for h in range(GH):
                            last = mm(square(t, 0)[:, h, 0:p], Lm[t][0:p, h, 0:p], XT[t][0:p, h, 0:p],
                                      start=True, stop=True)
                        last.then_inc(done, 1)
                        yield at[t, f"X {lev} pe"]
                        begin(pe, t, f"X {lev} pe")
                        for h in range(GH):
                            mm(square(t, 1)[:, h, 0:p], P1[t][0:p, h, 0:p], X[t][0:p, h, 0:p], start=True, stop=True)
                            last = mm(square(t, 2)[:, h, 0:p], X[t][0:p, h, 0:p], P1[t][0:p, h, 0:p],
                                      start=True, stop=True)
                        last.then_inc(done, 1)
                    yield at[t, "solve pe"]
                    begin(pe, t, "solve pe")
                    for h in range(GH):
                        mm(rows_of(t, 0)[:, h, :], XT[t][0:p, h, 0:p], Rv[t][0:p, h, :], start=True, stop=True)
                        last = mm(cols_of(t, 1)[:, h, 0:p], Rk[t][0:p, h, :], XT[t][0:p, h, 0:p], start=True, stop=True)
                    last.then_inc(done, 1)
                    if t < 2:
                        return
                    yield at[t, "wS pe"]
                    begin(pe, t, "wS pe")
                    for h in range(GH):
                        for b in range(DEC_B):
                            last = mm(cols_of(t, 0)[:, h, 4 * b:4 * b + 4], S0[:, b, h, :],
                                      wT[:, 2, h, 4 * b:4 * b + 4], start=True, stop=True)
                    last.then_inc(done, 1)
                    yield at[t, "wST pe"]
                    begin(pe, t, "wST pe")
                    for h in range(GH):
                        last = nc.tensor.transpose(rows_of(t, 1)[:, h, :], wS[:, h, :], ident[:])
                    last.then_inc(done, 1)
                    yield at[t, "o pe"]
                    begin(pe, t, "o pe")
                    for h in range(GH):
                        mm(cols_of(t, 0)[:, h, :], vs[:, h, :], inT[0:NS, 2, h, 0:NS], start=True, stop=True)
                        for b in range(DEC_B):
                            last = mm(cols_of(t, 2)[:, h, 4 * b:4 * b + 4], S0[:, b, h, :],
                                      qe[:, 2, h, 4 * b:4 * b + 4], start=True, stop=True)
                    last.then_inc(done, 1)
                    for h in range(GH):
                        yield at[t, f"S {h} pe"]
                        begin(pe, t, f"S {h} pe")
                        for hf in range(2):
                            last = mm(bank[6 + hf][:], kd[0:NS, 2, h, :], vm[:, hf * 4:hf * 4 + 4, :],
                                      start=True, stop=True)
                        last.then_inc(done, 1)

                pe.wait_ge(loaded, 16 * (6 + DEC_B))
                for t, (o, p) in enumerate(TILES):
                    for k in range(KC):
                        last = mm(bank[0][0:p, t * 8:t * 8 + 8], hT[:, k, o:o + p], wab[:, k, :],
                                  start=(k == 0), stop=(k == KC - 1))
                last.then_inc(turn["gates"], 1)
                interleave([tile(t) for t in range(3)])
                done = turn["main"]
                for n in range(4):
                    t, r = n // 2, slice(n % 2 * CHUNK, (n % 2 + 1) * CHUNK)
                    begin(pe, "main", f"c{n} wS pe")
                    for h in range(GH):
                        last = mm(heads[3][r, h, :], wT[:, t, h, r], S[:, h, :], start=True, stop=True)
                    last.then_inc(done, 1)
                    begin(pe, "main", f"c{n} o pe")
                    for h in range(GH):
                        mm(heads[4][:, h, 0:CHUNK], S[:, h, :], qe[:, t, h, r], start=True, stop=False)
                        mm(heads[4][:, h, 0:CHUNK], vn[r, h, :], inT[r, t, h, r], start=False, stop=True)
                        last = mm(heads[5][:, h, :], kd[r, t, h, :], vn[r, h, :], start=True, stop=True)
                    last.then_inc(done, 1)
                begin(pe, "main", "sum pe")
                for h in range(GH):
                    last = mm(bank[h][:, 0:NTOK], ones[:], sqr[:, h, :], start=True, stop=True)
                last.then_inc(done, 1)

            @block.scalar
            def _(act):
                ch = Chain(act, act_steps)
                A = nc.scalar.activation
                begin(act, "gates", "ab act")
                ch.step(A(beta[:], ab[:, :, 0:4], ACT.Sigmoid))
                ch.step(A(alog[:], alog[:], ACT.Exp))
                ch(A(gt[:], gt[:], ACT.Exp, scale=-1.0))
                A(gt[:], gt[:], ACT.Ln, bias=1.0).then_inc(turn["gates"], 1)
                for t, (o, p) in enumerate(TILES):
                    begin(act, t, "exps act")
                    A(dec[t][0:p, :, 0:p], dec[t][0:p, :, 0:p], ACT.Exp, scale=-1.0)
                    A(decT[t][0:p, :, 0:p], decT[t][0:p, :, 0:p], ACT.Exp)
                    A(eg[:, t, :, 0:p], cols_of(t, 1)[:, :, 0:p], ACT.Exp)
                    A(gc[t][0:p, 2:4, :], gc[t][0:p, 2:4, :], ACT.Exp).then_inc(turn[t], 1)
                begin(act, "main", "root act")
                A(sqr[:], sqr[:], ACT.Sqrt)
                A(zT[:, 20:24, :], zT[:, 20:24, :], ACT.Silu).then_inc(turn["main"], 1)

            @block.vector
            def _(dve):
                ch = Chain(dve, dve_steps)
                V = nc.vector
                TT, TS, STT = V.tensor_tensor, V.tensor_scalar, V.scalar_tensor_tensor

                def tile(t):
                    (o, p), done = TILES[t], turn[t]
                    yield at[t, "gsum dve"]
                    begin(dve, t, "gsum dve")
                    ch.step(V.tensor_copy(gc[t][0:p, 0:2, :],
                                          rows_of(t, 0)[:, 0, 0:8].rearrange("q (a h) -> q a h", a=2)))
                    V.tensor_copy(gbc[t][0:p, :, :], over(g[0:p, t, :], 2, 128)).then_inc(done, 1)
                    yield at[t, "args dve"]
                    begin(dve, t, "args dve")
                    ch.settle()
                    wide = square(t, 1)
                    for h in range(GH):
                        ch.step(TS(dec[t][0:p, h, 0:p], wide[:, h, 0:p], gc[t][0:p, 0, h:h + 1], 0.0,
                                   ALU.subtract, ALU.max))
                        ch.step(TS(decT[t][0:p, h, 0:p], wide[:, h, 0:p], gc[t][0:p, 0, h:h + 1], 0.0,
                                   ALU.subtract, ALU.min))
                    ch.step(V.tensor_copy(gc[t][0:p, 2, :], gc[t][0:p, 0, :]))
                    TT(gc[t][0:p, 3, :], gc[t][0:p, 1, :], gc[t][0:p, 0, :], ALU.subtract).then_inc(done, 1)
                    yield at[t, "cross dve"]
                    begin(dve, t, "cross dve")
                    ch.step(TT(gc[t][0:p, 4, :], gc[t][0:p, 2, :], beta[0:p, t, :], ALU.mult))
                    ch.step(TT(qe[:, t, :, 0:p], conv[:, 0:4, o:o + p], eg[:, t, :, 0:p], ALU.mult))
                    ch.step(TT(inT[0:p, t, :, 0:p], square(t, 2)[:, :, 0:p], decT[t][0:p, :, 0:p], ALU.mult))
                    for h in range(GH):
                        ch.step(STT(out=L[t][0:p, h, 0:p], in0=square(t, 0)[:, h, 0:p], scalar=beta[0:p, t, h:h + 1],
                                    in1=dec[t][0:p, h, 0:p], op0=ALU.mult, op1=ALU.mult))
                    ch.settle()
                    ch.step(TT(inT[0:p, t, :, 0:p], inT[0:p, t, :, 0:p], over(GM(t, 0)[0:p, 0:p], 1, 4), ALU.mult))
                    TT(L[t][0:p, :, 0:p], L[t][0:p, :, 0:p], over(GM(t, 2)[0:p, 0:p], 1, 4), ALU.mult).then_inc(done, 1)
                    yield at[t, "rows dve"]
                    begin(dve, t, "rows dve")
                    mask = lambda lev: over(cst[0:p, 6 + lev, 0:p], 1, 4)
                    for h in range(GH):
                        ch.step(TS(Rv[t][0:p, h, :], rows_of(t, 1)[:, h, :], beta[0:p, t, h:h + 1], None, ALU.mult))
                        ch.step(TS(Rk[t][0:p, h, :], rows_of(t, 0)[:, h, :], gc[t][0:p, 4, h:h + 1], None, ALU.mult))
                        ch.step(TS(kd[0:p, t, h, :], rows_of(t, 0)[:, h, :], gc[t][0:p, 3, h:h + 1], None, ALU.mult))
                    ch.settle()
                    ch.step(V.tensor_copy(X[t][0:p, :, 0:p], over(ident[0:p, 0:p], 1, 4)))
                    ch.step(V.tensor_copy(XT[t][0:p, :, 0:p], over(ident[0:p, 0:p], 1, 4)))
                    TT(Lm[t][0:p, :, 0:p], L[t][0:p, :, 0:p], mask(0), ALU.mult).then_inc(done, 1)
                    for lev in range(levels[t]):
                        yield at[t, f"P {lev} dve"]
                        begin(dve, t, f"P {lev} dve")
                        V.tensor_copy(P1[t][0:p, :, 0:p], square(t, 0)[:, :, 0:p]).then_inc(done, 1)
                        yield at[t, f"X {lev} dve"]
                        begin(dve, t, f"X {lev} dve")
                        ch.step(TT(X[t][0:p, :, 0:p], X[t][0:p, :, 0:p], square(t, 1)[:, :, 0:p], ALU.subtract))
                        if lev + 1 < levels[t]:
                            ch.step(TT(Lm[t][0:p, :, 0:p], L[t][0:p, :, 0:p], mask(lev + 1), ALU.mult))
                        TT(XT[t][0:p, :, 0:p], XT[t][0:p, :, 0:p], square(t, 2)[:, :, 0:p], ALU.subtract
                           ).then_inc(done, 1)
                    yield at[t, "solve dve"]
                    begin(dve, t, "solve dve")
                    ch.step(V.tensor_copy(u[0:p, t, :, :], rows_of(t, 0)))
                    V.tensor_copy(wT[:, t, :, 0:p], cols_of(t, 1)[:, :, 0:p]).then_inc(done, 1)
                    if t < 2:
                        return
                    yield at[t, "wS dve"]
                    begin(dve, t, "wS dve")
                    V.tensor_copy(wS[:], cols_of(t, 0)).then_inc(done, 1)
                    yield at[t, "v dve"]
                    begin(dve, t, "v dve")
                    TT(vs[:], u[0:NS, 2, :, :], rows_of(t, 1), ALU.subtract).then_inc(done, 1)
                    yield at[t, "o dve"]
                    begin(dve, t, "o dve")
                    ch(V.tensor_copy(oT[:, :, SEQ:], cols_of(t, 0)))
                    ch.step(TT(oT[:, :, SEQ:], oT[:, :, SEQ:], cols_of(t, 2), ALU.add))
                    for h in range(GH):
                        glast = eg[:, 2, h, 0:NS].rearrange("p (b t) -> p b t", t=DEC_T)[:, :, DEC_T - 1]
                        ch.step(TT(S0[:, :, h, :], S0[:, :, h, :], over(glast, 2, 128), ALU.mult))
                    ch.settle()
                    spread = lambda h: TT(vm[:], over(vs[:, h, :], 1, DEC_B), over(own[0:NS, :], 2, 128), ALU.mult)
                    spread(0).then_inc(done, 1)
                    for h in range(GH):
                        yield at[t, f"S {h} dve"]
                        begin(dve, t, f"S {h} dve")
                        for hf in range(2):
                            d = S0[:, hf * 4:hf * 4 + 4, h, :]
                            last = TT(d, d, heads[6 + hf], ALU.add)
                            if hf == 0 or h + 1 < GH:
                                ch.step(last)
                        (spread(h + 1) if h + 1 < GH else last).then_inc(done, 1)

                ch.step(V.memset(ab[:], 0.0))
                ch.step(V.memset(ones[:], 1.0))
                ch(V.memset(S[:], 0.0))
                begin(dve, "gates", "ab dve")
                for t, (o, p) in enumerate(TILES):
                    ch.step(V.tensor_copy(ab[0:p, t, :], bank[0][0:p, t * 8:t * 8 + 8]))
                ch.settle()
                ch(TT(ab[:, :, 4:8], ab[:, :, 4:8], over(dtb[:], 1, 3), ALU.add))
                ch(TS(gt[:], ab[:, :, 4:8], -1.0, None, ALU.mult))
                TT(gt[:], gt[:], ab[:, :, 4:8], ALU.max).then_inc(turn["gates"], 1)
                begin(dve, "gates", "g dve")
                ch(STT(out=gt[:], in0=ab[:, :, 4:8], scalar=0.0, in1=gt[:], op0=ALU.max, op1=ALU.add))
                STT(out=g[:], in0=gt[:], scalar=-1.0, in1=over(alog[:], 1, 3), op0=ALU.mult,
                    op1=ALU.mult).then_inc(turn["gates"], 1)
                interleave([tile(t) for t in range(3)])
                done = turn["main"]
                for n in range(4):
                    t, r = n // 2, slice(n % 2 * CHUNK, (n % 2 + 1) * CHUNK)
                    begin(dve, "main", f"c{n} v dve")
                    ch.settle()
                    TT(vn[r, :, :], u[r, t, :, :], heads[3][r, :, :], ALU.subtract).then_inc(done, 1)
                    begin(dve, "main", f"c{n} S dve")
                    ch.step(V.tensor_copy(oT[:, :, n * CHUNK:(n + 1) * CHUNK], heads[4][:, :, 0:CHUNK]))
                    for h in range(GH):
                        last = STT(out=S[:, h, :], in0=S[:, h, :], scalar=eg[:, t, h, r.stop - 1:r.stop],
                                   in1=heads[5][:, h, :], op0=ALU.mult, op1=ALU.add)
                    last.then_inc(done, 1)
                begin(dve, "main", "square dve")
                ch.settle()
                TT(sqr[:], oT[:], oT[:], ALU.mult).then_inc(done, 1)
                begin(dve, "main", "root dve")
                for h in range(GH):
                    last = TS(sqr[:, h, :], bank[h][:, 0:NTOK], 1.0 / GD, EPS, ALU.mult, ALU.add)
                last.then_inc(done, 1)
                begin(dve, "main", "out dve")
                ch.step(TS(oT[:], oT[:], gn[:, 0:1], None, ALU.mult))
                ch(V.reciprocal(sqr[:], sqr[:]))
                ch(TT(oT[:], oT[:], sqr[:], ALU.mult))
                TT(mixT[:, 4:8, :], oT[:], zT[:, 20:24, :], ALU.mult).then_inc(done, 1)


def keys_phase(nc, name, K, keys, keysT):
    with ExitStack() as ctx:
        P = Phase(nc, ctx, name)
        rows = P.sb("rows", [128, 2 * PH, 64])
        pt = P.ps("pt", [128, PH * 128])
        loaded, ready, copied = P.sem("loaded"), P.sem("ready"), P.sem("copied")
        with nc.Block() as block:
            @block.sync
            def _(sp):
                sp.dma_start(rows[:], keys.rearrange("h c m k -> m (h c) k")).then_inc(loaded, 16)

            @block.tensor
            def _(pe):
                pe.wait_ge(loaded, 16)
                for h in range(PH):
                    last = nc.tensor.transpose(pt[:, h * 128:(h + 1) * 128], rows[:, 2 * h:2 * h + 2, :],
                                               K["ident"][:])
                last.then_inc(ready, 1)

            @block.scalar
            def _(act):
                act.wait_ge(ready, 1)
                nc.scalar.activation(keysT[:], pt[:].rearrange("p (h m) -> p h m", h=PH), ACT.Copy).then_inc(copied, 1)


RING = 8


def experts_phase(nc, name, K, T, qT, keysT, layer):
    x, h = K["x"], K["h"]
    u_tab, v_tab = (T[n].rearrange("l e d -> (l e) d") for n in ("peer_u", "peer_v"))
    heads = (PH, PH, 2)
    slots = tuple(n * TOPK for n in heads)
    groups = (2, 0, 1)
    place = {g: i for i, g in enumerate(groups)}
    loops = tuple((kind, g) for g in groups for kind in "uv")
    by_dve = lambda g: (3, 7) if g == 1 else ()
    halves = [slots[g] // RING for _, g in loops]
    before = {l: sum(halves[:i]) for i, l in enumerate(loops)}
    diags, n_diag = {}, 0
    for g in groups:
        diags[g] = n_diag
        n_diag += slots[g] // RING * (RING - len(by_dve(g)))
    acts = {g: sum(slots[i] // RING for i in groups[:place[g]]) for g in groups}

    with ExitStack() as ctx:
        P = Phase(nc, ctx, name)
        NH2 = 2 * PH
        iota = P.sb("iota", [128, 16])
        sc = P.sb("scores", [128, NH2, NKEY])
        ts, ti = P.sb("top", [128, NH2, TOPK]), P.sb("top_at", [128, NH2, TOPK], U32)
        tif = P.sb("top_at_f", [128, NH2, TOPK])
        cand, cand2 = P.sb("cand", [128, PH, TOPK * TOPK]), P.sb("cand2", [128, PH, TOPK * TOPK])
        bs, bp = P.sb("best", [128, PH, TOPK]), P.sb("best_at", [128, PH, TOPK], U32)
        be = P.sb("best_exp", [128, 3, PH, TOPK])
        part, partf = P.sb("part", [128, 2, SLOTS], U32), P.sb("part_f", [128, 2, SLOTS])
        hot = P.sb("one_hot", [128, SLOTS, TOPK])
        rowf, total = P.sb("row_f", [128, 2, SLOTS]), P.sb("total", [128, PH])
        idx, gate = P.sb("idx", [128, 3, SLOTS], U32), P.sb("gate", [128, 3, SLOTS])
        h_s = P.sb("h_s", [128, D])
        ring, cur = P.sb("ring", [128, RING, D]), P.sb("cur_idx", [128, 2, RING], U32)
        dots, weights = P.sb("dots", [128, 3, SLOTS]), P.sb("weights", [128, 3, SLOTS])
        dot_blk, w_blk = P.sb("dot_block", [128, 2, RING]), P.sb("weight_block", [128, 2, RING])
        diag, zero, four = P.sb("diag", [128, RING, 128]), P.sb("zero", [128, 128]), P.sb("four", [128, 32])
        side = P.sb("dve_sum", [128, D])
        ps = [P.ps("scores_p", [128, NH2 * NKEY]), P.ps("scores_s", [128, 1024])]
        acc = P.ps("acc", [128, D])
        landed = [P.sem(f"landed{r}") for r in range(RING)]
        freed = [P.sem(f"freed{r}") for r in range(RING)]
        consts_in, dve_steps, score_ready, exp_ready, gelu_ready, idx_copied, issued = (
            P.sem(n) for n in ("consts_in", "dve_steps", "score_ready", "exp_ready", "gelu_ready", "idx_copied",
                               "issued"))
        blk_ready, w_ready, diag_ready, acc_done, side_steps = (
            P.sem(n) for n in ("blk_ready", "w_ready", "diag_ready", "acc_done", "side_steps"))
        hid = lambda g: h[:, g, :] if g < 2 else h_s[:]
        def score(g, n):
            c = (n % 2 * PH + n // 2) * NKEY if g < 2 else n % 2 * 512 + n // 2 * NKEY
            return ps[g // 2][:, c:c + NKEY]
        mark = {}

        with nc.Block() as block:
            @block.vector
            def _(dve):
                ch = Chain(dve, dve_steps)
                V = nc.vector

                def search(g):
                    nh = heads[g]
                    n2, sl = 2 * nh, nh * TOPK
                    dve.wait_ge(score_ready, place[g] + 1)
                    for n in range(n2):
                        ch.step(V.max(ts[:, n, 0:8], score(g, n)))
                    for n in range(n2):
                        ch.settle(lag=n2 - 1)
                        ch.step(V.match_replace(sc[:, n, :], ts[:, n, 0:8], score(g, n), NEG))
                    for n in range(n2):
                        ch.settle(lag=n2 - 1)
                        ch.step(V.max(ts[:, n, 8:16], sc[:, n, :]))
                    for n in range(n2):
                        ch.step(V.max_index(ti[:, n, 0:8], ts[:, n, 0:8], score(g, n)))
                    mark["scores", g] = ch.n
                    for n in range(n2):
                        ch.settle(lag=2 * n2 - 1)
                        ch.step(V.max_index(ti[:, n, 8:16], ts[:, n, 8:16], sc[:, n, :]))
                    ch.settle()
                    ch.step(V.tensor_copy(tif[:, 0:n2], ti[:, 0:n2]))
                    for i in range(nh):
                        ch.step(V.tensor_tensor(cand[:, i, :].rearrange("q (a b) -> q a b", a=TOPK),
                                                over(ts[:, 2 * i, :], 2, TOPK), over(ts[:, 2 * i + 1, :], 1, TOPK),
                                                ALU.add))
                    for i in range(nh):
                        ch.settle(lag=nh - 1)
                        ch.step(V.max(bs[:, i, 0:8], cand[:, i, :]))
                    for i in range(nh):
                        ch.settle(lag=nh - 1)
                        ch.step(V.match_replace(cand2[:, i, :], bs[:, i, 0:8], cand[:, i, :], NEG))
                    for i in range(nh):
                        ch.settle(lag=nh - 1)
                        ch.step(V.max(bs[:, i, 8:16], cand2[:, i, :]))
                    for i in range(nh):
                        ch.step(V.max_index(bp[:, i, 0:8], bs[:, i, 0:8], cand[:, i, :]))
                    for i in range(nh):
                        ch.settle(lag=2 * nh - 1)
                        ch.step(V.max_index(bp[:, i, 8:16], bs[:, i, 8:16], cand2[:, i, :]))
                    ch.settle()
                    ch(V.tensor_tensor(be[:, g, 0:nh], bs[:, 0:nh], over(bs[:, 0:nh, 0], 2, TOPK), ALU.subtract))
                    mark["exp", g] = ch.n
                    bpv = bp[:, 0:nh].rearrange("q h k -> q (h k)")
                    ch.step(V.tensor_scalar(part[:, 0, 0:sl], bpv, 4, None, ALU.logical_shift_right))
                    ch(V.tensor_scalar(part[:, 1, 0:sl], bpv, 15, None, ALU.bitwise_and))
                    ch(V.tensor_copy(partf[:, :, 0:sl], part[:, :, 0:sl]))
                    for half in range(2):
                        hv = hot[:, 0:sl, :]
                        ch(V.tensor_tensor(hv, over(partf[:, half, 0:sl], 2, TOPK), over(iota[:, :], 1, sl),
                                           ALU.is_equal))
                        for i in range(nh):
                            hs = hot[:, i * TOPK:(i + 1) * TOPK, :]
                            ch.step(V.tensor_tensor(hs, hs, over(tif[:, 2 * i + half, :], 1, TOPK), ALU.mult))
                        ch.settle()
                        ch(V.tensor_reduce(rowf[:, half, 0:sl], hv, AX_X, ALU.add))
                    ch(V.tensor_scalar(rowf[:, 0, 0:sl], rowf[:, 0, 0:sl], float(NKEY), float(layer * NKEY * NKEY),
                                       ALU.mult, ALU.add))
                    ch(V.tensor_tensor(idx[:, g, 0:sl], rowf[:, 0, 0:sl], rowf[:, 1, 0:sl], ALU.add))
                    mark["idx", g] = ch.n

                def gates(g):
                    nh = heads[g]
                    dve.wait_ge(exp_ready, place[g] + 1)
                    ch(V.tensor_reduce(total[:, 0:nh], be[:, g, 0:nh], AX_X, ALU.add))
                    ch(V.reciprocal(total[:, 0:nh], total[:, 0:nh]))
                    ch(V.tensor_tensor(gate[:, g, 0:slots[g]].rearrange("q (h k) -> q h k", h=nh), be[:, g, 0:nh],
                                       over(total[:, 0:nh], 2, TOPK), ALU.mult))
                    dve.wait_ge(gelu_ready, place[g] + 1)
                    ch(V.tensor_tensor(weights[:, g, 0:slots[g]], weights[:, g, 0:slots[g]], gate[:, g, 0:slots[g]],
                                       ALU.mult))
                    mark["weights", g] = ch.n

                def dot_products(g):
                    k0 = before["u", g]
                    with dve.Fori(0, slots[g] // (2 * RING)) as i:
                        for hf in range(2):
                            for r in range(RING):
                                dve.wait_ge(landed[r], (i * 2 + (k0 + hf + 1)) * 16)
                                V.tensor_tensor_reduce(out=ring[:, r, :], in0=ring[:, r, :], in1=hid(g), scale=1.0,
                                                       scalar=0.0, op0=ALU.mult, op1=ALU.add,
                                                       accum_out=dot_blk[:, hf, r:r + 1]).then_inc(freed[r], 1)
                            dve.wait_ge(freed[RING - 1], i * 2 + (k0 + hf + 2))
                            V.tensor_copy(dots[:, g, bass.ds(i * (2 * RING) + hf * RING, RING)],
                                          dot_blk[:, hf, :]).then_inc(blk_ready, 1)

                def own_sums(g):
                    k0, mine = before["v", g], by_dve(g)
                    sd = side[:]
                    with dve.Fori(0, slots[g] // (2 * RING)) as i:
                        for hf in range(2):
                            for j, r in enumerate(mine):
                                dve.wait_ge(landed[r], (i * 2 + (k0 + hf + 1)) * 16)
                                dve.wait_ge(w_ready, i * 2 + (acts[g] + hf + 1))
                                dve.wait_ge(side_steps, i * (2 * len(mine)) + (hf * len(mine) + j + 1))
                                V.scalar_tensor_tensor(out=sd, in0=ring[:, r, :], scalar=w_blk[:, hf, r:r + 1],
                                                       in1=sd, op0=ALU.mult, op1=ALU.add).then_inc(side_steps, 1)
                                dve.wait_ge(side_steps, i * (2 * len(mine)) + (hf * len(mine) + j + 2))
                                dve.sem_inc(freed[r], 1)

                def add_group(g):
                    o, p = TILES[g]
                    dve.wait_ge(acc_done, place[g] + 1)
                    ch(V.tensor_tensor(x[0:p, g, :], x[0:p, g, :], acc[0:p, :], ALU.add))
                    mark["added", g] = ch.n

                ch.step(V.memset(zero[:], 0.0))
                V.memset(side[:], 0.0).then_inc(side_steps, 1)
                for r in range(RING):
                    dve.sem_inc(freed[r], 1)
                dve.wait_ge(consts_in, 16 * 6)
                search(2)
                dot_products(2)
                gates(2)
                search(0)
                add_group(2)
                dot_products(0)
                gates(0)
                search(1)
                add_group(0)
                dot_products(1)
                gates(1)
                own_sums(1)
                add_group(1)

            @block.scalar
            def _(act):
                A = nc.scalar.activation

                def exps(g):
                    act.wait_ge(dve_steps, mark["exp", g])
                    A(be[:, g, 0:heads[g]], be[:, g, 0:heads[g]], ACT.Exp).then_inc(exp_ready, 1)

                def gelu(g):
                    act.wait_ge(blk_ready, acts[g] + slots[g] // RING)
                    A(weights[:, g, 0:slots[g]], dots[:, g, 0:slots[g]], ACT.Gelu).then_inc(gelu_ready, 1)

                def diagonals(g):
                    idn, w = (K["ident"], 128) if g < 2 else (four, 32)
                    act.wait_ge(dve_steps, mark["weights", g])
                    with act.Fori(0, slots[g] // (2 * RING)) as i:
                        for hf in range(2):
                            k = before["v", g] + hf
                            A(w_blk[:, hf, :], weights[:, g, bass.ds(i * (2 * RING) + hf * RING, RING)], ACT.Copy
                              ).then_inc(w_ready, 1)
                            act.wait_ge(w_ready, i * 2 + (acts[g] + hf + 1))
                            for r in range(RING):
                                act.wait_ge(freed[r], i * 2 + (k + 1))
                                if r not in by_dve(g):
                                    A(diag[:, r, 0:w], idn[:, 0:w], ACT.Copy, scale=w_blk[:, hf, r:r + 1]
                                      ).then_inc(diag_ready, 1)

                act.wait_ge(consts_in, 16 * 6)
                for g in groups:
                    exps(g)
                    gelu(g)
                    diagonals(g)

            @block.tensor
            def _(pe):
                def scores(g):
                    o, p = TILES[g]
                    for n in range(2 * PH):
                        r = slice(n % 2 * 64, n % 2 * 64 + 64)
                        q, m = (slice(0, 128), n) if g < 2 else (slice(n // 4 * 32, n // 4 * 32 + 32), n % 4)
                        last = nc.tensor.matmul(score(g, m)[q, :], qT[r, n // 2, o:o + p], keysT[r, n // 2, :],
                                                start=True, stop=True)
                    last.then_inc(score_ready, 1)

                def weighted_sum(g):
                    w = 128 if g < 2 else 32
                    mine = [r for r in range(RING) if r not in by_dve(g)]
                    if place[g]:
                        pe.wait_ge(dve_steps, mark["added", groups[place[g] - 1]])
                    for c in range(2):
                        nc.tensor.matmul(acc[0:w, c * 512:(c + 1) * 512], zero[:, 0:w],
                                         h[:, 0, c * 512:(c + 1) * 512], start=True, stop=False)
                    with pe.Fori(0, slots[g] // (2 * RING)) as i:
                        for hf in range(2):
                            k = before["v", g] + hf
                            for j, r in enumerate(mine):
                                pe.wait_ge(landed[r], (i * 2 + (k + 1)) * 16)
                                pe.wait_ge(diag_ready, i * (2 * len(mine)) + (diags[g] + hf * len(mine) + j + 1))
                                for c in range(2):
                                    last = nc.tensor.matmul(acc[0:w, c * 512:(c + 1) * 512], diag[:, r, 0:w],
                                                            ring[:, r, c * 512:(c + 1) * 512], start=False, stop=False)
                                last.then_inc(freed[r], 1)
                    if by_dve(g):
                        pe.wait_ge(side_steps, 1 + slots[g] // RING * len(by_dve(g)))
                    one, rhs = (K["ident"][:], side[:]) if by_dve(g) else (zero[:, 0:w], h[:, 0, :])
                    for c in range(2):
                        last = nc.tensor.matmul(acc[0:w, c * 512:(c + 1) * 512], one, rhs[:, c * 512:(c + 1) * 512],
                                                start=False, stop=True)
                    last.then_inc(acc_done, 1)

                scores(2)
                scores(0)
                pe.wait_ge(dve_steps, 1)
                weighted_sum(2)
                pe.wait_ge(dve_steps, mark["scores", 0])
                scores(1)
                weighted_sum(0)
                weighted_sum(1)

            @block.sync
            def _(sp):
                sp.dma_start(iota[:], T["c_iota"]).then_inc(consts_in, 16)
                sp.dma_start(four[:], T["c_four"]).then_inc(consts_in, 16)
                for q in range(4):
                    sp.dma_start(h_s[32 * q:32 * q + 32, :], h[0:NS, 2, :]).then_inc(consts_in, 16)

            @block.gpsimd
            def _(pool):
                for kind, g in loops:
                    k0 = before[kind, g]
                    if kind == "u":
                        pool.wait_ge(dve_steps, mark["idx", g])
                    with pool.Fori(0, slots[g] // (2 * RING)) as i:
                        for hf in range(2):
                            nc.gpsimd.tensor_copy(cur[:, hf, :], idx[:, g, bass.ds(i * (2 * RING) + hf * RING, RING)]
                                                  ).then_inc(idx_copied, 1)
                            pool.wait_ge(idx_copied, i * 2 + (k0 + hf + 1))
                            for r in range(RING):
                                pool.wait_ge(freed[r], i * 2 + (k0 + hf + 1))
                                pool.sem_inc(issued, 1)
                                pool.indirect_dma_start(ring[:, r, :], None, u_tab if kind == "u" else v_tab,
                                                        bass.IndirectOffsetOnAxis(ap=cur[:, hf, r:r + 1], axis=0)
                                                        ).then_inc(landed[r], 16)


def ple_phase(nc, name, K, T, layer):
    x, hT = K["x"], K["hT"]
    with ExitStack() as ctx:
        P = Phase(nc, ctx, name)
        pr, pT = P.sb("p_rows", [128, 3, PLE]), P.sb("pT", [128, 2, NTOK])
        wg, wp = P.sb("w_gate", [128, 2, KC, 512]), P.sb("w_proj", [128, 2, D])
        sg = P.sb("gate", [128, 2, 512])
        pt = P.ps("pt", [128, 512])
        acc = [P.ps(f"acc{b}", [128, 2, 512]) for b in range(2)]
        p_in, wg_in, wp_in = P.sem("p_in"), [P.sem(f"wg_in{c}") for c in range(2)], P.sem("wp_in")
        pt_ready, pT_ready, acc_ready, gate_ready, acc_free, dve_steps = (
            P.sem(s) for s in ("pt_ready", "pT_ready", "acc_ready", "gate_ready", "acc_free", "dve_steps"))
        jobs = [(c, t) for c in range(2) for t in range(3)]
        with nc.Block() as block:
            @block.sync
            def _(sp):
                sp.dma_start(pr[:, 0:2, :], T["p_prompt"][layer, 0].rearrange("(t p) d -> p t d", p=128)).then_inc(p_in, 16)
                sp.dma_start(pr[0:NS, 2, :], T["p_sample"][layer].rearrange("b t d -> (b t) d")).then_inc(p_in, 16)
                sp.dma_start(wp[:], T["ple_proj"][layer].rearrange("(k p) n -> p k n", p=128)).then_inc(wp_in, 16)
                for c in range(2):
                    sp.dma_start(wg[:, c, :, :], T["ple_gate"][layer].rearrange("(k p) n -> p k n", p=128)
                                 [:, :, c * 512:(c + 1) * 512]).then_inc(wg_in[c], 16)

            @block.tensor
            def _(pe):
                pe.wait_ge(p_in, 32)
                for t, (o, p) in enumerate(TILES):
                    if t:
                        pe.wait_ge(pT_ready, t)
                    for k in range(2):
                        last = nc.tensor.transpose(pt[:, k * 128:k * 128 + p], pr[0:p, t, k * 128:(k + 1) * 128],
                                                   K["ident"][0:p, 0:p])
                    last.then_inc(pt_ready, 1)
                pe.wait_ge(pT_ready, 3)
                pe.wait_ge(wp_in, 16)
                for n, (c, t) in enumerate(jobs):
                    o, p = TILES[t]
                    if t == 0:
                        pe.wait_ge(wg_in[c], 16)
                    if n >= 2:
                        pe.wait_ge(acc_free, n - 1)
                    for k in range(KC):
                        nc.tensor.matmul(acc[n % 2][0:p, 0, :], hT[:, k, o:o + p], wg[:, c, k, :],
                                         start=(k == 0), stop=(k == KC - 1))
                    for k in range(2):
                        last = nc.tensor.matmul(acc[n % 2][0:p, 1, :], pT[:, k, o:o + p],
                                                wp[:, k, c * 512:(c + 1) * 512], start=(k == 0), stop=(k == 1))
                    last.then_inc(acc_ready, 1)

            @block.scalar
            def _(act):
                for t, (o, p) in enumerate(TILES):
                    act.wait_ge(pt_ready, t + 1)
                    nc.scalar.activation(pT[:, :, o:o + p], pt[:, 0:256].rearrange("q (k c) -> q k c", k=2)[:, :, 0:p],
                                         ACT.Copy).then_inc(pT_ready, 1)
                for n, (c, t) in enumerate(jobs):
                    p = TILES[t][1]
                    act.wait_ge(acc_ready, n + 1)
                    if n >= 2:
                        act.wait_ge(acc_free, n - 1)
                    nc.scalar.activation(sg[0:p, n % 2, :], acc[n % 2][0:p, 0, :], ACT.Sigmoid).then_inc(gate_ready, 1)

            @block.vector
            def _(dve):
                ch = Chain(dve, dve_steps)
                for n, (c, t) in enumerate(jobs):
                    p = TILES[t][1]
                    dve.wait_ge(gate_ready, n + 1)
                    ch(nc.vector.tensor_tensor(sg[0:p, n % 2, :], sg[0:p, n % 2, :], acc[n % 2][0:p, 1, :], ALU.mult))
                    xs = x[0:p, t, c * 512:(c + 1) * 512]
                    nc.vector.tensor_tensor(xs, xs, sg[0:p, n % 2, :], ALU.add).then_inc(acc_free, 1)


def tail(nc, K, T, layer, phases=99, stop=99):
    h, hT = K["h"], K["hT"]
    norm_phase(nc, f"nf{layer}", K, T["norm_ffn"][layer:layer + 1, :], h, hT)
    with ExitStack() as ctx:
        P = Phase(nc, ctx, f"peer{layer}")
        qT, keysT = P.sb("qT", [128, PH, NTOK]), P.sb("keysT", [128, PH, NKEY])
        keys_phase(nc, f"keys{layer}", K, T["peer_keys"][layer], keysT)
        columns_phase(nc, f"wq{layer}", K, hT, T["peer_wq"][layer], D, qT)
        experts_phase(nc, f"exp{layer}", K, T, qT, keysT, layer)
    if phases == stop: return
    norm_phase(nc, f"np{layer}", K, T["norm_ple"][layer:layer + 1, :], h, hT)
    ple_phase(nc, f"ple{layer}", K, T, layer)


def qkv_phase(nc, name, K, T, qP, kP, vP, qS, kS, vS, cache_out):
    hT = K["hT"]
    w = T["w_in_c"][0].rearrange("(k p) n -> p k n", p=128)
    chunks, WR = 18, 2
    jobs = [(c, t) for c in range(chunks) for t in range(3)]
    turned = [n for n, (c, t) in enumerate(jobs) if c < 12]

    def k_stores(slot, n):
        kept = lambda c, t: t == 2 or TILES[t][0] >= SEQ - min(PATTERNS[c % 6 // 2][0], SEQ)
        return sum(1 for m in turned[:n] if m % 4 == slot and jobs[m][0] >= 6 and kept(*jobs[m]))

    with ExitStack() as ctx:
        P = Phase(nc, ctx, name)
        wt = P.sb("w", [128, WR, KC, 512])
        rope = P.sb("rope", [128, 3, 2, ROT])
        rows = P.sb("rows", [128, 4, 4, HD])
        r1, r2 = P.sb("r1", [128, 2, 4, ROT]), P.sb("r2", [128, 2, 4, ROT])
        acc = [P.ps(f"acc{b}", [128, 512]) for b in range(4)]
        pt = [P.ps(f"pt{b}", [128, 512]) for b in range(4)]
        w_in = [P.sem(f"w_in{r}") for r in range(WR)]
        rope_in, product_ready, copied, dve_steps, roped, turned_ready, turned_out, stored = (
            P.sem(s) for s in ("rope_in", "product_ready", "copied", "dve_steps", "roped", "turned_ready",
                               "turned_out", "stored"))
        slot_stored = [P.sem(f"slot_stored{i}") for i in range(4)]
        with nc.Block() as block:
            @block.sync
            def _(sp):
                sp.dma_start(rope[:], T["c_rope"].rearrange("p (t a r) -> p t a r", t=3, a=2)).then_inc(rope_in, 16)
                for c in range(chunks):
                    if c >= WR:
                        sp.wait_ge(product_ready, 3 * (c - WR + 1))
                    sp.dma_start(wt[:, c % WR, :, :], w[:, :, c * 512:(c + 1) * 512]).then_inc(w_in[c % WR], 16)

            @block.gpsimd
            def _(pool):
                n_out = 0
                for n, (c, t) in enumerate(jobs):
                    kind, gi, half = c // 6, c % 6 // 2, c % 2
                    if kind == 0:
                        continue
                    o, p = TILES[t]
                    if kind == 1:
                        pool.wait_ge(roped, turned.index(n) + 1)
                        src = rows[0:p, turned.index(n) % 4, :, :]
                    else:
                        pool.wait_ge(copied, n + 1)
                        src = (vP[:, t] if t < 2 else vS[:])[:, gi, half * 4:half * 4 + 4, :]
                    hs = slice(half * 4, half * 4 + 4)
                    keep = min(PATTERNS[gi][0], SEQ)
                    done = slot_stored[turned.index(n) % 4] if kind == 1 else stored
                    if t < 2:
                        if o >= SEQ - keep:
                            pool.dma_start(T[f"out_kv{gi}_p"][0, 0, o - SEQ + keep:o - SEQ + keep + 128, kind - 1, hs, :],
                                           src).then_inc(done, 16)
                            n_out += kind == 2
                    else:
                        full = T[f"out_kv{gi}_s"].shape[2]
                        pool.dma_start(T[f"out_kv{gi}_s"][0, :, full - DEC_T:full, kind - 1, hs, :], src).then_inc(
                            done, 16)
                        n_out += kind == 2
                pool.wait_ge(stored, 16 * n_out)
                for i in range(4):
                    pool.wait_ge(slot_stored[i], 16 * k_stores(i, len(turned)))

            @block.tensor
            def _(pe):
                def turn(m):
                    n = turned[m]
                    o, p = TILES[jobs[n][1]]
                    pe.wait_ge(roped, m + 1)
                    if m >= 4:
                        pe.wait_ge(turned_out, m - 3)
                    for h in range(4):
                        last = nc.tensor.transpose(pt[m % 4][:, h * 128:h * 128 + p], rows[0:p, m % 4, h, :],
                                                   K["ident"][0:p, 0:p])
                    last.then_inc(turned_ready, 1)

                for n, (c, t) in enumerate(jobs):
                    o, p = TILES[t]
                    if t == 0:
                        pe.wait_ge(w_in[c % WR], 16 * (c // WR + 1))
                    if n >= 4:
                        pe.wait_ge(copied, n - 3)
                        if n - 4 < len(turned):
                            pe.wait_ge(roped, n - 3)
                    for k in range(KC):
                        last = nc.tensor.matmul(acc[n % 4][0:p, :], hT[:, k, o:o + p], wt[:, c % WR, k, :],
                                                start=(k == 0), stop=(k == KC - 1))
                    last.then_inc(product_ready, 1)
                    if 2 <= n < len(turned) + 2:
                        turn(n - 2)

            @block.scalar
            def _(act):
                for n, (c, t) in enumerate(jobs):
                    p = TILES[t][1]
                    act.wait_ge(product_ready, n + 1)
                    if t == 0 and c in (1, 5, 9, 13):
                        roll_cache(act, T, 2, cache_out, (4 + c // 4,))
                    gi, half = c % 6 // 2, c % 2
                    if c < 12:
                        if n >= 4:
                            act.wait_ge(turned_ready, n - 3)
                            if k_stores(n % 4, n):
                                act.wait_ge(slot_stored[n % 4], 16 * k_stores(n % 4, n))
                        dst = rows[0:p, n % 4, :, :]
                    else:
                        dst = (vP[:, t] if t < 2 else vS[:])[:, gi, half * 4:half * 4 + 4, :]
                    nc.scalar.activation(dst, acc[n % 4][0:p, :].rearrange("q (h e) -> q h e", h=4), ACT.Copy
                                         ).then_inc(copied, 1)
                    if 3 <= n < len(turned) + 3:
                        m = n - 3
                        cm, tm = jobs[turned[m]]
                        om, pm = TILES[tm]
                        dstT = (qP if cm < 6 else kP) if tm < 2 else (qS if cm < 6 else kS)
                        om = om % SEQ
                        h0 = cm % 6 * 4
                        act.wait_ge(turned_ready, m + 1)
                        nc.scalar.activation(dstT[:, h0:h0 + 4, om:om + pm],
                                             pt[m % 4][:].rearrange("q (h c) -> q h c", h=4)[:, :, 0:pm], ACT.Copy
                                             ).then_inc(turned_out, 1)

            @block.vector
            def _(dve):
                ch = Chain(dve, dve_steps)
                V = nc.vector
                dve.wait_ge(rope_in, 16)
                HR = ROT // 2
                for m, n in enumerate(turned):
                    c, t = jobs[n]
                    p = TILES[t][1]
                    a4 = acc[n % 4][0:p, :].rearrange("q (h e) -> q h e", h=4)
                    dve.wait_ge(copied, n + 1)
                    a, b = r1[0:p, m % 2], r2[0:p, m % 2]
                    ch.step(V.tensor_tensor(a, a4[:, :, 0:ROT], over(rope[0:p, t, 0, :], 1, 4), ALU.mult))
                    ch.step(V.tensor_tensor(b[:, :, 0:HR], a4[:, :, HR:ROT], over(rope[0:p, t, 1, 0:HR], 1, 4), ALU.mult))
                    ch(V.tensor_tensor(b[:, :, HR:], a4[:, :, 0:HR], over(rope[0:p, t, 1, HR:], 1, 4), ALU.mult))
                    V.tensor_tensor(rows[0:p, m % 4, :, 0:ROT], a, b, ALU.add).then_inc(roped, 1)


def prompt_attention_phase(nc, name, K, T, qT, kT, v, mixT):
    units = [(h, it) for it in range(2) for h in range(CH)]
    with ExitStack() as ctx:
        P = Phase(nc, ctx, name)
        band = P.sb("band", [128, 2, NG, SEQ])
        s, pT = P.sb("s", [128, 2, NG, SEQ]), P.sb("pT", [128, 2, NG * 2, 128])
        st = P.sb("stats", [128, 2, 4])
        ps = [P.ps(f"scores{b}", [128, 1024]) for b in range(2)]
        pp = P.ps("turned", [128, 1024])
        po = [P.ps(f"out{b}", [128, 512]) for b in range(2)]
        band_in, score_ready, dve_steps, max_ready, exp_ready, norm_ready, turned, copied, out_ready, out_done = (
            P.sem(x) for x in ("band_in", "score_ready", "dve_steps", "max_ready", "exp_ready", "norm_ready",
                               "turned", "copied", "out_ready", "out_done"))
        with nc.Block() as block:
            @block.sync
            def _(sp):
                sp.dma_start(band[:], T["c_band"].rearrange("p (t g n) -> p t g n", t=2, g=NG)).then_inc(band_in, 16)

            @block.tensor
            def _(pe):
                def scores(n):
                    h, it = units[n]
                    if n >= 2:
                        pe.wait_ge(max_ready, n - 1)
                    for gi in range(NG):
                        last = nc.tensor.matmul(ps[n % 2][:, gi * SEQ:gi * SEQ + 128 * (it + 1)],
                                                qT[:, gi * CH + h, it * 128:(it + 1) * 128],
                                                kT[:, gi * CH + h, 0:128 * (it + 1)], start=True, stop=True)
                    last.then_inc(score_ready, 1)

                scores(0)
                for n, (h, it) in enumerate(units):
                    if n + 1 < len(units):
                        scores(n + 1)
                    pe.wait_ge(norm_ready, n + 1)
                    if n:
                        pe.wait_ge(copied, n)
                    for gi in range(NG):
                        for jt in range(it + 1):
                            last = nc.tensor.transpose(pp[:, (gi * 2 + jt) * 128:(gi * 2 + jt + 1) * 128],
                                                       s[:, n % 2, gi, jt * 128:(jt + 1) * 128], K["ident"][:])
                    last.then_inc(turned, 1)
                    pe.wait_ge(copied, n + 1)
                    if n >= 2:
                        pe.wait_ge(out_done, n - 1)
                    parts = [(gi, jt) for gi in range(NG) for jt in range(it + 1)]
                    for m, (gi, jt) in enumerate(parts):
                        last = nc.tensor.matmul(po[n % 2][:, 0:128], v[:, jt, gi, h, :], pT[:, n % 2, gi * 2 + jt, :],
                                                start=(m == 0), stop=(m == len(parts) - 1))
                    last.then_inc(out_ready, 1)

            @block.vector
            def _(dve):
                ch = Chain(dve, dve_steps)
                V = nc.vector
                dve.wait_ge(band_in, 16)
                for n, (h, it) in enumerate(units):
                    w = 128 * (it + 1)
                    sv = s[:, n % 2, :, 0:w]
                    dve.wait_ge(score_ready, n + 1)
                    if n >= 2:
                        dve.wait_ge(turned, n - 1)
                    ch(V.scalar_tensor_tensor(out=sv, in0=ps[n % 2][:, 0:NG * SEQ].rearrange("p (g n) -> p g n", g=NG)[:, :, 0:w],
                                              scalar=ATT_SCALE, in1=band[:, it, :, 0:w], op0=ALU.mult, op1=ALU.add))
                    ch(V.tensor_reduce(st[:, n % 2, 0:1], sv, mybir.AxisListType.XY, ALU.max))
                    V.tensor_scalar(st[:, n % 2, 1:2], st[:, n % 2, 0:1], -1.0, None, ALU.mult).then_inc(max_ready, 1)
                    dve.wait_ge(exp_ready, n + 1)
                    ch(V.reciprocal(st[:, n % 2, 3:4], st[:, n % 2, 2:3]))
                    V.tensor_scalar(sv, sv, st[:, n % 2, 3:4], None, ALU.mult).then_inc(norm_ready, 1)

            @block.scalar
            def _(act):
                for n, (h, it) in enumerate(units):
                    sv = s[:, n % 2, :, 0:128 * (it + 1)]
                    act.wait_ge(max_ready, n + 1)
                    nc.scalar.activation(sv, sv, ACT.Exp, bias=st[:, n % 2, 1:2], accum_out=st[:, n % 2, 2:3]
                                         ).then_inc(exp_ready, 1)
                    act.wait_ge(turned, n + 1)
                    src = pp[:, 0:NG * 256].rearrange("p (g j n) -> p g j n", g=NG, j=2)[:, :, 0:it + 1, :]
                    if n >= 2:
                        act.wait_ge(out_ready, n - 1)
                    nc.scalar.activation(pT[:, n % 2].rearrange("p (g j) n -> p g j n", j=2)[:, :, 0:it + 1, :], src,
                                         ACT.Copy).then_inc(copied, 1)
                    act.wait_ge(out_ready, n + 1)
                    nc.scalar.activation(mixT[:, h, it * 128:(it + 1) * 128], po[n % 2][:, 0:128], ACT.Copy
                                         ).then_inc(out_done, 1)


def sample_attention_phase(nc, name, K, T, qS, kS, vS, mixT):
    KT, NB, NEWK = 7, 4, 3
    WID = KT * 128 + NEWK * NS
    caches = [T["cache_kv_w128"][0], T["cache_kv_w512"][0], T["cache_kv_w2048"][0]]

    def key_tiles(dst, b, kv):
        c0, c1, c2 = (c[b, :, kv, :, :].rearrange("r h e -> r (h e)") for c in caches)
        c1 = c1.rearrange("(r t) c -> r t c", t=4)
        c2 = c2.rearrange("(r t) c -> r t c", t=16)
        out = [(dst[:, 0, :], c0), (dst[:, 1:5, :], c1)]
        for half in range(2):
            out.append((dst[half * 64:half * 64 + 64, 5:7, :],
                        c2[:, half:half + 3:2, :]))
        return out

    with ExitStack() as ctx:
        P = Phase(nc, ctx, name)
        kc, vc = P.sb("k_rows", [128, 2, KT, D]), P.sb("v_rows", [128, 2, KT, D])
        kTc = P.sb("k_cols", [128, 2, D])
        mask = P.sb("mask", [128, 2, WID])
        sT, s = P.sb("sT", [128, KT + NEWK, 128]), P.sb("s", [128, D])
        pT, st = P.sb("pT", [128, KT + NEWK, 128]), P.sb("stats", [128, 4])
        p_kt = [P.ps(f"keys{b}", [128, 1024]) for b in range(2)]
        p_sc = P.ps("scores", [128, 512])
        p_w = P.ps("wide", [128, 1024])
        mask_in, keys_ready, keys_copied, col_ready, col_copied = (
            P.sem(x) for x in ("mask_in", "keys_ready", "keys_copied", "col_ready", "col_copied"))
        k_in, v_in = ([P.sem(f"{x}{i}") for i in range(2)] for x in ("k_in", "v_in"))
        new_ready, new_copied, row_ready, dve_steps, max_ready, exp_ready, norm_ready = (
            P.sem(x) for x in ("new_ready", "new_copied", "row_ready", "dve_steps", "max_ready", "exp_ready",
                               "norm_ready"))
        back_ready, back_copied, out_ready, out_done, wide_copied, cols_ready = (
            P.sem(x) for x in ("back_ready", "back_copied", "out_ready", "out_done", "wide_copied", "cols_ready"))
        span = lambda k: slice(k * 128, k * 128 + 128) if k < KT else slice(896 + (k - KT) * NS, 896 + (k - KT + 1) * NS)
        with nc.Block() as block:
            @block.sync
            def _(sp):
                sp.dma_start(mask[:], T["c_samp"].rearrange("p (b n) -> p b n", b=2)).then_inc(mask_in, 16)
                for b in range(DEC_B):
                    if b >= 2:
                        sp.wait_ge(keys_ready, KT * (b - 1))
                    for to, frm in key_tiles(kc[:, b % 2], b, 0):
                        sp.dma_start(to, frm).then_inc(k_in[b % 2], 16)

            @block.gpsimd
            def _(pool):
                for b in range(DEC_B):
                    if b >= 2:
                        pool.wait_ge(out_ready, b - 1)
                    for to, frm in key_tiles(vc[:, b % 2], b, 1):
                        pool.dma_start(to, frm).then_inc(v_in[b % 2], 16)

            @block.tensor
            def _(pe):
                mm = nc.tensor.matmul
                group = lambda k: 0 if k == 0 else (1 if k < 5 else 2)
                tiles = [(b, k) for b in range(DEC_B) for k in range(KT)]

                def turn(n):
                    b, k = tiles[n]
                    if k == 0:
                        pe.wait_ge(k_in[b % 2], 64 * (b // 2 + 1))
                    if n >= 2:
                        pe.wait_ge(keys_copied, n - 1)
                    if n == NB * KT + 1:
                        pe.wait_ge(out_done, 1)
                    for h in range(CH):
                        last = nc.tensor.transpose(p_kt[n % 2][:, h * 128:(h + 1) * 128],
                                                   kc[:, b % 2, k, h * 128:(h + 1) * 128], K["ident"][:])
                    last.then_inc(keys_ready, 1)

                turn(0)
                for bb in range(2):
                    for b in range(bb * NB, bb * NB + NB):
                        for k in range(KT):
                            n = b * KT + k
                            if n + 1 < len(tiles):
                                turn(n + 1)
                            pe.wait_ge(keys_copied, n + 1)
                            if n:
                                pe.wait_ge(col_copied, n)
                            if n == NB * KT:
                                pe.wait_ge(new_copied, 1)
                            for h in range(CH):
                                q = qS[:, group(k) * CH + h, 4 * b:4 * b + 4]
                                last = mm(p_sc[:, h * 4:h * 4 + 4], kTc[:, n % 2, h * 128:(h + 1) * 128], q,
                                          start=True, stop=True)
                            last.then_inc(col_ready, 1)
                    pe.wait_ge(col_copied, (bb + 1) * NB * KT)
                    for gi in range(NG):
                        for h in range(CH):
                            q = qS[:, gi * CH + h, 16 * bb:16 * bb + 16].rearrange("e (b t) -> e b t", t=4)
                            dst = p_sc[0:NS, gi * 128:(gi + 1) * 128].rearrange("j (b h t) -> j b h t", b=4, h=CH)
                            last = mm(dst[:, :, h, :], kS[:, gi * CH + h, :], q, start=True, stop=True)
                    last.then_inc(new_ready, 1)
                    pe.wait_ge(new_copied, bb + 1)
                    if bb:
                        pe.wait_ge(wide_copied, bb)
                    for k in range(KT + NEWK):
                        r = 128 if k < KT else NS
                        last = nc.tensor.transpose(p_w[:, span(k)], sT[0:r, k, :], K["ident"][0:r, 0:r])
                    last.then_inc(row_ready, 1)
                    pe.wait_ge(norm_ready, bb + 1)
                    for half in range(2):
                        ks = range(0, 8) if half == 0 else range(8, KT + NEWK)
                        if half:
                            pe.wait_ge(back_copied, 2 * bb + 1)
                        for k in ks:
                            r = 128 if k < KT else NS
                            last = nc.tensor.transpose(p_w[0:r, (k % 8) * 128:(k % 8) * 128 + 128], s[:, span(k)],
                                                       K["ident"][:])
                        last.then_inc(back_ready, 1)
                    pe.wait_ge(back_copied, 2 * bb + 2)
                    for b4 in range(NB):
                        b = bb * NB + b4
                        pe.wait_ge(v_in[b % 2], 64 * (b // 2 + 1))
                        c = slice(b4 * 32, b4 * 32 + 32)
                        for half in range(2):
                            for k in range(KT + NEWK):
                                cols = slice(half * 512, half * 512 + 512)
                                if k < KT:
                                    l, r = pT[:, k, c], vc[:, b % 2, k, cols]
                                else:
                                    l, r = pT[0:NS, k, c], vS[:, k - KT, half * 4:half * 4 + 4, :]
                                last = mm(p_w[c, cols], l, r, start=(k == 0), stop=(k == KT + NEWK - 1))
                        last.then_inc(out_ready, 1)
                    pe.wait_ge(wide_copied, bb + 1)
                    for h in range(CH):
                        last = nc.tensor.transpose(p_kt[1][:, h * 128:(h + 1) * 128],
                                                   s[:, h * 128:(h + 1) * 128], K["ident"][:])
                    last.then_inc(cols_ready, 1)

            @block.vector
            def _(dve):
                ch = Chain(dve, dve_steps)
                V = nc.vector
                dve.wait_ge(mask_in, 16)
                for bb in range(2):
                    for b in range(bb * NB, bb * NB + NB):
                        for k in range(KT):
                            n = b * KT + k
                            dve.wait_ge(keys_ready, n + 1)
                            if n >= 2:
                                dve.wait_ge(col_ready, n - 1)
                            V.tensor_copy(kTc[:, n % 2, :], p_kt[n % 2][:]).then_inc(keys_copied, 1)
                    dve.wait_ge(row_ready, bb + 1)
                    sw = s[:, 0:WID]
                    ch(V.scalar_tensor_tensor(out=sw, in0=p_w[:, 0:WID], scalar=ATT_SCALE, in1=mask[:, bb, :],
                                              op0=ALU.mult, op1=ALU.add))
                    ch(V.tensor_reduce(st[:, 0:1], sw, AX_X, ALU.max))
                    V.tensor_scalar(st[:, 1:2], st[:, 0:1], -1.0, None, ALU.mult).then_inc(max_ready, 1)
                    dve.wait_ge(exp_ready, bb + 1)
                    ch(V.reciprocal(st[:, 3:4], st[:, 2:3]))
                    V.tensor_scalar(sw, sw, st[:, 3:4], None, ALU.mult).then_inc(norm_ready, 1)
                    dve.wait_ge(out_ready, NB * (bb + 1))
                    V.tensor_copy(s[:], p_w[:]).then_inc(wide_copied, 1)

            @block.scalar
            def _(act):
                A = nc.scalar.activation
                for bb in range(2):
                    if bb:
                        act.wait_ge(row_ready, bb)
                    for b in range(bb * NB, bb * NB + NB):
                        for k in range(KT):
                            act.wait_ge(col_ready, b * KT + k + 1)
                            A(sT[:, k, b % NB * 32:b % NB * 32 + 32], p_sc[:, 0:32], ACT.Copy).then_inc(col_copied, 1)
                    act.wait_ge(new_ready, bb + 1)
                    A(sT[0:NS, KT:, :], p_sc[0:NS, 0:NEWK * 128].rearrange("j (g n) -> j g n", g=NEWK), ACT.Copy
                      ).then_inc(new_copied, 1)
                    act.wait_ge(max_ready, bb + 1)
                    A(s[:, 0:WID], s[:, 0:WID], ACT.Exp, bias=st[:, 1:2], accum_out=st[:, 2:3]).then_inc(exp_ready, 1)
                    act.wait_ge(back_ready, 2 * bb + 1)
                    if bb:
                        act.wait_ge(out_ready, NB)
                    A(pT[:, 0:KT, :], p_w[:, 0:KT * 128].rearrange("p (k n) -> p k n", k=KT), ACT.Copy)
                    A(pT[0:NS, KT, :], p_w[0:NS, KT * 128:(KT + 1) * 128], ACT.Copy).then_inc(back_copied, 1)
                    act.wait_ge(back_ready, 2 * bb + 2)
                    A(pT[0:NS, KT + 1:, :], p_w[0:NS, 0:256].rearrange("p (k n) -> p k n", k=2), ACT.Copy
                      ).then_inc(back_copied, 1)
                    act.wait_ge(cols_ready, bb + 1)
                    dst = mixT[:, :, SEQ + 16 * bb:SEQ + 16 * bb + 16].rearrange("e h (b t) -> e h b t", t=4)
                    src = p_kt[1][:].rearrange("e (g b h t) -> e g h b t", g=CH, b=4, h=CH)
                    for h in range(CH):
                        last = A(dst[:, h], src[:, h, h], ACT.Copy)
                    last.then_inc(out_done, 1)


OUTS = [("y_p", (1, SEQ, D)), ("y_s", (DEC_B, DEC_T, D)), ("conv_a_p", (1, 1, 30, D_A)),
        ("conv_qkv_p", (1, 1, 3, QKV_W)), ("delta_p", (1, 1, GH, GD, GD)),
        ("kv0_p", (1, 1, 128, 2, CH, HD)), ("kv1_p", (1, 1, SEQ, 2, CH, HD)), ("kv2_p", (1, 1, SEQ, 2, CH, HD)),
        ("conv_a_s", (1, DEC_B, 30, D_A)), ("conv_qkv_s", (1, DEC_B, 3, QKV_W)),
        ("delta_s", (1, DEC_B, GH, GD, GD)), ("kv0_s", (1, DEC_B, 128, 2, CH, HD)),
        ("kv1_s", (1, DEC_B, 512, 2, CH, HD)), ("kv2_s", (1, DEC_B, PAST + DEC_T, 2, CH, HD))]


def build(nc, T, phases=99):
    with ExitStack() as ctx:
        P = Phase(nc, ctx, "all", clears=False)
        K = {"x": P.sb("x", [128, 3, D]), "ident": P.sb("ident", [128, 128]), "h": P.sb("h", [128, 3, D]),
             "hT": P.sb("hT", [128, KC, NTOK])}
        x, h, hT = K["x"], K["h"], K["hT"]
        mixT = P.sb("mixT", [128, KC, NTOK])
        x_in = P.sem("x_in")
        with nc.Block() as block:
            @block.sync
            def _(sp):
                sp.dma_start(K["ident"][:], T["c_ident"]).then_inc(x_in, 16)
                sp.dma_start(x[:, 0:2, :], T["x_prompt"][0].rearrange("(t p) d -> p t d", p=128)).then_inc(x_in, 16)
                sp.dma_start(x[0:NS, 2, :], T["x_sample"].rearrange("b t d -> (b t) d")).then_inc(x_in, 16)
                sp.wait_ge(x_in, 48)
        cache_out = P.sem("cache_out")
        norm_phase(nc, "n0", K, T["norm_mix"][0:1, :], h, hT)
        if phases == 1: return dump(nc, T, h)
        with ExitStack() as c2:
            P0 = Phase(nc, c2, "l0")
            zT, conv = P0.sb("zT", [128, 24, NTOK]), P0.sb("conv", [128, 12, NTOK])
            columns_phase(nc, "ab", K, hT, T["w_in_ab"][0], IN_AB - 8, zT)
            conv_phase(nc, "cv", K, T, zT, mixT, conv, cache_out)
            delta_phase(nc, "gd", K, T, hT, zT, conv, mixT, cache_out)
        add_rows_phase(nc, "oab", K, mixT, T["w_out_ab"][0])
        if phases == 2: return dump(nc, T, x)
        tail(nc, K, T, 0, phases, 3)
        if phases in (3, 4): return dump(nc, T, x)
        norm_phase(nc, "n1", K, T["norm_mix"][1:2, :], h, hT)
        with ExitStack() as c2:
            P1 = Phase(nc, c2, "l1")
            qS, kS = P1.sb("qS", [128, NG * CH, NS]), P1.sb("kS", [128, NG * CH, NS])
            vS = P1.sb("vS", [NS, NG, CH, HD])
            with ExitStack() as c3:
                P2 = Phase(nc, c3, "l1p")
                qP, kP = P2.sb("q", [128, NG * CH, SEQ]), P2.sb("k", [128, NG * CH, SEQ])
                vP = P2.sb("v", [128, 2, NG, CH, HD])
                qkv_phase(nc, "qkv", K, T, qP, kP, vP, qS, kS, vS, cache_out)
                prompt_attention_phase(nc, "pa", K, T, qP, kP, vP, mixT)
            sample_attention_phase(nc, "sa", K, T, qS, kS, vS, mixT)
        add_rows_phase(nc, "oc", K, mixT, T["w_out_c"][0])
        if phases == 5: return dump(nc, T, x)
        tail(nc, K, T, 1, phases, 6)
        if phases == 6: return dump(nc, T, x)
        y = [T["out_y_p"][0, 0:128, :], T["out_y_p"][0, 128:256, :], T["out_y_s"].rearrange("b t d -> (b t) d")]
        norm_phase(nc, "nl", K, T["norm_final"].rearrange("(a n) -> a n", a=1), h, None, y)
        with nc.Block() as block:
            @block.sync
            def _(sp):
                sp.wait_ge(cache_out, 16 * NG * DEC_B)


def roll_cache(eng, T, gi, cache_out, samples=range(DEC_B)):
    src, dst = T[f"cache_kv_w{PATTERNS[gi][0]}"][0], T[f"out_kv{gi}_s"][0]
    keep = dst.shape[1] - DEC_T
    drop = src.shape[1] - keep
    for b in samples:
        eng.dma_start(dst[b, 0:keep].rearrange("r k h e -> r (k h e)"),
                      src[b, drop:].rearrange("r k h e -> r (k h e)")).then_inc(cache_out, 16)


def dump(nc, T, x):
    with nc.semaphore("dbg") as s, nc.Block() as block:
        @block.sync
        def _(sp):
            sp.dma_start(T["dbg"][:, 0:2, :], x[:, 0:2, :]).then_inc(s, 16)
            sp.dma_start(T["dbg"][0:NS, 2, :], x[0:NS, 2, :]).then_inc(s, 16)
            sp.wait_ge(s, 32)


def kernel(**inputs):
    import concourse.bacc as bacc
    from concourse.bass_utils import run_bass_kernel_spmd

    nc = bacc.Bacc("TRN2", target_bir_lowering=False, num_devices=1)
    arrays = {k: np.ascontiguousarray(v) for k, v in inputs.items()}
    arrays.update({f"c_{k}": v for k, v in shape_constants().items()})
    T = {k: nc.dram_tensor(f"in_{k}", a.shape, mybir.dt.from_np(a.dtype), kind="ExternalInput").ap()
         for k, a in arrays.items()}
    for name, shape in OUTS:
        T[f"out_{name}"] = nc.dram_tensor(f"out_{name}", shape, F32, kind="ExternalOutput").ap()
    build(nc, T)
    r = run_bass_kernel_spmd(nc, [{f"in_{k}": a for k, a in arrays.items()}], core_ids=[0]).results[0]
    return tuple(r[f"out_{name}"] for name, _ in OUTS)
```

```python
from contextlib import ExitStack

import numpy as np
import concourse.bass as bass
from concourse import mybir

F32 = mybir.dt.float32
U32 = mybir.dt.uint32
ALU = mybir.AluOpType
ACT = mybir.ActivationFunctionType
AX_X = mybir.AxisListType.X

D = 1024
KC = D // 128
SEQ, DEC_B, DEC_T = 256, 8, 4
PAST = 1024
NS = DEC_B * DEC_T
NTOK = SEQ + NS
TILES = ((0, 128), (128, 128), (256, NS))
DEPTH = 2
EPS = 1e-6
D_A = 512
CAW = 31
GH, GD = 4, 128
CQW = 4
QKV_W = 1536
IN_AB = 2 * D_A + QKV_W + GH * GD + 2 * GH
CHUNK = 64
PATTERNS = ((128, 1), (512, 4), (2048, 16))
NG, CH, HD = 3, 8, 128
ROT = HD // 4
THETA = 500000.0
NEG = -1.0e30
PH, NKEY, TOPK = 8, 128, 16
SLOTS = PH * TOPK
PLE = 256
ATT_SCALE = HD ** -0.5


class Chain:

    def __init__(self, eng, sem):
        self.eng, self.sem, self.n = eng, sem, 0

    def step(self, ins):
        self.n += 1
        ins.then_inc(self.sem, 1)

    def settle(self, lag=0):
        if self.n - lag > 0:
            self.eng.wait_ge(self.sem, self.n - lag)

    def __call__(self, ins):
        self.step(ins)
        self.settle()


class Phase:

    def __init__(self, nc, ctx, name, clears=True):
        self.nc, self.ctx, self.name, self.sems = nc, ctx, name, []
        if clears:
            ctx.callback(self.clear)

    def clear(self):
        if self.sems:
            self.nc.clear_and_free_semaphores(self.sems)
            self.nc.all_engine_barrier(sem_only=True)

    def sb(self, name, shape, dt=F32):
        return self.ctx.enter_context(self.nc.sbuf_tensor(f"{self.name}_{name}", shape, dt))

    def ps(self, name, shape):
        return self.ctx.enter_context(self.nc.psum_tensor(f"{self.name}_{name}", shape, F32))

    def sem(self, name):
        self.sems.append(self.nc.alloc_semaphore(f"{self.name}_{name}"))
        return self.sems[-1]


def broadcast_rows(dram_row, n, parts=128):
    return bass.AP(tensor=dram_row.tensor, offset=dram_row.offset, ap=[[0, parts], [1, n]])


def over(ap, axis, n):
    pat = [list(p) for p in ap.ap]
    pat.insert(axis, [0, n])
    return bass.AP(tensor=ap.tensor, offset=ap.offset, ap=pat)


def shape_constants():
    i = np.arange(128)
    c = {}
    c["ident"] = np.eye(128)
    tok = np.concatenate([np.arange(SEQ), PAST + np.tile(np.arange(DEC_T), DEC_B), np.zeros(96)])
    inv = 1.0 / (np.float32(THETA) ** (np.arange(0, ROT, 2, dtype=np.float32) / np.float32(ROT)))
    ang = (tok.astype(np.float32)[:, None] * inv.astype(np.float32)[None, :]).astype(np.float32)
    cos, sin = np.cos(ang.astype(np.float64)), np.sin(ang.astype(np.float64))
    cc = np.concatenate([cos, cos, -sin, sin], 1)
    c["rope"] = cc.reshape(3, 128, 64).transpose(1, 0, 2).reshape(128, 192)
    c["four"] = np.tile(np.eye(32), (4, 1))
    c["iota"] = np.tile(np.arange(16.0), (128, 1))
    g = []
    for size in (CHUNK, DEC_T):
        same = i[:, None] // size == i[None, :] // size
        g += [same & (i[:, None] <= i[None, :]), same, same & (i[:, None] > i[None, :])]
    for lev in range(6):
        s = 1 << lev
        g.append((i[:, None] // (2 * s) == i[None, :] // (2 * s))
                 & (i[:, None] % (2 * s) >= s) & (i[None, :] % (2 * s) < s))
    c["gdn"] = np.stack([m.astype(float) for m in g], 1).reshape(128, -1)
    c["owner"] = np.repeat((i[:32, None] // DEC_T == np.arange(DEC_B)[None]).astype(float), 1, 1)
    c["owner"] = np.tile(c["owner"], (4, 1))
    m = np.full((128, 2, NG, SEQ), NEG)
    for it in range(2):
        rel = (it * 128 + i)[:, None] - np.arange(SEQ)[None]
        for gi, (win, dil) in enumerate(PATTERNS):
            m[:, it, gi][(rel >= 0) & (rel % dil == 0) & (rel // dil <= win // dil)] = 0
    c["band"] = m.reshape(128, -1)
    s = np.full((128, 2, 7 * 128 + 3 * NS), NEG)
    for p in range(128):
        b4, t = p // 32, p % DEC_T
        for bb in range(2):
            b = bb * 4 + b4
            s[p, bb, t:128] = 0
            for k in range(1, 7):
                s[p, bb, 128 * k + 32 * t:128 * k + 32 * t + 32] = 0
            s[p, bb, 896 + b * DEC_T:896 + b * DEC_T + t + 1] = 0
            for gi in (1, 2):
                s[p, bb, 896 + gi * NS + b * DEC_T + t] = 0
    c["samp"] = s.reshape(128, -1)
    c["spread"] = (i[:NS, None] == np.arange(DEC_B * 128)[None] // 32).astype(float)
    return {k: np.ascontiguousarray(v, dtype=np.float32) for k, v in c.items()}


def norm_phase(nc, name, K, gain, h, hT=None, out=None, ahead=(), keys=None):
    x = K["x"]
    with ExitStack() as ctx:
        P = Phase(nc, ctx, name)
        gain_b, st = P.sb("gain", [128, D]), P.sb("st", [128, 3, 3])
        pt = [P.ps(f"pt{t}", [128, KC * 128]) for t in range(3)] if hT is not None else None
        gain_in, mean_ready, root_ready, rows_ready, cols_ready, stored, steps = (
            P.sem(s) for s in ("gain_in", "mean_ready", "root_ready", "rows_ready", "cols_ready", "stored",
                               "dve_steps"))
        hT_done, keys_in, keys_ready = P.sem("hT_done"), P.sem("keys_in"), P.sem("keys_ready")
        if keys:
            key_rows, p_keys = P.sb("key_rows", [128, 2 * PH, 64]), P.ps("p_keys", [128, PH * 128])
        with nc.Block() as block:
            @block.sync
            def _(sp):
                if keys:
                    sp.dma_start(key_rows[:], keys[0].rearrange("h c m k -> m (h c) k")).then_inc(keys_in, 16)
                sp.dma_start(gain_b[:], broadcast_rows(gain, D)).then_inc(gain_in, 16)
                for to, frm, landed in ahead:
                    sp.dma_start(to, frm).then_inc(landed, 16)
                if out is not None:
                    for t, (o, p) in enumerate(TILES):
                        sp.wait_ge(rows_ready, t + 1)
                        sp.dma_start(out[t], h[0:p, t, :]).then_inc(stored, 16)
                    sp.wait_ge(stored, 48)

            @block.scalar
            def _(act):
                act.wait_ge(mean_ready, 1)
                nc.scalar.activation(st[:, :, 1], st[:, :, 0], ACT.Sqrt).then_inc(root_ready, 1)
                if keys:
                    act.wait_ge(keys_ready, 1)
                    nc.scalar.activation(keys[1][:], p_keys[:].rearrange("p (h m) -> p h m", h=PH), ACT.Copy
                                         ).then_inc(hT_done, 1)
                if hT is not None:
                    for t, (o, p) in enumerate(TILES):
                        act.wait_ge(cols_ready, t + 1)
                        nc.scalar.activation(
                            hT[:, :, o:o + p], pt[t][:, 0:KC * 128].rearrange("q (k c) -> q k c", k=KC)[:, :, 0:p],
                            ACT.Copy).then_inc(hT_done, 1)

            @block.vector
            def _(dve):
                ch = Chain(dve, steps)
                ch(nc.vector.memset(st[:], 1.0))
                for t, (o, p) in enumerate(TILES):
                    ch.step(nc.vector.tensor_tensor_reduce(
                        out=h[0:p, t, :], in0=x[0:p, t, :], in1=x[0:p, t, :], scale=1.0, scalar=0.0,
                        op0=ALU.mult, op1=ALU.add, accum_out=st[0:p, t, 0:1]))
                ch.settle()
                nc.vector.tensor_scalar(st[:, :, 0], st[:, :, 0], 1.0 / D, EPS, ALU.mult, ALU.add).then_inc(
                    mean_ready, 1)
                dve.wait_ge(root_ready, 1)
                ch(nc.vector.reciprocal(st[:, :, 2], st[:, :, 1]))
                dve.wait_ge(gain_in, 16)
                for t, (o, p) in enumerate(TILES):
                    nc.vector.scalar_tensor_tensor(
                        out=h[0:p, t, :], in0=x[0:p, t, :], scalar=st[0:p, t, 2:3], in1=gain_b[0:p, :],
                        op0=ALU.mult, op1=ALU.mult).then_inc(rows_ready, 1)

            if hT is not None:
                @block.tensor
                def _(pe):
                    if keys:
                        pe.wait_ge(keys_in, 16)
                        for n in range(PH):
                            last = nc.tensor.transpose(p_keys[:, n * 128:(n + 1) * 128],
                                                       key_rows[:, 2 * n:2 * n + 2, :], K["ident"][:])
                        last.then_inc(keys_ready, 1)
                    for t, (o, p) in enumerate(TILES):
                        pe.wait_ge(rows_ready, t + 1)
                        for k in range(KC):
                            last = nc.tensor.transpose(pt[t][:, k * 128:k * 128 + p],
                                                       h[0:p, t, k * 128:(k + 1) * 128], K["ident"][0:p, 0:p])
                        last.then_inc(cols_ready, 1)


BANKS = 6


class WeightRing:

    def __init__(self, P, w, width, slots):
        self.w, self.kc = w.rearrange("(k p) n -> p k n", p=128), w.shape[0] // 128
        self.chunks = [(c, min(512, width - c)) for c in range(0, width, 512)]
        self.slots = min(slots, len(self.chunks))
        self.sb = P.sb("w", [128, self.slots, self.kc, 512])
        self.landed = [P.sem(f"w_in{r}") for r in range(self.slots)]
        self.start = [self.load(c) for c in range(self.slots)]

    def load(self, c):
        c0, n = self.chunks[c]
        return self.sb[:, c % self.slots, :, 0:n], self.w[:, :, c0:c0 + n], self.landed[c % self.slots]


def linear_phase(nc, name, xT, w, width, rows, consume, on="vector", ahead=None, after=None):
    with ExitStack() as ctx:
        P = Phase(nc, ctx, name)
        W = ahead or WeightRing(P, w, width, 3)
        wt, kc, ring, chunks = W.sb, W.kc, W.slots, W.chunks
        acc = [P.ps(f"acc{b}", [128, 512]) for b in range(BANKS)]
        product_ready, bank_free = P.sem("product_ready"), P.sem("bank_free")
        parts = 3 if rows else 4
        jobs = [(c, s, part) for c, (_, n) in enumerate(chunks) for s in (c,)
                for part in range(parts if rows else n // 128)]
        done_by = [sum(1 for j in jobs if j[0] <= c) for c in range(len(chunks))]
        with nc.Block() as block:
            @block.sync
            def _(sp):
                for c in range(ring if ahead else 0, len(chunks)):
                    if c >= ring:
                        sp.wait_ge(product_ready, done_by[c - ring])
                    to, frm, landed = W.load(c)
                    sp.dma_start(to, frm).then_inc(landed, 16)
                if after:
                    after(sp)

            @block.tensor
            def _(pe):
                for n, (c, _, part) in enumerate(jobs):
                    if n == 0 or jobs[n - 1][0] != c:
                        pe.wait_ge(W.landed[c % ring], 16 * (c // ring + 1))
                    if n >= BANKS:
                        pe.wait_ge(bank_free, n - BANKS + 1)
                    for k in range(kc):
                        if rows:
                            o, p = TILES[part]
                            last = nc.tensor.matmul(acc[n % BANKS][0:p, 0:chunks[c][1]], xT[:, k, o:o + p],
                                                    wt[:, c % ring, k, 0:chunks[c][1]],
                                                    start=(k == 0), stop=(k == kc - 1))
                        else:
                            last = nc.tensor.matmul(acc[n % BANKS][:, 0:NTOK],
                                                    wt[:, c % ring, k, part * 128:(part + 1) * 128],
                                                    xT[:, k, 0:NTOK], start=(k == 0), stop=(k == kc - 1))
                    last.then_inc(product_ready, 1)

            def take(eng):
                for n, (c, _, part) in enumerate(jobs):
                    eng.wait_ge(product_ready, n + 1)
                    consume(eng, c, part, acc[n % BANKS]).then_inc(bank_free, 1)

            if on == "vector":
                block.vector(take)
            else:
                block.scalar(take)


def add_rows_phase(nc, name, K, xT, w, ahead=None):
    x = K["x"]

    def consume(eng, c, part, acc):
        o, p = TILES[part]
        cols = x[0:p, part, c * 512:(c + 1) * 512]
        return nc.vector.tensor_tensor(cols, cols, acc[0:p, :], ALU.add)

    linear_phase(nc, name, xT, w, D, True, consume, ahead=ahead)


def columns_phase(nc, name, xT, w, width, outT, ahead=None, after=None):
    def consume(eng, c, part, acc):
        return nc.scalar.activation(outT[:, c * 4 + part, :], acc[:, 0:NTOK], ACT.Copy)

    linear_phase(nc, name, xT, w, width, False, consume, on="scalar", ahead=ahead, after=after)


def conv_phase(nc, name, K, T, zT, mixT, conv, cache_out):
    PE_A = 1
    diag_groups = [(True, c, k, min(4, CAW - k)) for c in range(4 - PE_A, 4) for k in range(0, CAW, 4)]
    n_a = len(diag_groups)
    diag_groups += [(False, c, 0, CQW) for c in range(12)]
    with ExitStack() as ctx:
        P = Phase(nc, ctx, name)
        ra = P.sb("rows_state_a", [120, 2, D_A])
        rw = P.sb("rows_weights_a", [34, D_A])
        rq = P.sb("rows_qkv", [28, QKV_W])
        glu = P.sb("glu", [128, 4, NTOK])
        pa = P.sb("padded_a", [128, 4, CAW - 1 + SEQ])
        sa = P.sb("sample_a", [128, 4, DEC_B, CAW - 1 + DEC_T])
        pq = P.sb("padded_q", [128, 12, CQW - 1 + SEQ])
        sq = P.sb("sample_q", [128, 12, DEC_B, CQW - 1 + DEC_T])
        wa, wq = P.sb("taps_a", [128, 4, 34]), P.sb("taps_q", [128, 12, CQW])
        ca, tmp, ones = P.sb("conv_a", [128, 4, NTOK]), P.sb("tmp", [128, 8, NTOK]), P.sb("ones", [128, 128])
        root, diag = P.sb("root", [128, 4, NTOK]), P.sb("diag", [128, 2, 4, 128])
        tail_a, tail_q = P.sb("tail_a", [62, D_A]), P.sb("tail_q", [35, QKV_W])
        p_hist, p_w = P.ps("p_hist", [128, 1024]), P.ps("p_w", [128, 512])
        p_sum = P.ps("p_sum", [128, 4 * 512])
        loaded, hist_ready, w_ready, sig_ready = (
            P.sem(s) for s in ("loaded", "hist_ready", "w_ready", "sig_ready"))
        dve_steps, tail_ready, tail_copied, stored = (
            P.sem(s) for s in ("dve_steps", "tail_ready", "tail_copied", "stored"))
        sum_ready, root_ready, silu_ready, qkv_silu, diag_ready, group_done = (
            P.sem(s) for s in ("sum_ready", "root_ready", "silu_ready", "qkv_silu", "diag_ready", "group_done"))
        A0, Q0 = NTOK - NS - 30, NTOK - NS - 3

        mark = {}
        with nc.Block() as block:
            @block.vector
            def _(dve):
                ch = Chain(dve, dve_steps)
                V = nc.vector
                ch.step(V.memset(ones[:], 1.0))
                ch.step(V.memset(pa[:, :, 0:30], 0.0))
                ch.step(V.memset(pq[:, :, 0:3], 0.0))
                ch.step(V.tensor_copy(pq[:, :, 3:], zT[:, 8:20, 0:SEQ]))
                for c in range(12):
                    ch.step(V.tensor_copy(sq[:, c, :, 3:], zT[:, 8 + c, SEQ:].rearrange("p (b t) -> p b t", b=DEC_B)))
                dve.wait_ge(sig_ready, 1)
                ch(V.tensor_tensor(glu[:], zT[:, 0:4, :], zT[:, 4:8, :], ALU.mult))
                mark["glu"] = ch.n
                ch.step(V.tensor_copy(pa[:, :, 30:], glu[:, :, 0:SEQ]))
                for c in range(4):
                    ch.step(V.tensor_copy(sa[:, c, :, 30:], glu[:, c, SEQ:].rearrange("p (b t) -> p b t", b=DEC_B)))
                dve.wait_ge(hist_ready, 1)
                for hf in range(2):
                    for c in range(4):
                        ch.step(V.tensor_copy(
                            sa[:, c, hf * 4:hf * 4 + 4, 0:30],
                            p_hist[:, hf * 512 + c * 120:hf * 512 + (c + 1) * 120].rearrange(
                                "p (b t) -> p b t", b=4)))
                dve.wait_ge(w_ready, 1)
                ch.step(V.tensor_copy(wa[:], p_w[:, 0:136].rearrange("p (c r) -> p c r", c=4)))
                pw = p_w[:, 136:472].rearrange("p (c r) -> p c r", c=12)
                ch.step(V.tensor_copy(wq[:], pw[:, :, 24:28]))
                for c in range(12):
                    ch.step(V.tensor_copy(sq[:, c, :, 0:3], pw[:, c, 0:24].rearrange("p (b t) -> p b t", b=DEC_B)))
                ch.settle()
                mark["padded"] = ch.n

                def conv_taps(taps, tiles, pad, smp, wt, acc, bias):
                    for k in range(taps):
                        for c in range(tiles):
                            for part in range(2):
                                if k:
                                    ch.settle(lag=2 * tiles - 1)
                                if part == 0:
                                    src, dst = pad[:, c, k:k + SEQ], acc[:, c, 0:SEQ]
                                else:
                                    src = smp[:, c, :, k:k + DEC_T]
                                    dst = acc[:, c, SEQ:].rearrange("p (b t) -> p b t", b=DEC_B)
                                if k == 0:
                                    ch.step(V.tensor_scalar(dst, src, wt[:, c, 0:1], bias(c), ALU.mult, ALU.add))
                                else:
                                    ch.step(V.scalar_tensor_tensor(out=dst, in0=src, scalar=wt[:, c, k:k + 1],
                                                                   in1=dst, op0=ALU.mult, op1=ALU.add))
                    ch.settle()

                conv_taps(CAW, 4 - PE_A, pa, sa, wa, ca, lambda c: wa[:, c, 31:32])
                dve.wait_ge(group_done, n_a)
                for c in range(PE_A):
                    ch.step(V.tensor_scalar(ca[:, 4 - PE_A + c, :], p_hist[:, c * 512:c * 512 + NTOK],
                                            wa[:, 4 - PE_A + c, 31:32], None, ALU.add))
                mark["sum", 0] = ch.n
                dve.wait_ge(sum_ready, 1)
                for c in range(4):
                    ch.step(V.scalar_tensor_tensor(out=ca[:, c, :], in0=p_sum[:, 0:NTOK], scalar=-1.0 / D_A,
                                                   in1=ca[:, c, :], op0=ALU.mult, op1=ALU.add))
                ch.settle()
                ch(V.tensor_tensor(tmp[:, 0:4, :], ca[:], ca[:], ALU.mult))
                mark["sum", 1] = ch.n
                dve.wait_ge(sum_ready, 2)
                ch(V.tensor_scalar(root[:, 0, :], p_sum[:, 0:NTOK], 1.0 / D_A, EPS, ALU.mult, ALU.add))
                mark["root", 0] = ch.n
                dve.wait_ge(root_ready, 1)
                ch(V.reciprocal(root[:, 0, :], root[:, 0, :]))
                for c in range(4):
                    ch.step(V.tensor_tensor(ca[:, c, :], ca[:, c, :], root[:, 0, :], ALU.mult))
                ch.settle()
                mark["silu"] = ch.n
                dve.wait_ge(qkv_silu, 12)
                for n in range(2):
                    ch(V.tensor_tensor(tmp[:, n * 4:n * 4 + 4], conv[:, n * 4:n * 4 + 4, :],
                                       conv[:, n * 4:n * 4 + 4, :], ALU.mult))
                    mark["sum", 2 + n] = ch.n
                for n in range(2):
                    dve.wait_ge(sum_ready, 3 + n)
                    ch(V.tensor_scalar(root[:], p_sum[:].rearrange("p (c n) -> p c n", c=4)[:, :, 0:NTOK], 1.0,
                                       EPS, ALU.mult, ALU.add))
                    mark["root", 1 + n] = ch.n
                    dve.wait_ge(root_ready, 2 + n)
                    ch(V.reciprocal(root[:], root[:]))
                    ch(V.scalar_tensor_tensor(out=conv[:, n * 4:n * 4 + 4, :], in0=conv[:, n * 4:n * 4 + 4, :],
                                              scalar=GD ** -0.5 if n == 0 else 1.0, in1=root[:],
                                              op0=ALU.mult, op1=ALU.mult))

            @block.sync
            def _(sp):
                st = T["state_conv_a"][0].rearrange("b r c -> (b r) c")
                for hf in range(2):
                    sp.dma_start(ra[:, hf, :], st[hf * 120:(hf + 1) * 120, :]).then_inc(loaded, 16)
                sp.dma_start(rw[0:31, :], T["conv_a_w"][0]).then_inc(loaded, 16)
                for n, w in enumerate(("conv_a_b", "ln_a_g", "ln_a_b")):
                    sp.dma_start(rw[31 + n:32 + n, :], T[w]).then_inc(loaded, 16)
                sp.dma_start(rq[0:24, :], T["state_conv_qkv"][0].rearrange("b r c -> (b r) c")).then_inc(loaded, 16)
                sp.dma_start(rq[24:28, :], T["conv_qkv_w"][0]).then_inc(loaded, 16)
                sp.dma_start(T["out_conv_a_s"][0, :, 0:26, :], T["state_conv_a"][0, :, 4:30, :]).then_inc(stored, 16)
                roll_cache(sp, T, 1, cache_out, range(2, DEC_B))
                sp.wait_ge(tail_copied, 4)
                sp.dma_start(T["out_conv_a_p"][0, 0], tail_a[0:30, :]).then_inc(stored, 16)
                sp.dma_start(T["out_conv_qkv_p"][0, 0], tail_q[0:3, :]).then_inc(stored, 16)
                for b in range(DEC_B):
                    sp.dma_start(T["out_conv_a_s"][0, b, 26:30, :],
                                 tail_a[30 + 4 * b:34 + 4 * b, :]).then_inc(stored, 16)
                    sp.dma_start(T["out_conv_qkv_s"][0, b, :, :],
                                 tail_q[4 + 4 * b:7 + 4 * b, :]).then_inc(stored, 16)
                sp.wait_ge(stored, 16 * (3 + 2 * DEC_B))

            @block.tensor
            def _(pe):
                idn = K["ident"]
                pe.wait_ge(loaded, 128)
                for hf in range(2):
                    for c in range(4):
                        last = nc.tensor.transpose(p_hist[:, hf * 512 + c * 120:hf * 512 + (c + 1) * 120],
                                                   ra[0:120, hf, c * 128:(c + 1) * 128], idn[0:120, 0:120])
                last.then_inc(hist_ready, 1)
                for c in range(4):
                    nc.tensor.transpose(p_w[:, c * 34:(c + 1) * 34], rw[0:34, c * 128:(c + 1) * 128],
                                        idn[0:34, 0:34])
                for c in range(12):
                    last = nc.tensor.transpose(p_w[:, 136 + c * 28:136 + (c + 1) * 28],
                                               rq[0:28, c * 128:(c + 1) * 128], idn[0:28, 0:28])
                last.then_inc(w_ready, 1)
                pe.wait_ge(dve_steps, mark["glu"])
                for r in range(4):
                    for c in range(4):
                        if r == 0:
                            last = nc.tensor.transpose(p_sum[0:62, c * 128:(c + 1) * 128], glu[:, c, A0:NTOK], idn[:])
                        else:
                            last = nc.tensor.transpose(p_sum[0:35, r * 512 + c * 128:r * 512 + (c + 1) * 128],
                                                       zT[:, 8 + (r - 1) * 4 + c, Q0:NTOK], idn[:])
                    last.then_inc(tail_ready, 1)
                pe.wait_ge(dve_steps, mark["padded"])
                pe.wait_ge(tail_copied, 4)

                def taps(i):
                    is_a, c, k0, n = diag_groups[i]
                    pad, smp = (pa, sa) if is_a else (pq, sq)
                    if is_a:
                        dst = p_hist[:, (c - 4 + PE_A) * 512:(c - 4 + PE_A) * 512 + NTOK]
                    else:
                        dst = p_sum[:, (1 + c % 3) * 512:(1 + c % 3) * 512 + NTOK]
                        if c >= 3:
                            pe.wait_ge(qkv_silu, c - 2)
                    last_tap = CAW - 1 if is_a else CQW - 1
                    pe.wait_ge(diag_ready, i + 1)
                    for part in range(2):
                        for k in range(k0, k0 + n):
                            src = pad[:, c, k:k + SEQ] if part == 0 else smp[:, c, :, k:k + DEC_T]
                            out = dst[:, 0:SEQ] if part == 0 else dst[:, SEQ:].rearrange("p (b t) -> p b t", b=DEC_B)
                            last = nc.tensor.matmul(out, diag[:, i % 2, k - k0, :], src,
                                                    start=(k == 0 and part == 0),
                                                    stop=(k == last_tap and part == 1))
                    last.then_inc(group_done, 1)

                def sums(n):
                    pe.wait_ge(dve_steps, mark["sum", n])
                    if n == 3:
                        pe.wait_ge(dve_steps, mark["root", 1])
                    if n == 2:
                        pe.wait_ge(qkv_silu, 12)
                    src = ca if n == 0 else tmp
                    for c in range(4):
                        dst = p_sum[:, 0:NTOK] if n < 2 else p_sum[:, c * 512:c * 512 + NTOK]
                        s = src[:, (n == 3) * 4 + c, :]
                        last = nc.tensor.matmul(dst, ones[:], s, start=(c == 0 or n > 1), stop=(c == 3 or n > 1))
                    last.then_inc(sum_ready, 1)

                for i in range(len(diag_groups)):
                    taps(i)
                for n in range(4):
                    sums(n)

            @block.scalar
            def _(act):
                nc.scalar.activation(zT[:, 4:8, :], zT[:, 4:8, :], ACT.Sigmoid).then_inc(sig_ready, 1)
                for r in range(4):
                    act.wait_ge(tail_ready, r + 1)
                    src = p_sum[0:62 if r == 0 else 35, r * 512:(r + 1) * 512]
                    dst = tail_a[:] if r == 0 else tail_q[:, (r - 1) * 512:r * 512]
                    nc.scalar.activation(dst, src, ACT.Copy).then_inc(tail_copied, 1)
                act.wait_ge(dve_steps, mark["padded"])

                def take(i):
                    c = diag_groups[i][1]
                    act.wait_ge(group_done, i + 1)
                    b = (1 + c % 3) * 512
                    nc.scalar.activation(conv[:, c, :], p_sum[:, b:b + NTOK], ACT.Silu).then_inc(qkv_silu, 1)

                for i, (is_a, c, k0, n) in enumerate(diag_groups):
                    if i >= 2:
                        act.wait_ge(group_done, i - 1)
                    for k in range(n):
                        last = nc.scalar.activation(diag[:, i % 2, k, :], K["ident"][:], ACT.Copy,
                                                    scale=(wa if is_a else wq)[:, c, k0 + k:k0 + k + 1])
                    last.then_inc(diag_ready, 1)
                    if i > n_a:
                        take(i - 1)
                take(len(diag_groups) - 1)
                act.wait_ge(dve_steps, mark["root", 0])
                nc.scalar.activation(root[:, 0, :], root[:, 0, :], ACT.Sqrt).then_inc(root_ready, 1)
                act.wait_ge(dve_steps, mark["silu"])
                for c in range(4):
                    nc.scalar.activation(mixT[:, c, :], ca[:, c, :], ACT.Silu, scale=wa[:, c, 32:33],
                                         bias=wa[:, c, 33:34]).then_inc(silu_ready, 1)
                for n in (1, 2):
                    act.wait_ge(dve_steps, mark["root", n])
                    nc.scalar.activation(root[:], root[:], ACT.Sqrt).then_inc(root_ready, 1)
                act.wait_ge(silu_ready, 4)


def delta_phase(nc, name, K, T, hT, zT, conv, mixT, cache_out):
    levels = (6, 6, 2)
    order = {"gates": ["ab pe", "ab dve", "ab act", "g dve"], "main": [], 0: [], 1: [], 2: []}
    for t in range(3):
        order[t] += ["gsum pe", "gsum dve", "wide pe", "args dve", "exps act", "cross pe", "cross dve", "rows pe",
                     "rows dve"]
        for lev in range(levels[t]):
            order[t] += [f"P {lev} pe", f"P {lev} dve", f"X {lev} pe", f"X {lev} dve"]
        order[t] += ["solve pe", "solve dve"]
    order[2] += ["wS pe", "wS dve", "wST pe", "v dve", "o pe", "o dve"]
    for h in range(GH):
        order[2] += [f"S {h} pe", f"S {h} dve"]
    for n in range(4):
        order["main"] += [f"c{n} wS pe", f"c{n} v dve", f"c{n} o pe", f"c{n} S dve"]
    order["main"] += ["square dve", "sum pe", "root dve", "root act", "out dve"]
    at = {(lane, n): i for lane, names in order.items() for i, n in enumerate(names)}

    def interleave(lanes):
        heads_of = [[next(lane), i, lane] for i, lane in enumerate(lanes)]
        while heads_of:
            first = min(heads_of, key=lambda e: e[:2])
            first[0] = next(first[2], None)
            if first[0] is None:
                heads_of.remove(first)

    with ExitStack() as ctx:
        P = Phase(nc, ctx, name)
        cst = P.sb("masks", [128, 12, 128])
        own = P.sb("owner", [128, DEC_B])
        wab = P.sb("w_ab", [128, KC, 8])
        alog, dtb, gn = P.sb("a_log", [128, 4]), P.sb("dt_bias", [128, 4]), P.sb("norm_gain", [128, 1])
        ab, gt = P.sb("ab", [128, 3, 8]), P.sb("g_tmp", [128, 3, 4])
        beta, g = P.sb("beta", [128, 3, 4]), P.sb("g", [128, 3, 4])
        per_tile = lambda name, shape: [P.sb(f"{name}{t}", shape) for t in range(3)]
        gc = per_tile("gc", [128, 5, 4])
        gbc = per_tile("g_wide", [128, 4, 128])
        dec, decT = per_tile("decay", [128, 4, 128]), per_tile("decayT", [128, 4, 128])
        eg = P.sb("exp_gcum", [128, 3, 4, 128])
        L, Lm = per_tile("L", [128, 4, 128]), gbc
        X, XT, P1 = dec, decT, per_tile("P1", [128, 4, 128])
        inT = P.sb("intraT", [128, 3, 4, 128])
        Rv, Rk, kd = per_tile("Rv", [128, 4, 128]), per_tile("Rk", [128, 4, 128]), P.sb("k_decay", [128, 3, 4, 128])
        u, wT, qe = P.sb("u", [128, 3, 4, 128]), P.sb("wT", [128, 3, 4, 128]), P.sb("q_exp", [128, 3, 4, 128])
        S, vn, vs = P.sb("S", [128, 4, 128]), P.sb("v_new", [128, 4, 128]), P.sb("v_new_s", [NS, 4, 128])
        S0 = P.sb("S_sample", [128, DEC_B, 4, 128])
        wS, vm = P.sb("wS", [128, 4, 32]), P.sb("v_owner", [32, DEC_B, 128])
        oT, ones = P.sb("oT", [128, 4, NTOK]), P.sb("ones", [128, 128])
        sqr = P.sb("sqr", [128, 4, NTOK])
        bank = [P.ps(f"bank{i}", [128, 512]) for i in range(8)]
        loaded, dve_steps, act_steps, stored = (P.sem(s) for s in ("loaded", "dve_steps", "act_steps", "stored"))
        turn = {"gates": P.sem("gate_turn"), "main": P.sem("main_turn")}
        turn.update({t: P.sem(f"tile{t}_turn") for t in range(3)})
        heads = [b[:].rearrange("q (h c) -> q h c", h=4) for b in bank]
        ident = K["ident"]
        GM = lambda t, k: cst[:, (3 if t == 2 else 0) + k, :]

        def rows_of(t, k):
            return heads[3 * t + k][0:TILES[t][1], :, :]

        def cols_of(t, k):
            if t < 2:
                return heads[3 * t + k]
            return bank[6 + k % 2][:, k // 2 * 128:k // 2 * 128 + 128].rearrange("q (h c) -> q h c", h=4)

        square = lambda t, k: cols_of(t, k)[0:TILES[t][1]]

        def begin(eng, lane, what):
            if lane == "main" and what == "c0 wS pe":
                eng.wait_ge(turn[0], len(order[0]))
                eng.wait_ge(turn[1], len(order[1]))
            elif lane in (0, 1, 2) and at[lane, what] == 0:
                eng.wait_ge(turn["gates"], len(order["gates"]))
            elif at[lane, what]:
                eng.wait_ge(turn[lane], at[lane, what])

        with nc.Block() as block:
            @block.sync
            def _(sp):
                sp.dma_start(wab[:], T["w_in_ab"][0].rearrange("(k p) n -> p k n", p=128)[:, :, IN_AB - 8:IN_AB]
                             ).then_inc(loaded, 16)
                sp.dma_start(cst[:], T["c_gdn"].rearrange("p (k n) -> p k n", k=12)).then_inc(loaded, 16)
                sp.dma_start(own[:], T["c_owner"]).then_inc(loaded, 16)
                sp.dma_start(alog[:], broadcast_rows(T["a_log"], 4)).then_inc(loaded, 16)
                sp.dma_start(dtb[:], broadcast_rows(T["dt_bias"], 4)).then_inc(loaded, 16)
                sp.dma_start(gn[:], T["gdn_norm_g"].rearrange("a n -> n a")).then_inc(loaded, 16)
                for b in range(DEC_B):
                    sp.dma_start(S0[:, b, :, :], T["state_delta"][0, b].rearrange("h k v -> k h v")
                                 ).then_inc(loaded, 16)
                roll_cache(sp, T, 2, cache_out, range(4))
                sp.wait_ge(turn["main"], at["main", "c3 S dve"] + 1)
                sp.dma_start(T["out_delta_p"][0, 0].rearrange("h k v -> k h v"), S[:]).then_inc(stored, 16)
                sp.wait_ge(turn[2], len(order[2]))
                for b in range(DEC_B):
                    sp.dma_start(T["out_delta_s"][0, b].rearrange("h k v -> k h v"), S0[:, b, :, :]
                                 ).then_inc(stored, 16)
                sp.wait_ge(stored, 16 * (1 + DEC_B))

            @block.tensor
            def _(pe):
                mm = nc.tensor.matmul

                def tile(t):
                    (o, p), done = TILES[t], turn[t]
                    yield at[t, "gsum pe"]
                    begin(pe, t, "gsum pe")
                    g0 = rows_of(t, 0)[:, 0, 0:8]
                    mm(g0[:, 0:4], GM(t, 0)[0:p, 0:p], g[0:p, t, :], start=True, stop=True)
                    mm(g0[:, 4:8], GM(t, 1)[0:p, 0:p], g[0:p, t, :], start=True, stop=True).then_inc(done, 1)
                    yield at[t, "wide pe"]
                    begin(pe, t, "wide pe")
                    for h in range(GH):
                        last = mm(cols_of(t, 1)[:, h, 0:p], gbc[t][0:p, h, :], GM(t, 0)[0:p, 0:p], start=True, stop=True)
                    last.then_inc(done, 1)
                    yield at[t, "cross pe"]
                    begin(pe, t, "cross pe")
                    for h in range(GH):
                        kk, qq = conv[:, 4 + h, o:o + p], conv[:, h, o:o + p]
                        mm(square(t, 0)[:, h, 0:p], kk, kk, start=True, stop=True)
                        last = mm(square(t, 2)[:, h, 0:p], kk, qq, start=True, stop=True)
                    last.then_inc(done, 1)
                    yield at[t, "rows pe"]
                    begin(pe, t, "rows pe")
                    for h in range(GH):
                        nc.tensor.transpose(rows_of(t, 0)[:, h, :], conv[:, 4 + h, o:o + p], ident[:])
                        last = nc.tensor.transpose(rows_of(t, 1)[:, h, :], conv[:, 8 + h, o:o + p], ident[:])
                    last.then_inc(done, 1)
                    for lev in range(levels[t]):
                        yield at[t, f"P {lev} pe"]
                        begin(pe, t, f"P {lev} pe")
                        for h in range(GH):
                            last = mm(square(t, 0)[:, h, 0:p], Lm[t][0:p, h, 0:p], XT[t][0:p, h, 0:p],
                                      start=True, stop=True)
                        last.then_inc(done, 1)
                        yield at[t, f"X {lev} pe"]
                        begin(pe, t, f"X {lev} pe")
                        for h in range(GH):
                            mm(square(t, 1)[:, h, 0:p], P1[t][0:p, h, 0:p], X[t][0:p, h, 0:p], start=True, stop=True)
                            last = mm(square(t, 2)[:, h, 0:p], X[t][0:p, h, 0:p], P1[t][0:p, h, 0:p],
                                      start=True, stop=True)
                        last.then_inc(done, 1)
                    yield at[t, "solve pe"]
                    begin(pe, t, "solve pe")
                    for h in range(GH):
                        mm(rows_of(t, 0)[:, h, :], XT[t][0:p, h, 0:p], Rv[t][0:p, h, :], start=True, stop=True)
                        last = mm(cols_of(t, 1)[:, h, 0:p], Rk[t][0:p, h, :], XT[t][0:p, h, 0:p], start=True, stop=True)
                    last.then_inc(done, 1)
                    if t < 2:
                        return
                    yield at[t, "wS pe"]
                    begin(pe, t, "wS pe")
                    for h in range(GH):
                        for b in range(DEC_B):
                            last = mm(cols_of(t, 0)[:, h, 4 * b:4 * b + 4], S0[:, b, h, :],
                                      wT[:, 2, h, 4 * b:4 * b + 4], start=True, stop=True)
                    last.then_inc(done, 1)
                    yield at[t, "wST pe"]
                    begin(pe, t, "wST pe")
                    for h in range(GH):
                        last = nc.tensor.transpose(rows_of(t, 1)[:, h, :], wS[:, h, :], ident[:])
                    last.then_inc(done, 1)
                    yield at[t, "o pe"]
                    begin(pe, t, "o pe")
                    for h in range(GH):
                        mm(cols_of(t, 0)[:, h, :], vs[:, h, :], inT[0:NS, 2, h, 0:NS], start=True, stop=True)
                        for b in range(DEC_B):
                            last = mm(cols_of(t, 2)[:, h, 4 * b:4 * b + 4], S0[:, b, h, :],
                                      qe[:, 2, h, 4 * b:4 * b + 4], start=True, stop=True)
                    last.then_inc(done, 1)
                    for h in range(GH):
                        yield at[t, f"S {h} pe"]
                        begin(pe, t, f"S {h} pe")
                        for hf in range(2):
                            last = mm(bank[6 + hf][:], kd[0:NS, 2, h, :], vm[:, hf * 4:hf * 4 + 4, :],
                                      start=True, stop=True)
                        last.then_inc(done, 1)

                pe.wait_ge(loaded, 16 * (6 + DEC_B))
                for t, (o, p) in enumerate(TILES):
                    for k in range(KC):
                        last = mm(bank[0][0:p, t * 8:t * 8 + 8], hT[:, k, o:o + p], wab[:, k, :],
                                  start=(k == 0), stop=(k == KC - 1))
                last.then_inc(turn["gates"], 1)
                interleave([tile(t) for t in range(3)])
                done = turn["main"]
                for n in range(4):
                    t, r = n // 2, slice(n % 2 * CHUNK, (n % 2 + 1) * CHUNK)
                    begin(pe, "main", f"c{n} wS pe")
                    for h in range(GH):
                        last = mm(heads[3][r, h, :], wT[:, t, h, r], S[:, h, :], start=True, stop=True)
                    last.then_inc(done, 1)
                    begin(pe, "main", f"c{n} o pe")
                    for h in range(GH):
                        mm(heads[4][:, h, 0:CHUNK], S[:, h, :], qe[:, t, h, r], start=True, stop=False)
                        mm(heads[4][:, h, 0:CHUNK], vn[r, h, :], inT[r, t, h, r], start=False, stop=True)
                        last = mm(heads[5][:, h, :], kd[r, t, h, :], vn[r, h, :], start=True, stop=True)
                    last.then_inc(done, 1)
                begin(pe, "main", "sum pe")
                for h in range(GH):
                    last = mm(bank[h][:, 0:NTOK], ones[:], sqr[:, h, :], start=True, stop=True)
                last.then_inc(done, 1)

            @block.scalar
            def _(act):
                ch = Chain(act, act_steps)
                A = nc.scalar.activation
                begin(act, "gates", "ab act")
                ch.step(A(beta[:], ab[:, :, 0:4], ACT.Sigmoid))
                ch.step(A(alog[:], alog[:], ACT.Exp))
                ch(A(gt[:], gt[:], ACT.Exp, scale=-1.0))
                A(gt[:], gt[:], ACT.Ln, bias=1.0).then_inc(turn["gates"], 1)
                for t, (o, p) in enumerate(TILES):
                    begin(act, t, "exps act")
                    A(dec[t][0:p, :, 0:p], dec[t][0:p, :, 0:p], ACT.Exp, scale=-1.0)
                    A(decT[t][0:p, :, 0:p], decT[t][0:p, :, 0:p], ACT.Exp)
                    A(eg[:, t, :, 0:p], cols_of(t, 1)[:, :, 0:p], ACT.Exp)
                    A(gc[t][0:p, 2:4, :], gc[t][0:p, 2:4, :], ACT.Exp).then_inc(turn[t], 1)
                begin(act, "main", "root act")
                A(sqr[:], sqr[:], ACT.Sqrt)
                A(zT[:, 20:24, :], zT[:, 20:24, :], ACT.Silu).then_inc(turn["main"], 1)

            @block.vector
            def _(dve):
                ch = Chain(dve, dve_steps)
                V = nc.vector
                TT, TS, STT = V.tensor_tensor, V.tensor_scalar, V.scalar_tensor_tensor

                def tile(t):
                    (o, p), done = TILES[t], turn[t]
                    yield at[t, "gsum dve"]
                    begin(dve, t, "gsum dve")
                    ch.step(V.tensor_copy(gc[t][0:p, 0:2, :],
                                          rows_of(t, 0)[:, 0, 0:8].rearrange("q (a h) -> q a h", a=2)))
                    V.tensor_copy(gbc[t][0:p, :, :], over(g[0:p, t, :], 2, 128)).then_inc(done, 1)
                    yield at[t, "args dve"]
                    begin(dve, t, "args dve")
                    ch.settle()
                    wide = square(t, 1)
                    for h in range(GH):
                        ch.step(TS(dec[t][0:p, h, 0:p], wide[:, h, 0:p], gc[t][0:p, 0, h:h + 1], 0.0,
                                   ALU.subtract, ALU.max))
                        ch.step(TS(decT[t][0:p, h, 0:p], wide[:, h, 0:p], gc[t][0:p, 0, h:h + 1], 0.0,
                                   ALU.subtract, ALU.min))
                    ch.step(V.tensor_copy(gc[t][0:p, 2, :], gc[t][0:p, 0, :]))
                    TT(gc[t][0:p, 3, :], gc[t][0:p, 1, :], gc[t][0:p, 0, :], ALU.subtract).then_inc(done, 1)
                    yield at[t, "cross dve"]
                    begin(dve, t, "cross dve")
                    ch.step(TT(gc[t][0:p, 4, :], gc[t][0:p, 2, :], beta[0:p, t, :], ALU.mult))
                    ch.step(TT(qe[:, t, :, 0:p], conv[:, 0:4, o:o + p], eg[:, t, :, 0:p], ALU.mult))
                    ch.step(TT(inT[0:p, t, :, 0:p], square(t, 2)[:, :, 0:p], decT[t][0:p, :, 0:p], ALU.mult))
                    for h in range(GH):
                        ch.step(STT(out=L[t][0:p, h, 0:p], in0=square(t, 0)[:, h, 0:p], scalar=beta[0:p, t, h:h + 1],
                                    in1=dec[t][0:p, h, 0:p], op0=ALU.mult, op1=ALU.mult))
                    ch.settle()
                    ch.step(TT(inT[0:p, t, :, 0:p], inT[0:p, t, :, 0:p], over(GM(t, 0)[0:p, 0:p], 1, 4), ALU.mult))
                    TT(L[t][0:p, :, 0:p], L[t][0:p, :, 0:p], over(GM(t, 2)[0:p, 0:p], 1, 4), ALU.mult).then_inc(done, 1)
                    yield at[t, "rows dve"]
                    begin(dve, t, "rows dve")
                    mask = lambda lev: over(cst[0:p, 6 + lev, 0:p], 1, 4)
                    for h in range(GH):
                        ch.step(TS(Rv[t][0:p, h, :], rows_of(t, 1)[:, h, :], beta[0:p, t, h:h + 1], None, ALU.mult))
                        ch.step(TS(Rk[t][0:p, h, :], rows_of(t, 0)[:, h, :], gc[t][0:p, 4, h:h + 1], None, ALU.mult))
                        ch.step(TS(kd[0:p, t, h, :], rows_of(t, 0)[:, h, :], gc[t][0:p, 3, h:h + 1], None, ALU.mult))
                    ch.settle()
                    ch.step(V.tensor_copy(X[t][0:p, :, 0:p], over(ident[0:p, 0:p], 1, 4)))
                    ch.step(V.tensor_copy(XT[t][0:p, :, 0:p], over(ident[0:p, 0:p], 1, 4)))
                    TT(Lm[t][0:p, :, 0:p], L[t][0:p, :, 0:p], mask(0), ALU.mult).then_inc(done, 1)
                    for lev in range(levels[t]):
                        yield at[t, f"P {lev} dve"]
                        begin(dve, t, f"P {lev} dve")
                        V.tensor_copy(P1[t][0:p, :, 0:p], square(t, 0)[:, :, 0:p]).then_inc(done, 1)
                        yield at[t, f"X {lev} dve"]
                        begin(dve, t, f"X {lev} dve")
                        ch.step(TT(X[t][0:p, :, 0:p], X[t][0:p, :, 0:p], square(t, 1)[:, :, 0:p], ALU.subtract))
                        if lev + 1 < levels[t]:
                            ch.step(TT(Lm[t][0:p, :, 0:p], L[t][0:p, :, 0:p], mask(lev + 1), ALU.mult))
                        TT(XT[t][0:p, :, 0:p], XT[t][0:p, :, 0:p], square(t, 2)[:, :, 0:p], ALU.subtract
                           ).then_inc(done, 1)
                    yield at[t, "solve dve"]
                    begin(dve, t, "solve dve")
                    ch.step(V.tensor_copy(u[0:p, t, :, :], rows_of(t, 0)))
                    V.tensor_copy(wT[:, t, :, 0:p], cols_of(t, 1)[:, :, 0:p]).then_inc(done, 1)
                    if t < 2:
                        return
                    yield at[t, "wS dve"]
                    begin(dve, t, "wS dve")
                    V.tensor_copy(wS[:], cols_of(t, 0)).then_inc(done, 1)
                    yield at[t, "v dve"]
                    begin(dve, t, "v dve")
                    TT(vs[:], u[0:NS, 2, :, :], rows_of(t, 1), ALU.subtract).then_inc(done, 1)
                    yield at[t, "o dve"]
                    begin(dve, t, "o dve")
                    ch(V.tensor_copy(oT[:, :, SEQ:], cols_of(t, 0)))
                    ch.step(TT(oT[:, :, SEQ:], oT[:, :, SEQ:], cols_of(t, 2), ALU.add))
                    for h in range(GH):
                        glast = eg[:, 2, h, 0:NS].rearrange("p (b t) -> p b t", t=DEC_T)[:, :, DEC_T - 1]
                        ch.step(TT(S0[:, :, h, :], S0[:, :, h, :], over(glast, 2, 128), ALU.mult))
                    ch.settle()
                    spread = lambda h: TT(vm[:], over(vs[:, h, :], 1, DEC_B), over(own[0:NS, :], 2, 128), ALU.mult)
                    spread(0).then_inc(done, 1)
                    for h in range(GH):
                        yield at[t, f"S {h} dve"]
                        begin(dve, t, f"S {h} dve")
                        for hf in range(2):
                            d = S0[:, hf * 4:hf * 4 + 4, h, :]
                            last = TT(d, d, heads[6 + hf], ALU.add)
                            if hf == 0 or h + 1 < GH:
                                ch.step(last)
                        (spread(h + 1) if h + 1 < GH else last).then_inc(done, 1)

                ch.step(V.memset(ab[:], 0.0))
                ch.step(V.memset(ones[:], 1.0))
                ch(V.memset(S[:], 0.0))
                begin(dve, "gates", "ab dve")
                for t, (o, p) in enumerate(TILES):
                    ch.step(V.tensor_copy(ab[0:p, t, :], bank[0][0:p, t * 8:t * 8 + 8]))
                ch.settle()
                ch(TT(ab[:, :, 4:8], ab[:, :, 4:8], over(dtb[:], 1, 3), ALU.add))
                ch(TS(gt[:], ab[:, :, 4:8], -1.0, None, ALU.mult))
                TT(gt[:], gt[:], ab[:, :, 4:8], ALU.max).then_inc(turn["gates"], 1)
                begin(dve, "gates", "g dve")
                ch(STT(out=gt[:], in0=ab[:, :, 4:8], scalar=0.0, in1=gt[:], op0=ALU.max, op1=ALU.add))
                STT(out=g[:], in0=gt[:], scalar=-1.0, in1=over(alog[:], 1, 3), op0=ALU.mult,
                    op1=ALU.mult).then_inc(turn["gates"], 1)
                interleave([tile(t) for t in range(3)])
                done = turn["main"]
                for n in range(4):
                    t, r = n // 2, slice(n % 2 * CHUNK, (n % 2 + 1) * CHUNK)
                    begin(dve, "main", f"c{n} v dve")
                    ch.settle()
                    TT(vn[r, :, :], u[r, t, :, :], heads[3][r, :, :], ALU.subtract).then_inc(done, 1)
                    begin(dve, "main", f"c{n} S dve")
                    ch.step(V.tensor_copy(oT[:, :, n * CHUNK:(n + 1) * CHUNK], heads[4][:, :, 0:CHUNK]))
                    for h in range(GH):
                        last = STT(out=S[:, h, :], in0=S[:, h, :], scalar=eg[:, t, h, r.stop - 1:r.stop],
                                   in1=heads[5][:, h, :], op0=ALU.mult, op1=ALU.add)
                    last.then_inc(done, 1)
                begin(dve, "main", "square dve")
                ch.settle()
                TT(sqr[:], oT[:], oT[:], ALU.mult).then_inc(done, 1)
                begin(dve, "main", "root dve")
                for h in range(GH):
                    last = TS(sqr[:, h, :], bank[h][:, 0:NTOK], 1.0 / GD, EPS, ALU.mult, ALU.add)
                last.then_inc(done, 1)
                begin(dve, "main", "out dve")
                ch.step(TS(oT[:], oT[:], gn[:, 0:1], None, ALU.mult))
                ch(V.reciprocal(sqr[:], sqr[:]))
                ch(TT(oT[:], oT[:], sqr[:], ALU.mult))
                TT(mixT[:, 4:8, :], oT[:], zT[:, 20:24, :], ALU.mult).then_inc(done, 1)


RING = 8


def experts_phase(nc, name, K, T, qT, keysT, layer):
    x, h = K["x"], K["h"]
    u_tab, v_tab = (T[n].rearrange("l e d -> (l e) d") for n in ("peer_u", "peer_v"))
    heads = (PH, PH, 2)
    slots = tuple(n * TOPK for n in heads)
    groups = (2, 0, 1)
    place = {g: i for i, g in enumerate(groups)}
    loops = tuple((kind, g) for g in groups for kind in "uv")
    by_dve = lambda g: (3, 7) if g == 1 else ()
    halves = [slots[g] // RING for _, g in loops]
    before = {l: sum(halves[:i]) for i, l in enumerate(loops)}
    diags, n_diag = {}, 0
    for g in groups:
        diags[g] = n_diag
        n_diag += slots[g] // RING * (RING - len(by_dve(g)))
    acts = {g: sum(slots[i] // RING for i in groups[:place[g]]) for g in groups}

    with ExitStack() as ctx:
        P = Phase(nc, ctx, name)
        NH2 = 2 * PH
        iota = P.sb("iota", [128, 16])
        sc = P.sb("scores", [128, NH2, NKEY])
        ts, ti = P.sb("top", [128, NH2, TOPK]), P.sb("top_at", [128, NH2, TOPK], U32)
        tif = P.sb("top_at_f", [128, NH2, TOPK])
        cand, cand2 = P.sb("cand", [128, PH, TOPK * TOPK]), P.sb("cand2", [128, PH, TOPK * TOPK])
        bs, bp = P.sb("best", [128, PH, TOPK]), P.sb("best_at", [128, PH, TOPK], U32)
        be = P.sb("best_exp", [128, 3, PH, TOPK])
        part, partf = P.sb("part", [128, 2, SLOTS], U32), P.sb("part_f", [128, 2, SLOTS])
        hot = P.sb("one_hot", [128, SLOTS, TOPK])
        rowf, total = P.sb("row_f", [128, 2, SLOTS]), P.sb("total", [128, PH])
        idx, gate = P.sb("idx", [128, 3, SLOTS], U32), P.sb("gate", [128, 3, SLOTS])
        h_s = P.sb("h_s", [128, D])
        ring, cur = P.sb("ring", [128, RING, D]), P.sb("cur_idx", [128, 2, RING], U32)
        dots, weights = P.sb("dots", [128, 3, SLOTS]), P.sb("weights", [128, 3, SLOTS])
        dot_blk, w_blk = P.sb("dot_block", [128, 2, RING]), P.sb("weight_block", [128, 2, RING])
        diag, zero, four = P.sb("diag", [128, RING, 128]), P.sb("zero", [128, 128]), P.sb("four", [128, 32])
        side = P.sb("dve_sum", [128, D])
        ps = [P.ps("scores_p", [128, NH2 * NKEY]), P.ps("scores_s", [128, 1024])]
        acc = P.ps("acc", [128, D])
        landed = [P.sem(f"landed{r}") for r in range(RING)]
        freed = [P.sem(f"freed{r}") for r in range(RING)]
        consts_in, dve_steps, score_ready, exp_ready, gelu_ready, idx_copied, issued = (
            P.sem(n) for n in ("consts_in", "dve_steps", "score_ready", "exp_ready", "gelu_ready", "idx_copied",
                               "issued"))
        blk_ready, w_ready, diag_ready, acc_done, side_steps = (
            P.sem(n) for n in ("blk_ready", "w_ready", "diag_ready", "acc_done", "side_steps"))
        hid = lambda g: h[:, g, :] if g < 2 else h_s[:]
        def score(g, n):
            c = (n % 2 * PH + n // 2) * NKEY if g < 2 else n % 2 * 512 + n // 2 * NKEY
            return ps[g // 2][:, c:c + NKEY]
        mark = {}

        with nc.Block() as block:
            @block.vector
            def _(dve):
                ch = Chain(dve, dve_steps)
                V = nc.vector

                def search(g):
                    nh = heads[g]
                    n2, sl = 2 * nh, nh * TOPK
                    dve.wait_ge(score_ready, place[g] + 1)
                    for n in range(n2):
                        ch.step(V.max(ts[:, n, 0:8], score(g, n)))
                    for n in range(n2):
                        ch.settle(lag=n2 - 1)
                        ch.step(V.match_replace(sc[:, n, :], ts[:, n, 0:8], score(g, n), NEG))
                    for n in range(n2):
                        ch.settle(lag=n2 - 1)
                        ch.step(V.max(ts[:, n, 8:16], sc[:, n, :]))
                    for n in range(n2):
                        ch.step(V.max_index(ti[:, n, 0:8], ts[:, n, 0:8], score(g, n)))
                    mark["scores", g] = ch.n
                    for n in range(n2):
                        ch.settle(lag=2 * n2 - 1)
                        ch.step(V.max_index(ti[:, n, 8:16], ts[:, n, 8:16], sc[:, n, :]))
                    ch.settle()
                    ch.step(V.tensor_copy(tif[:, 0:n2], ti[:, 0:n2]))
                    for i in range(nh):
                        ch.step(V.tensor_tensor(cand[:, i, :].rearrange("q (a b) -> q a b", a=TOPK),
                                                over(ts[:, 2 * i, :], 2, TOPK), over(ts[:, 2 * i + 1, :], 1, TOPK),
                                                ALU.add))
                    for i in range(nh):
                        ch.settle(lag=nh - 1)
                        ch.step(V.max(bs[:, i, 0:8], cand[:, i, :]))
                    for i in range(nh):
                        ch.settle(lag=nh - 1)
                        ch.step(V.match_replace(cand2[:, i, :], bs[:, i, 0:8], cand[:, i, :], NEG))
                    for i in range(nh):
                        ch.settle(lag=nh - 1)
                        ch.step(V.max(bs[:, i, 8:16], cand2[:, i, :]))
                    for i in range(nh):
                        ch.step(V.max_index(bp[:, i, 0:8], bs[:, i, 0:8], cand[:, i, :]))
                    for i in range(nh):
                        ch.settle(lag=2 * nh - 1)
                        ch.step(V.max_index(bp[:, i, 8:16], bs[:, i, 8:16], cand2[:, i, :]))
                    ch.settle()
                    ch(V.tensor_tensor(be[:, g, 0:nh], bs[:, 0:nh], over(bs[:, 0:nh, 0], 2, TOPK), ALU.subtract))
                    mark["exp", g] = ch.n
                    bpv = bp[:, 0:nh].rearrange("q h k -> q (h k)")
                    ch.step(V.tensor_scalar(part[:, 0, 0:sl], bpv, 4, None, ALU.logical_shift_right))
                    ch(V.tensor_scalar(part[:, 1, 0:sl], bpv, 15, None, ALU.bitwise_and))
                    ch(V.tensor_copy(partf[:, :, 0:sl], part[:, :, 0:sl]))
                    for half in range(2):
                        hv = hot[:, 0:sl, :]
                        ch(V.tensor_tensor(hv, over(partf[:, half, 0:sl], 2, TOPK), over(iota[:, :], 1, sl),
                                           ALU.is_equal))
                        for i in range(nh):
                            hs = hot[:, i * TOPK:(i + 1) * TOPK, :]
                            ch.step(V.tensor_tensor(hs, hs, over(tif[:, 2 * i + half, :], 1, TOPK), ALU.mult))
                        ch.settle()
                        ch(V.tensor_reduce(rowf[:, half, 0:sl], hv, AX_X, ALU.add))
                    ch(V.tensor_scalar(rowf[:, 0, 0:sl], rowf[:, 0, 0:sl], float(NKEY), float(layer * NKEY * NKEY),
                                       ALU.mult, ALU.add))
                    ch(V.tensor_tensor(idx[:, g, 0:sl], rowf[:, 0, 0:sl], rowf[:, 1, 0:sl], ALU.add))
                    mark["idx", g] = ch.n

                def gates(g):
                    nh = heads[g]
                    dve.wait_ge(exp_ready, place[g] + 1)
                    ch(V.tensor_reduce(total[:, 0:nh], be[:, g, 0:nh], AX_X, ALU.add))
                    ch(V.reciprocal(total[:, 0:nh], total[:, 0:nh]))
                    ch(V.tensor_tensor(gate[:, g, 0:slots[g]].rearrange("q (h k) -> q h k", h=nh), be[:, g, 0:nh],
                                       over(total[:, 0:nh], 2, TOPK), ALU.mult))
                    dve.wait_ge(gelu_ready, place[g] + 1)
                    ch(V.tensor_tensor(weights[:, g, 0:slots[g]], weights[:, g, 0:slots[g]], gate[:, g, 0:slots[g]],
                                       ALU.mult))
                    mark["weights", g] = ch.n

                def dot_products(g):
                    k0 = before["u", g]
                    with dve.Fori(0, slots[g] // (2 * RING)) as i:
                        for hf in range(2):
                            for r in range(RING):
                                dve.wait_ge(landed[r], (i * 2 + (k0 + hf + 1)) * 16)
                                V.tensor_tensor_reduce(out=ring[:, r, :], in0=ring[:, r, :], in1=hid(g), scale=1.0,
                                                       scalar=0.0, op0=ALU.mult, op1=ALU.add,
                                                       accum_out=dot_blk[:, hf, r:r + 1]).then_inc(freed[r], 1)
                            dve.wait_ge(freed[RING - 1], i * 2 + (k0 + hf + 2))
                            V.tensor_copy(dots[:, g, bass.ds(i * (2 * RING) + hf * RING, RING)],
                                          dot_blk[:, hf, :]).then_inc(blk_ready, 1)

                def own_sums(g):
                    k0, mine = before["v", g], by_dve(g)
                    sd = side[:]
                    with dve.Fori(0, slots[g] // (2 * RING)) as i:
                        for hf in range(2):
                            for j, r in enumerate(mine):
                                dve.wait_ge(landed[r], (i * 2 + (k0 + hf + 1)) * 16)
                                dve.wait_ge(w_ready, i * 2 + (acts[g] + hf + 1))
                                dve.wait_ge(side_steps, i * (2 * len(mine)) + (hf * len(mine) + j + 1))
                                V.scalar_tensor_tensor(out=sd, in0=ring[:, r, :], scalar=w_blk[:, hf, r:r + 1],
                                                       in1=sd, op0=ALU.mult, op1=ALU.add).then_inc(side_steps, 1)
                                dve.wait_ge(side_steps, i * (2 * len(mine)) + (hf * len(mine) + j + 2))
                                dve.sem_inc(freed[r], 1)

                def add_group(g):
                    o, p = TILES[g]
                    dve.wait_ge(acc_done, place[g] + 1)
                    ch(V.tensor_tensor(x[0:p, g, :], x[0:p, g, :], acc[0:p, :], ALU.add))
                    mark["added", g] = ch.n

                ch.step(V.memset(zero[:], 0.0))
                V.memset(side[:], 0.0).then_inc(side_steps, 1)
                for r in range(RING):
                    dve.sem_inc(freed[r], 1)
                dve.wait_ge(consts_in, 16 * 6)
                search(2)
                dot_products(2)
                gates(2)
                search(0)
                add_group(2)
                dot_products(0)
                gates(0)
                search(1)
                add_group(0)
                dot_products(1)
                gates(1)
                own_sums(1)
                add_group(1)

            @block.scalar
            def _(act):
                A = nc.scalar.activation

                def exps(g):
                    act.wait_ge(dve_steps, mark["exp", g])
                    A(be[:, g, 0:heads[g]], be[:, g, 0:heads[g]], ACT.Exp).then_inc(exp_ready, 1)

                def gelu(g):
                    act.wait_ge(blk_ready, acts[g] + slots[g] // RING)
                    A(weights[:, g, 0:slots[g]], dots[:, g, 0:slots[g]], ACT.Gelu).then_inc(gelu_ready, 1)

                def diagonals(g):
                    idn, w = (K["ident"], 128) if g < 2 else (four, 32)
                    act.wait_ge(dve_steps, mark["weights", g])
                    with act.Fori(0, slots[g] // (2 * RING)) as i:
                        for hf in range(2):
                            k = before["v", g] + hf
                            A(w_blk[:, hf, :], weights[:, g, bass.ds(i * (2 * RING) + hf * RING, RING)], ACT.Copy
                              ).then_inc(w_ready, 1)
                            act.wait_ge(w_ready, i * 2 + (acts[g] + hf + 1))
                            for r in range(RING):
                                act.wait_ge(freed[r], i * 2 + (k + 1))
                                if r not in by_dve(g):
                                    A(diag[:, r, 0:w], idn[:, 0:w], ACT.Copy, scale=w_blk[:, hf, r:r + 1]
                                      ).then_inc(diag_ready, 1)

                act.wait_ge(consts_in, 16 * 6)
                for g in groups:
                    exps(g)
                    gelu(g)
                    diagonals(g)

            @block.tensor
            def _(pe):
                def scores(g):
                    o, p = TILES[g]
                    for n in range(2 * PH):
                        r = slice(n % 2 * 64, n % 2 * 64 + 64)
                        q, m = (slice(0, 128), n) if g < 2 else (slice(n // 4 * 32, n // 4 * 32 + 32), n % 4)
                        last = nc.tensor.matmul(score(g, m)[q, :], qT[r, n // 2, o:o + p], keysT[r, n // 2, :],
                                                start=True, stop=True)
                    last.then_inc(score_ready, 1)

                def weighted_sum(g):
                    w = 128 if g < 2 else 32
                    mine = [r for r in range(RING) if r not in by_dve(g)]
                    if place[g]:
                        pe.wait_ge(dve_steps, mark["added", groups[place[g] - 1]])
                    for c in range(2):
                        nc.tensor.matmul(acc[0:w, c * 512:(c + 1) * 512], zero[:, 0:w],
                                         h[:, 0, c * 512:(c + 1) * 512], start=True, stop=False)
                    with pe.Fori(0, slots[g] // (2 * RING)) as i:
                        for hf in range(2):
                            k = before["v", g] + hf
                            for j, r in enumerate(mine):
                                pe.wait_ge(landed[r], (i * 2 + (k + 1)) * 16)
                                pe.wait_ge(diag_ready, i * (2 * len(mine)) + (diags[g] + hf * len(mine) + j + 1))
                                for c in range(2):
                                    last = nc.tensor.matmul(acc[0:w, c * 512:(c + 1) * 512], diag[:, r, 0:w],
                                                            ring[:, r, c * 512:(c + 1) * 512], start=False, stop=False)
                                last.then_inc(freed[r], 1)
                    if by_dve(g):
                        pe.wait_ge(side_steps, 1 + slots[g] // RING * len(by_dve(g)))
                    one, rhs = (K["ident"][:], side[:]) if by_dve(g) else (zero[:, 0:w], h[:, 0, :])
                    for c in range(2):
                        last = nc.tensor.matmul(acc[0:w, c * 512:(c + 1) * 512], one, rhs[:, c * 512:(c + 1) * 512],
                                                start=False, stop=True)
                    last.then_inc(acc_done, 1)

                scores(2)
                scores(0)
                pe.wait_ge(dve_steps, 1)
                weighted_sum(2)
                pe.wait_ge(dve_steps, mark["scores", 0])
                scores(1)
                weighted_sum(0)
                weighted_sum(1)

            @block.sync
            def _(sp):
                sp.dma_start(iota[:], T["c_iota"]).then_inc(consts_in, 16)
                sp.dma_start(four[:], T["c_four"]).then_inc(consts_in, 16)
                for q in range(4):
                    sp.dma_start(h_s[32 * q:32 * q + 32, :], h[0:NS, 2, :]).then_inc(consts_in, 16)

            @block.gpsimd
            def _(pool):
                for kind, g in loops:
                    k0 = before[kind, g]
                    if kind == "u":
                        pool.wait_ge(dve_steps, mark["idx", g])
                    with pool.Fori(0, slots[g] // (2 * RING)) as i:
                        for hf in range(2):
                            nc.gpsimd.tensor_copy(cur[:, hf, :], idx[:, g, bass.ds(i * (2 * RING) + hf * RING, RING)]
                                                  ).then_inc(idx_copied, 1)
                            pool.wait_ge(idx_copied, i * 2 + (k0 + hf + 1))
                            for r in range(RING):
                                pool.wait_ge(freed[r], i * 2 + (k0 + hf + 1))
                                pool.sem_inc(issued, 1)
                                pool.indirect_dma_start(ring[:, r, :], None, u_tab if kind == "u" else v_tab,
                                                        bass.IndirectOffsetOnAxis(ap=cur[:, hf, r:r + 1], axis=0)
                                                        ).then_inc(landed[r], 16)


def ple_inputs(P, T, layer):
    pr, wp = P.sb("p_rows", [128, 3, PLE]), P.sb("w_proj", [128, 2, D])
    p_in, wp_in = P.sem("p_in"), P.sem("wp_in")
    W = WeightRing(P, T["ple_gate"][layer], D, 2)
    start = [(pr[:, 0:2, :], T["p_prompt"][layer, 0].rearrange("(t p) d -> p t d", p=128), p_in),
             (pr[0:NS, 2, :], T["p_sample"][layer].rearrange("b t d -> (b t) d"), p_in),
             (wp[:], T["ple_proj"][layer].rearrange("(k p) n -> p k n", p=128), wp_in)]
    return {"pr": pr, "wp": wp, "p_in": p_in, "wp_in": wp_in, "W": W, "start": start + W.start}


def ple_phase(nc, name, K, I):
    x, hT = K["x"], K["hT"]
    with ExitStack() as ctx:
        P = Phase(nc, ctx, name)
        pr, wp, p_in, wp_in = (I[n] for n in ("pr", "wp", "p_in", "wp_in"))
        wg, wg_in = I["W"].sb, I["W"].landed
        pT = P.sb("pT", [128, 2, NTOK])
        sg = P.sb("gate", [128, 2, 512])
        pt = P.ps("pt", [128, 512])
        acc = [P.ps(f"acc{b}", [128, 2, 512]) for b in range(2)]
        pt_ready, pT_ready, acc_ready, gate_ready, acc_free, dve_steps = (
            P.sem(s) for s in ("pt_ready", "pT_ready", "acc_ready", "gate_ready", "acc_free", "dve_steps"))
        jobs = [(c, t) for c in range(2) for t in range(3)]
        with nc.Block() as block:
            @block.tensor
            def _(pe):
                pe.wait_ge(p_in, 32)
                for t, (o, p) in enumerate(TILES):
                    if t:
                        pe.wait_ge(pT_ready, t)
                    for k in range(2):
                        last = nc.tensor.transpose(pt[:, k * 128:k * 128 + p], pr[0:p, t, k * 128:(k + 1) * 128],
                                                   K["ident"][0:p, 0:p])
                    last.then_inc(pt_ready, 1)
                pe.wait_ge(pT_ready, 3)
                pe.wait_ge(wp_in, 16)
                for n, (c, t) in enumerate(jobs):
                    o, p = TILES[t]
                    if t == 0:
                        pe.wait_ge(wg_in[c], 16)
                    if n >= 2:
                        pe.wait_ge(acc_free, n - 1)
                    for k in range(KC):
                        nc.tensor.matmul(acc[n % 2][0:p, 0, :], hT[:, k, o:o + p], wg[:, c, k, :],
                                         start=(k == 0), stop=(k == KC - 1))
                    for k in range(2):
                        last = nc.tensor.matmul(acc[n % 2][0:p, 1, :], pT[:, k, o:o + p],
                                                wp[:, k, c * 512:(c + 1) * 512], start=(k == 0), stop=(k == 1))
                    last.then_inc(acc_ready, 1)

            @block.scalar
            def _(act):
                for t, (o, p) in enumerate(TILES):
                    act.wait_ge(pt_ready, t + 1)
                    nc.scalar.activation(pT[:, :, o:o + p], pt[:, 0:256].rearrange("q (k c) -> q k c", k=2)[:, :, 0:p],
                                         ACT.Copy).then_inc(pT_ready, 1)
                for n, (c, t) in enumerate(jobs):
                    p = TILES[t][1]
                    act.wait_ge(acc_ready, n + 1)
                    if n >= 2:
                        act.wait_ge(acc_free, n - 1)
                    nc.scalar.activation(sg[0:p, n % 2, :], acc[n % 2][0:p, 0, :], ACT.Sigmoid).then_inc(gate_ready, 1)

            @block.vector
            def _(dve):
                ch = Chain(dve, dve_steps)
                for n, (c, t) in enumerate(jobs):
                    p = TILES[t][1]
                    dve.wait_ge(gate_ready, n + 1)
                    ch(nc.vector.tensor_tensor(sg[0:p, n % 2, :], sg[0:p, n % 2, :], acc[n % 2][0:p, 1, :], ALU.mult))
                    xs = x[0:p, t, c * 512:(c + 1) * 512]
                    nc.vector.tensor_tensor(xs, xs, sg[0:p, n % 2, :], ALU.add).then_inc(acc_free, 1)


def tail(nc, K, T, layer, phases=99, stop=99):
    h, hT = K["h"], K["hT"]
    with ExitStack() as ctx:
        P = Phase(nc, ctx, f"peer{layer}")
        qT, keysT = P.sb("qT", [128, PH, NTOK]), P.sb("keysT", [128, PH, NKEY])
        with ExitStack() as c2:
            W = WeightRing(Phase(nc, c2, f"wq_ring{layer}"), T["peer_wq"][layer], D, 2)
            norm_phase(nc, f"nf{layer}", K, T["norm_ffn"][layer:layer + 1, :], h, hT, ahead=W.start,
                       keys=(T["peer_keys"][layer], keysT))
            columns_phase(nc, f"wq{layer}", hT, T["peer_wq"][layer], D, qT, ahead=W)
        experts_phase(nc, f"exp{layer}", K, T, qT, keysT, layer)
    if phases == stop: return
    with ExitStack() as ctx:
        P = Phase(nc, ctx, f"ple_in{layer}")
        I = ple_inputs(P, T, layer)
        norm_phase(nc, f"np{layer}", K, T["norm_ple"][layer:layer + 1, :], h, hT, ahead=I["start"])
        ple_phase(nc, f"ple{layer}", K, I)


def qkv_phase(nc, name, K, T, W, qP, kP, vP, qS, kS, vS, cache_out):
    hT = K["hT"]
    wt, w_in, WR = W.sb, W.landed, W.slots
    chunks = len(W.chunks)
    jobs = [(c, t) for c in range(chunks) for t in range(3)]
    turned = [n for n, (c, t) in enumerate(jobs) if c < 12]

    def k_stores(slot, n):
        kept = lambda c, t: t == 2 or TILES[t][0] >= SEQ - min(PATTERNS[c % 6 // 2][0], SEQ)
        return sum(1 for m in turned[:n] if m % 4 == slot and jobs[m][0] >= 6 and kept(*jobs[m]))

    with ExitStack() as ctx:
        P = Phase(nc, ctx, name)
        rope = P.sb("rope", [128, 3, 2, ROT])
        rows = P.sb("rows", [128, 4, 4, HD])
        r1, r2 = P.sb("r1", [128, 2, 4, ROT]), P.sb("r2", [128, 2, 4, ROT])
        acc = [P.ps(f"acc{b}", [128, 512]) for b in range(4)]
        pt = [P.ps(f"pt{b}", [128, 512]) for b in range(4)]
        rope_in, product_ready, copied, dve_steps, roped, turned_ready, turned_out, stored = (
            P.sem(s) for s in ("rope_in", "product_ready", "copied", "dve_steps", "roped", "turned_ready",
                               "turned_out", "stored"))
        slot_stored = [P.sem(f"slot_stored{i}") for i in range(4)]
        with nc.Block() as block:
            @block.sync
            def _(sp):
                sp.dma_start(rope[:], T["c_rope"].rearrange("p (t a r) -> p t a r", t=3, a=2)).then_inc(rope_in, 16)
                for c in range(WR, chunks):
                    sp.wait_ge(product_ready, 3 * (c - WR + 1))
                    to, frm, landed = W.load(c)
                    sp.dma_start(to, frm).then_inc(landed, 16)

            @block.gpsimd
            def _(pool):
                n_out = 0
                for n, (c, t) in enumerate(jobs):
                    kind, gi, half = c // 6, c % 6 // 2, c % 2
                    if kind == 0:
                        continue
                    o, p = TILES[t]
                    if kind == 1:
                        pool.wait_ge(roped, turned.index(n) + 1)
                        src = rows[0:p, turned.index(n) % 4, :, :]
                    else:
                        pool.wait_ge(copied, n + 1)
                        src = (vP[:, t] if t < 2 else vS[:])[:, gi, half * 4:half * 4 + 4, :]
                    hs = slice(half * 4, half * 4 + 4)
                    keep = min(PATTERNS[gi][0], SEQ)
                    done = slot_stored[turned.index(n) % 4] if kind == 1 else stored
                    if t < 2:
                        if o >= SEQ - keep:
                            pool.dma_start(T[f"out_kv{gi}_p"][0, 0, o - SEQ + keep:o - SEQ + keep + 128, kind - 1, hs, :],
                                           src).then_inc(done, 16)
                            n_out += kind == 2
                    else:
                        full = T[f"out_kv{gi}_s"].shape[2]
                        pool.dma_start(T[f"out_kv{gi}_s"][0, :, full - DEC_T:full, kind - 1, hs, :], src).then_inc(
                            done, 16)
                        n_out += kind == 2
                pool.wait_ge(stored, 16 * n_out)
                for i in range(4):
                    pool.wait_ge(slot_stored[i], 16 * k_stores(i, len(turned)))

            @block.tensor
            def _(pe):
                def turn(m):
                    n = turned[m]
                    o, p = TILES[jobs[n][1]]
                    pe.wait_ge(roped, m + 1)
                    if m >= 4:
                        pe.wait_ge(turned_out, m - 3)
                    for h in range(4):
                        last = nc.tensor.transpose(pt[m % 4][:, h * 128:h * 128 + p], rows[0:p, m % 4, h, :],
                                                   K["ident"][0:p, 0:p])
                    last.then_inc(turned_ready, 1)

                for n, (c, t) in enumerate(jobs):
                    o, p = TILES[t]
                    if t == 0:
                        pe.wait_ge(w_in[c % WR], 16 * (c // WR + 1))
                    if n >= 4:
                        pe.wait_ge(copied, n - 3)
                        if n - 4 < len(turned):
                            pe.wait_ge(roped, n - 3)
                    for k in range(KC):
                        last = nc.tensor.matmul(acc[n % 4][0:p, :], hT[:, k, o:o + p], wt[:, c % WR, k, :],
                                                start=(k == 0), stop=(k == KC - 1))
                    last.then_inc(product_ready, 1)
                    if 2 <= n < len(turned) + 2:
                        turn(n - 2)

            @block.scalar
            def _(act):
                for n, (c, t) in enumerate(jobs):
                    p = TILES[t][1]
                    act.wait_ge(product_ready, n + 1)
                    if t == 0 and c in (1, 5, 9, 13):
                        roll_cache(act, T, 2, cache_out, (4 + c // 4,))
                    gi, half = c % 6 // 2, c % 2
                    if c < 12:
                        if n >= 4:
                            act.wait_ge(turned_ready, n - 3)
                            if k_stores(n % 4, n):
                                act.wait_ge(slot_stored[n % 4], 16 * k_stores(n % 4, n))
                        dst = rows[0:p, n % 4, :, :]
                    else:
                        dst = (vP[:, t] if t < 2 else vS[:])[:, gi, half * 4:half * 4 + 4, :]
                    nc.scalar.activation(dst, acc[n % 4][0:p, :].rearrange("q (h e) -> q h e", h=4), ACT.Copy
                                         ).then_inc(copied, 1)
                    if 3 <= n < len(turned) + 3:
                        m = n - 3
                        cm, tm = jobs[turned[m]]
                        om, pm = TILES[tm]
                        dstT = (qP if cm < 6 else kP) if tm < 2 else (qS if cm < 6 else kS)
                        om = om % SEQ
                        h0 = cm % 6 * 4
                        act.wait_ge(turned_ready, m + 1)
                        nc.scalar.activation(dstT[:, h0:h0 + 4, om:om + pm],
                                             pt[m % 4][:].rearrange("q (h c) -> q h c", h=4)[:, :, 0:pm], ACT.Copy
                                             ).then_inc(turned_out, 1)

            @block.vector
            def _(dve):
                ch = Chain(dve, dve_steps)
                V = nc.vector
                dve.wait_ge(rope_in, 16)
                HR = ROT // 2
                for m, n in enumerate(turned):
                    c, t = jobs[n]
                    p = TILES[t][1]
                    a4 = acc[n % 4][0:p, :].rearrange("q (h e) -> q h e", h=4)
                    dve.wait_ge(copied, n + 1)
                    a, b = r1[0:p, m % 2], r2[0:p, m % 2]
                    ch.step(V.tensor_tensor(a, a4[:, :, 0:ROT], over(rope[0:p, t, 0, :], 1, 4), ALU.mult))
                    ch.step(V.tensor_tensor(b[:, :, 0:HR], a4[:, :, HR:ROT], over(rope[0:p, t, 1, 0:HR], 1, 4), ALU.mult))
                    ch(V.tensor_tensor(b[:, :, HR:], a4[:, :, 0:HR], over(rope[0:p, t, 1, HR:], 1, 4), ALU.mult))
                    V.tensor_tensor(rows[0:p, m % 4, :, 0:ROT], a, b, ALU.add).then_inc(roped, 1)


def prompt_attention_phase(nc, name, K, T, qT, kT, v, mixT, k_first, k_first_in):
    units = [(h, it) for it in range(2) for h in range(CH)]
    with ExitStack() as ctx:
        P = Phase(nc, ctx, name)
        band = P.sb("band", [128, 2, NG, SEQ])
        s, pT = P.sb("s", [128, 3, NG, SEQ]), P.sb("pT", [128, 2, NG * 2, 128])
        st = P.sb("stats", [128, 3, 4])
        ps = [P.ps(f"scores{b}", [128, 1024]) for b in range(2)]
        pp = P.ps("turned", [128, 1024])
        po = [P.ps(f"out{b}", [128, 512]) for b in range(2)]
        band_in, score_ready, dve_steps, max_ready, exp_ready, norm_ready, turned, copied, out_ready, out_done = (
            P.sem(x) for x in ("band_in", "score_ready", "dve_steps", "max_ready", "exp_ready", "norm_ready",
                               "turned", "copied", "out_ready", "out_done"))
        with nc.Block() as block:
            @block.sync
            def _(sp):
                sp.dma_start(band[:], T["c_band"].rearrange("p (t g n) -> p t g n", t=2, g=NG)).then_inc(band_in, 16)
                for to, frm in key_tiles(T, k_first[:], 0, 0):
                    sp.dma_start(to, frm).then_inc(k_first_in, 16)

            @block.tensor
            def _(pe):
                def scores(n):
                    h, it = units[n]
                    if n >= 2:
                        pe.wait_ge(max_ready, n - 1)
                    for gi in range(NG):
                        last = nc.tensor.matmul(ps[n % 2][:, gi * SEQ:gi * SEQ + 128 * (it + 1)],
                                                qT[:, gi * CH + h, it * 128:(it + 1) * 128],
                                                kT[:, gi * CH + h, 0:128 * (it + 1)], start=True, stop=True)
                    last.then_inc(score_ready, 1)

                scores(0)
                scores(1)
                for n, (h, it) in enumerate(units):
                    if n + 2 < len(units):
                        scores(n + 2)
                    pe.wait_ge(norm_ready, n + 1)
                    if n:
                        pe.wait_ge(copied, n)
                    for gi in range(NG):
                        for jt in range(it + 1):
                            last = nc.tensor.transpose(pp[:, (gi * 2 + jt) * 128:(gi * 2 + jt + 1) * 128],
                                                       s[:, n % 3, gi, jt * 128:(jt + 1) * 128], K["ident"][:])
                    last.then_inc(turned, 1)
                    pe.wait_ge(copied, n + 1)
                    if n >= 2:
                        pe.wait_ge(out_done, n - 1)
                    parts = [(gi, jt) for gi in range(NG) for jt in range(it + 1)]
                    for m, (gi, jt) in enumerate(parts):
                        last = nc.tensor.matmul(po[n % 2][:, 0:128], v[:, jt, gi, h, :], pT[:, n % 2, gi * 2 + jt, :],
                                                start=(m == 0), stop=(m == len(parts) - 1))
                    last.then_inc(out_ready, 1)

            @block.vector
            def _(dve):
                ch = Chain(dve, dve_steps)
                V = nc.vector
                dve.wait_ge(band_in, 16)

                def maximum(n):
                    it = units[n][1]
                    w = 128 * (it + 1)
                    sv = s[:, n % 3, :, 0:w]
                    dve.wait_ge(score_ready, n + 1)
                    if n >= 3:
                        dve.wait_ge(turned, n - 2)
                    ch(V.scalar_tensor_tensor(out=sv, in0=ps[n % 2][:, 0:NG * SEQ].rearrange("p (g n) -> p g n", g=NG)[:, :, 0:w],
                                              scalar=ATT_SCALE, in1=band[:, it, :, 0:w], op0=ALU.mult, op1=ALU.add))
                    ch(V.tensor_reduce(st[:, n % 3, 0:1], sv, mybir.AxisListType.XY, ALU.max))
                    V.tensor_scalar(st[:, n % 3, 1:2], st[:, n % 3, 0:1], -1.0, None, ALU.mult).then_inc(max_ready, 1)

                maximum(0)
                for n, (h, it) in enumerate(units):
                    if n + 1 < len(units):
                        maximum(n + 1)
                    sv = s[:, n % 3, :, 0:128 * (it + 1)]
                    dve.wait_ge(exp_ready, n + 1)
                    ch(V.reciprocal(st[:, n % 3, 3:4], st[:, n % 3, 2:3]))
                    V.tensor_scalar(sv, sv, st[:, n % 3, 3:4], None, ALU.mult).then_inc(norm_ready, 1)

            @block.scalar
            def _(act):
                def exps(n):
                    sv = s[:, n % 3, :, 0:128 * (units[n][1] + 1)]
                    act.wait_ge(max_ready, n + 1)
                    nc.scalar.activation(sv, sv, ACT.Exp, bias=st[:, n % 3, 1:2], accum_out=st[:, n % 3, 2:3]
                                         ).then_inc(exp_ready, 1)

                exps(0)
                for n, (h, it) in enumerate(units):
                    if n + 1 < len(units):
                        exps(n + 1)
                    act.wait_ge(turned, n + 1)
                    src = pp[:, 0:NG * 256].rearrange("p (g j n) -> p g j n", g=NG, j=2)[:, :, 0:it + 1, :]
                    if n >= 2:
                        act.wait_ge(out_ready, n - 1)
                    nc.scalar.activation(pT[:, n % 2].rearrange("p (g j) n -> p g j n", j=2)[:, :, 0:it + 1, :], src,
                                         ACT.Copy).then_inc(copied, 1)
                    act.wait_ge(out_ready, n + 1)
                    nc.scalar.activation(mixT[:, h, it * 128:(it + 1) * 128], po[n % 2][:, 0:128], ACT.Copy
                                         ).then_inc(out_done, 1)


KT = 7
LOADS = 1 + 2 * DEC_T


def key_tiles(T, dst, b, kv):
    caches = [T["cache_kv_w128"][0], T["cache_kv_w512"][0], T["cache_kv_w2048"][0]]
    c0, c1, c2 = (c[b, :, kv, :, :].rearrange("r h e -> r (h e)") for c in caches)
    c1 = c1.rearrange("(m j t) c -> t m j c", j=4, t=PATTERNS[1][1])
    c2 = c2.rearrange("(m j t) c -> t m j c", j=2, t=PATTERNS[2][1])
    out = [(dst[:, 0, :], c0)]
    for t in range(DEC_T):
        rows = slice(32 * t, 32 * t + 32)
        out += [(dst[rows, 1:5, :], c1[t]), (dst[rows, 5:7, :], c2[t])]
    return out


def sample_attention_phase(nc, name, K, T, qS, kS, vS, mixT, k_first, k_first_in):
    NB, NT = 4, KT + 1
    WID = KT * 128 + NG * NS
    h, hT = K["h"], K["hT"]
    q_rows, out_rows = h[0:NS, 0:2, :], h[:, 2, :]
    flat = hT[:].rearrange("p k n -> p (k n)")
    v_new, spread = flat[0:NG * NS, 0:D], flat[0:NS, D:2 * D]

    with ExitStack() as ctx:
        P = Phase(nc, ctx, name)
        kc, vc = [k_first, P.sb("k_rows", [128, KT, D])], P.sb("v_rows", [128, 2, KT, D])
        kTc = P.sb("k_cols", [128, 2, 512])
        mask = P.sb("mask", [128, 2, WID])
        sT, s = P.sb("sT", [128, 2, NT, 128]), P.sb("s", [128, WID])
        dots = P.sb("dots", [128, 2, 6, CH])
        pT, st = P.sb("pT", [128, NT, 128]), P.sb("stats", [128, 4])
        p_q = [P.ps(f"q_spread{g}", [128, 1024]) for g in range(2)]
        p_w = P.ps("wide", [128, 1024])
        p_row = [p_w, p_q[0]]
        p_kt, p_sc = P.ps("keys", [128, 512]), P.ps("scores", [128, 512])
        const_in, qrow_ready, q_ready, keys_ready, keys_copied, col_ready, col_copied, dots_copied = (
            P.sem(x) for x in ("const_in", "qrow_ready", "q_ready", "keys_ready", "keys_copied", "col_ready",
                               "col_copied", "dots_copied"))
        k_in, v_in = [k_first_in, P.sem("k_in1")], [P.sem(f"v_in{i}") for i in range(2)]
        vnew_in, new_ready, new_copied, row_ready, dve_steps, exp_ready = (
            P.sem(x) for x in ("vnew_in", "new_ready", "new_copied", "row_ready", "dve_steps", "exp_ready"))
        back_ready, back_copied, out_ready, out_done, cols_ready = (
            P.sem(x) for x in ("back_ready", "back_copied", "out_ready", "out_done", "cols_ready"))
        cols = lambda b: slice(b % NB * 32, b % NB * 32 + 32)
        mark = {}
        with nc.Block() as block:
            @block.vector
            def _(dve):
                ch = Chain(dve, dve_steps)
                V = nc.vector

                def dot_products(b):
                    dve.wait_ge(k_in[b % 2], 16 * LOADS * (b // 2 + 1))
                    for g, (lo, hi) in enumerate(((1, 5), (5, 7))):
                        rows = kc[b % 2][:, lo:hi, :]
                        dve.wait_ge(q_ready, 2 * b + g + 1)
                        ch.step(V.tensor_tensor(rows, rows, over(p_q[g][:], 1, hi - lo), ALU.mult))
                        mark["q_used", b, g] = ch.n
                    if b >= 2:
                        dve.wait_ge(dots_copied, b - 1)
                    for g, (lo, hi) in enumerate(((1, 5), (5, 7))):
                        ch.settle(lag=1)
                        ch.step(V.tensor_reduce(dots[:, b % 2, lo - 1:hi - 1, :],
                                                kc[b % 2][:, lo:hi, :].rearrange("p j (h e) -> p j h e", h=CH),
                                                AX_X, ALU.add))
                    mark["dots", b] = ch.n

                def maximum(bb):
                    dve.wait_ge(row_ready, bb + 1)
                    ch(V.scalar_tensor_tensor(out=s[:], in0=p_row[bb][:, 0:WID], scalar=ATT_SCALE,
                                              in1=mask[:, bb, :], op0=ALU.mult, op1=ALU.add))
                    ch(V.tensor_reduce(st[:, 0:1], s[:], AX_X, ALU.max))
                    ch.step(V.tensor_scalar(st[:, 1:2], st[:, 0:1], -1.0, None, ALU.mult))
                    mark["max", bb] = ch.n

                def normalize(bb):
                    dve.wait_ge(exp_ready, bb + 1)
                    ch(V.reciprocal(st[:, 3:4], st[:, 2:3]))
                    ch.step(V.tensor_scalar(s[:], s[:], st[:, 3:4], None, ALU.mult))
                    mark["norm", bb] = ch.n

                def take_out(bb):
                    dve.wait_ge(out_ready, NB * (bb + 1))
                    if bb:
                        dve.wait_ge(cols_ready, bb)
                    ch.step(V.tensor_copy(out_rows, p_w[:]))
                    mark["out", bb] = ch.n

                dve.wait_ge(const_in, 32)
                for g in range(2):
                    dve.wait_ge(qrow_ready, g + 1)
                    ch.step(V.tensor_copy(q_rows[:, g, :], p_q[g][0:NS, :]))
                mark["q_rows"] = ch.n
                for b in range(5):
                    dot_products(b)
                maximum(0)
                dot_products(5)
                normalize(0)
                dot_products(6)
                dot_products(7)
                maximum(1)
                normalize(1)
                take_out(0)
                take_out(1)

            @block.tensor
            def _(pe):
                mm = nc.tensor.matmul

                def sample(b):
                    def turn(half):
                        if b or half:
                            pe.wait_ge(keys_copied, 2 * b + half)
                        for h in range(4):
                            e = slice((half * 4 + h) * 128, (half * 4 + h + 1) * 128)
                            last = nc.tensor.transpose(p_kt[:, h * 128:(h + 1) * 128], kc[b % 2][:, 0, e],
                                                       K["ident"][:])
                        last.then_inc(keys_ready, 1)

                    def spread_q(g):
                        pe.wait_ge(dve_steps, mark["q_used", b - 1, g] if b else mark["q_rows"])
                        for c in range(2):
                            e = slice(c * 512, c * 512 + 512)
                            last = mm(p_q[g][:, e], spread[:, b * 128:(b + 1) * 128], q_rows[:, g, e],
                                      start=True, stop=True)
                        last.then_inc(q_ready, 1)

                    def scores(half):
                        pe.wait_ge(keys_copied, 2 * b + half + 1)
                        if half == 0 and b:
                            pe.wait_ge(col_copied, b)
                            if b == NB:
                                pe.wait_ge(new_copied, 1)
                        for h in range(4):
                            hh = half * 4 + h
                            last = mm(p_sc[:, hh * 4:hh * 4 + 4],
                                      kTc[:, half, h * 128:(h + 1) * 128], qS[:, hh, 4 * b:4 * b + 4],
                                      start=True, stop=True)
                        last.then_inc(col_ready, 1)

                    pe.wait_ge(k_in[b % 2], 16 * LOADS * (b // 2 + 1))
                    turn(0)
                    spread_q(0)
                    turn(1)
                    scores(0)
                    spread_q(1)
                    scores(1)

                def new_rows(bb):
                    pe.wait_ge(col_copied, NB * (bb + 1))
                    for gi in range(NG):
                        for h in range(CH):
                            q = qS[:, gi * CH + h, 16 * bb:16 * bb + 16].rearrange("e (b t) -> e b t", t=DEC_T)
                            dst = p_sc[gi * NS:(gi + 1) * NS, 128:256].rearrange("j (b h t) -> j b h t", b=NB, h=CH)
                            last = mm(dst[:, :, h, :], kS[:, gi * CH + h, :], q, start=True, stop=True)
                    last.then_inc(new_ready, 1)

                def to_rows(bb):
                    pe.wait_ge(new_copied, bb + 1)
                    pe.wait_ge(col_copied, NB * (bb + 1))
                    pe.wait_ge(dots_copied, NB * (bb + 1))
                    for k in range(NT):
                        r = 128 if k < KT else NG * NS
                        last = nc.tensor.transpose(p_row[bb][:, k * 128:k * 128 + r], sT[0:r, bb, k, :],
                                                   K["ident"][0:r, 0:r])
                    last.then_inc(row_ready, 1)

                def weights_back(bb):
                    pe.wait_ge(dve_steps, mark["norm", bb])
                    for k in range(NT):
                        r = 128 if k < KT else NG * NS
                        last = nc.tensor.transpose(p_row[bb][0:r, k * 128:k * 128 + 128],
                                                   s[:, k * 128:k * 128 + r], K["ident"][:])
                    last.then_inc(back_ready, 1)

                def values(b):
                    pe.wait_ge(back_copied, b // NB + 1)
                    pe.wait_ge(v_in[b % 2], 16 * LOADS * (b // 2 + 1))
                    if b == NB:
                        pe.wait_ge(dve_steps, mark["out", 0])
                    for c in range(2):
                        e = slice(c * 512, c * 512 + 512)
                        for k in range(NT):
                            l, r = ((pT[:, k, cols(b)], vc[:, b % 2, k, e]) if k < KT else
                                    (pT[0:NG * NS, k, cols(b)], v_new[:, e]))
                            last = mm(p_w[cols(b), e], l, r, start=(k == 0), stop=(k == NT - 1))
                    last.then_inc(out_ready, 1)

                def to_columns(bb):
                    pe.wait_ge(dve_steps, mark["out", bb])
                    if bb:
                        pe.wait_ge(out_done, bb)
                    for h in range(CH):
                        last = nc.tensor.transpose(p_q[1][:, h * 128:(h + 1) * 128],
                                                   out_rows[:, h * 128:(h + 1) * 128], K["ident"][:])
                    last.then_inc(cols_ready, 1)

                for g in range(2):
                    for h in range(CH):
                        last = nc.tensor.transpose(p_q[g][0:NS, h * 128:(h + 1) * 128], qS[:, (g + 1) * CH + h, :],
                                                   K["ident"][:])
                    last.then_inc(qrow_ready, 1)
                pe.wait_ge(const_in, 32)
                for b in range(4):
                    sample(b)
                new_rows(0)
                sample(4)
                to_rows(0)
                sample(5)
                sample(6)
                weights_back(0)
                pe.wait_ge(vnew_in, 16 * NG)
                values(0)
                sample(7)
                values(1)
                new_rows(1)
                values(2)
                to_rows(1)
                values(3)
                weights_back(1)
                values(4)
                to_columns(0)
                for b in (5, 6, 7):
                    values(b)
                to_columns(1)

            @block.scalar
            def _(act):
                A = nc.scalar.activation

                def keys(b):
                    for half in range(2):
                        act.wait_ge(keys_ready, 2 * b + half + 1)
                        if b:
                            act.wait_ge(col_ready, 2 * b + half - 1)
                        A(kTc[:, half, :], p_kt[:], ACT.Copy).then_inc(keys_copied, 1)
                    act.wait_ge(col_ready, 2 * b + 2)
                    A(sT[:, b // NB, 0, cols(b)], p_sc[:, 0:32], ACT.Copy
                      ).then_inc(col_copied, 1)

                def take_dots(b):
                    act.wait_ge(dve_steps, mark["dots", b])
                    A(sT[:, b // NB, 1:KT, cols(b)].rearrange("p k (h t) -> p k h t", h=CH),
                      over(dots[:, b % 2, :, :], 3, DEC_T), ACT.Copy).then_inc(dots_copied, 1)

                def new_rows(bb):
                    act.wait_ge(new_ready, bb + 1)
                    A(sT[0:NG * NS, bb, KT, :], p_sc[0:NG * NS, 128:256], ACT.Copy).then_inc(new_copied, 1)

                def exps(bb):
                    act.wait_ge(dve_steps, mark["max", bb])
                    A(s[:], s[:], ACT.Exp, bias=st[:, 1:2], accum_out=st[:, 2:3]).then_inc(exp_ready, 1)

                def weights(bb):
                    act.wait_ge(back_ready, bb + 1)
                    if bb:
                        act.wait_ge(out_ready, NB)
                    A(pT[:, 0:KT, :], p_row[bb][:, 0:KT * 128].rearrange("p (k n) -> p k n", k=KT), ACT.Copy)
                    A(pT[0:NG * NS, KT, :], p_row[bb][0:NG * NS, KT * 128:NT * 128], ACT.Copy
                      ).then_inc(back_copied, 1)

                def to_mix(bb):
                    act.wait_ge(cols_ready, bb + 1)
                    dst = mixT[:, :, SEQ + 16 * bb:SEQ + 16 * bb + 16].rearrange("e h (b t) -> e h b t", t=DEC_T)
                    src = p_q[1][:].rearrange("e (g b h t) -> e g h b t", g=CH, b=NB, h=CH)
                    for h in range(CH):
                        last = A(dst[:, h], src[:, h, h], ACT.Copy)
                    last.then_inc(out_done, 1)

                keys(0)
                for b in (1, 2, 3):
                    keys(b)
                    take_dots(b - 1)
                new_rows(0)
                keys(4)
                take_dots(3)
                keys(5)
                take_dots(4)
                exps(0)
                keys(6)
                take_dots(5)
                weights(0)
                keys(7)
                take_dots(6)
                new_rows(1)
                take_dots(7)
                exps(1)
                weights(1)
                to_mix(0)
                to_mix(1)

            @block.sync
            def _(sp):
                sp.dma_start(spread, T["c_spread"]).then_inc(const_in, 16)
                sp.dma_start(mask[:], T["c_samp"].rearrange("p (b n) -> p b n", b=2)).then_inc(const_in, 16)
                for b in range(1, DEC_B):
                    if b >= 2:
                        sp.wait_ge(keys_ready, 2 * (b - 1))
                        sp.wait_ge(dve_steps, mark["dots", b - 2])
                    for to, frm in key_tiles(T, kc[b % 2][:], b, 0):
                        sp.dma_start(to, frm).then_inc(k_in[b % 2], 16)

            @block.gpsimd
            def _(pool):
                pool.wait_ge(k_in[0], 16 * LOADS)
                for gi in range(NG):
                    pool.dma_start(v_new[gi * NS:(gi + 1) * NS, :], vS[:, gi].rearrange("j h e -> j (h e)")
                                   ).then_inc(vnew_in, 16)
                for b in range(DEC_B):
                    if b >= 2:
                        pool.wait_ge(out_ready, b - 1)
                    for to, frm in key_tiles(T, vc[:, b % 2], b, 1):
                        pool.dma_start(to, frm).then_inc(v_in[b % 2], 16)


OUTS = [("y_p", (1, SEQ, D)), ("y_s", (DEC_B, DEC_T, D)), ("conv_a_p", (1, 1, 30, D_A)),
        ("conv_qkv_p", (1, 1, 3, QKV_W)), ("delta_p", (1, 1, GH, GD, GD)),
        ("kv0_p", (1, 1, 128, 2, CH, HD)), ("kv1_p", (1, 1, SEQ, 2, CH, HD)), ("kv2_p", (1, 1, SEQ, 2, CH, HD)),
        ("conv_a_s", (1, DEC_B, 30, D_A)), ("conv_qkv_s", (1, DEC_B, 3, QKV_W)),
        ("delta_s", (1, DEC_B, GH, GD, GD)), ("kv0_s", (1, DEC_B, 128, 2, CH, HD)),
        ("kv1_s", (1, DEC_B, 512, 2, CH, HD)), ("kv2_s", (1, DEC_B, PAST + DEC_T, 2, CH, HD))]


def build(nc, T, phases=99):
    with ExitStack() as ctx:
        P = Phase(nc, ctx, "all", clears=False)
        K = {"x": P.sb("x", [128, 3, D]), "ident": P.sb("ident", [128, 128]), "h": P.sb("h", [128, 3, D]),
             "hT": P.sb("hT", [128, KC, NTOK])}
        x, h, hT = K["x"], K["h"], K["hT"]
        mixT = P.sb("mixT", [128, KC, NTOK])
        x_in = P.sem("x_in")
        with nc.Block() as block:
            @block.sync
            def _(sp):
                sp.dma_start(K["ident"][:], T["c_ident"]).then_inc(x_in, 16)
                sp.dma_start(x[:, 0:2, :], T["x_prompt"][0].rearrange("(t p) d -> p t d", p=128)).then_inc(x_in, 16)
                sp.dma_start(x[0:NS, 2, :], T["x_sample"].rearrange("b t d -> (b t) d")).then_inc(x_in, 16)
                sp.wait_ge(x_in, 48)
        cache_out = P.sem("cache_out")
        with ExitStack() as c2:
            P0 = Phase(nc, c2, "l0")
            zT, conv = P0.sb("zT", [128, 24, NTOK]), P0.sb("conv", [128, 12, NTOK])
            with ExitStack() as c3:
                W = WeightRing(Phase(nc, c3, "ab_ring"), T["w_in_ab"][0], IN_AB - 8, 3)
                norm_phase(nc, "n0", K, T["norm_mix"][0:1, :], h, hT, ahead=W.start)
                def copies(sp):
                    roll_cache(sp, T, 0, cache_out)
                    roll_cache(sp, T, 1, cache_out, range(2))

                columns_phase(nc, "ab", hT, T["w_in_ab"][0], IN_AB - 8, zT, ahead=W, after=copies)
            conv_phase(nc, "cv", K, T, zT, mixT, conv, cache_out)
            delta_phase(nc, "gd", K, T, hT, zT, conv, mixT, cache_out)
        add_rows_phase(nc, "oab", K, mixT, T["w_out_ab"][0])
        if phases == 2: return dump(nc, T, x)
        tail(nc, K, T, 0, phases, 3)
        if phases in (3, 4): return dump(nc, T, x)
        with ExitStack() as c2:
            P1 = Phase(nc, c2, "l1")
            qS, kS = P1.sb("qS", [128, NG * CH, NS]), P1.sb("kS", [128, NG * CH, NS])
            k_first, k_first_in = P1.sb("k_first", [128, KT, D]), P1.sem("k_first_in")
            vS = P1.sb("vS", [NS, NG, CH, HD])
            with ExitStack() as c3:
                P2 = Phase(nc, c3, "l1p")
                qP, kP = P2.sb("q", [128, NG * CH, SEQ]), P2.sb("k", [128, NG * CH, SEQ])
                vP = P2.sb("v", [128, 2, NG, CH, HD])
                with ExitStack() as c4:
                    W = WeightRing(Phase(nc, c4, "qkv_ring"), T["w_in_c"][0], 3 * NG * CH * HD, 2)
                    norm_phase(nc, "n1", K, T["norm_mix"][1:2, :], h, hT, ahead=W.start)
                    qkv_phase(nc, "qkv", K, T, W, qP, kP, vP, qS, kS, vS, cache_out)
                prompt_attention_phase(nc, "pa", K, T, qP, kP, vP, mixT, k_first, k_first_in)
            sample_attention_phase(nc, "sa", K, T, qS, kS, vS, mixT, k_first, k_first_in)
        add_rows_phase(nc, "oc", K, mixT, T["w_out_c"][0])
        if phases == 5: return dump(nc, T, x)
        tail(nc, K, T, 1, phases, 6)
        if phases == 6: return dump(nc, T, x)
        y = [T["out_y_p"][0, 0:128, :], T["out_y_p"][0, 128:256, :], T["out_y_s"].rearrange("b t d -> (b t) d")]
        norm_phase(nc, "nl", K, T["norm_final"].rearrange("(a n) -> a n", a=1), h, None, y)
        with nc.Block() as block:
            @block.sync
            def _(sp):
                sp.wait_ge(cache_out, 16 * NG * DEC_B)


def roll_cache(eng, T, gi, cache_out, samples=range(DEC_B)):
    src, dst = T[f"cache_kv_w{PATTERNS[gi][0]}"][0], T[f"out_kv{gi}_s"][0]
    keep = dst.shape[1] - DEC_T
    drop = src.shape[1] - keep
    for b in samples:
        eng.dma_start(dst[b, 0:keep].rearrange("r k h e -> r (k h e)"),
                      src[b, drop:].rearrange("r k h e -> r (k h e)")).then_inc(cache_out, 16)


def dump(nc, T, x):
    with nc.semaphore("dbg") as s, nc.Block() as block:
        @block.sync
        def _(sp):
            sp.dma_start(T["dbg"][:, 0:2, :], x[:, 0:2, :]).then_inc(s, 16)
            sp.dma_start(T["dbg"][0:NS, 2, :], x[0:NS, 2, :]).then_inc(s, 16)
            sp.wait_ge(s, 32)


def kernel(**inputs):
    import concourse.bacc as bacc
    from concourse.bass_utils import run_bass_kernel_spmd

    nc = bacc.Bacc("TRN2", target_bir_lowering=False, num_devices=1)
    arrays = {k: np.ascontiguousarray(v) for k, v in inputs.items()}
    arrays.update({f"c_{k}": v for k, v in shape_constants().items()})
    T = {k: nc.dram_tensor(f"in_{k}", a.shape, mybir.dt.from_np(a.dtype), kind="ExternalInput").ap()
         for k, a in arrays.items()}
    for name, shape in OUTS:
        T[f"out_{name}"] = nc.dram_tensor(f"out_{name}", shape, F32, kind="ExternalOutput").ap()
    build(nc, T)
    r = run_bass_kernel_spmd(nc, [{f"in_{k}": a for k, a in arrays.items()}], core_ids=[0]).results[0]
    return tuple(r[f"out_{name}"] for name, _ in OUTS)
```
